# Optimizing a Trainium2 kernel written in Bass

```python
import math
import jax, jax.numpy as jnp
from jax import lax
import numpy as np

D_MODEL = 1024
BATCH = 1
SEQ = 1024
DEPTH = 1
DEC_BATCH = 8
DEC_SEQ = 8
PAST_LEN = 8192
PAGE_SIZE = 128

N_META = 16
MIX_WIDTH = 2 * D_MODEL
S5_WIDTH = MIX_WIDTH // 2
S5_CH_PER_GROUP = 16
S5_GROUPS = S5_WIDTH // S5_CH_PER_GROUP
S5_STATE = 64
M2_WIDTH = MIX_WIDTH - S5_WIDTH
M2_HEAD_DIM = 64
M2_HEADS = M2_WIDTH // M2_HEAD_DIM
M2_GROUPS = 2
M2_HPG = M2_HEADS // M2_GROUPS
M2_D_STATE = 128
M2_CONV = 4
M2_CHUNK = 128
M2_CONV_DIM = M2_WIDTH + 2 * M2_GROUPS * M2_D_STATE
IN_PROJ = S5_WIDTH + M2_WIDTH + M2_CONV_DIM + M2_HEADS
PEER_HEADS = 8
PEER_N_KEYS = 128
PEER_EXPERTS = PEER_N_KEYS * PEER_N_KEYS
PEER_KEY_DIM = 256
PEER_HALF = PEER_KEY_DIM // 2
PEER_TOPK = 16
PEER_BLOCK = 128
EPS = 1e-6

kernel_name = "hymba_s5_mamba2_peer_step"

F32 = jnp.float32

def rmsnorm(x, w):
    xf = x.astype(F32)
    y = xf * lax.rsqrt(jnp.mean(xf * xf, axis=-1, keepdims=True) + EPS) * w.astype(F32)
    return y.astype(x.dtype)

def _complex_affine_combine(e1, e2):
    a1r, a1i, b1r, b1i = e1
    a2r, a2i, b2r, b2i = e2
    return (a2r * a1r - a2i * a1i, a2r * a1i + a2i * a1r,
            a2r * b1r - a2i * b1i + b2r, a2r * b1i + a2i * b1r + b2i)

def s5_mixer(u, h0_re, h0_im, lam_re, lam_im, log_step, b_re, b_im, c_re, c_im, d_skip, w_glu):
    bsz, L, _ = u.shape
    uf = u.astype(F32)
    ug = uf.reshape(bsz, L, S5_GROUPS, S5_CH_PER_GROUP)
    step = jnp.exp(log_step.astype(F32))[:, None]
    lr = lam_re.astype(F32)
    li = lam_im.astype(F32)
    mag = jnp.exp(lr * step)
    ab_re = mag * jnp.cos(li * step)
    ab_im = mag * jnp.sin(li * step)
    den = lr * lr + li * li
    f_re = ((ab_re - 1.0) * lr + ab_im * li) / den
    f_im = (ab_im * lr - (ab_re - 1.0) * li) / den
    br = b_re.astype(F32)
    bi = b_im.astype(F32)
    bb_re = f_re[..., None] * br - f_im[..., None] * bi
    bb_im = f_re[..., None] * bi + f_im[..., None] * br
    bu_re = jnp.einsum('gpc,blgc->blgp', bb_re, ug)
    bu_im = jnp.einsum('gpc,blgc->blgp', bb_im, ug)
    a_re = jnp.broadcast_to(ab_re, (1, L, S5_GROUPS, S5_STATE))
    a_im = jnp.broadcast_to(ab_im, (1, L, S5_GROUPS, S5_STATE))
    acr, aci, hr, hi = lax.associative_scan(_complex_affine_combine, (a_re, a_im, bu_re, bu_im), axis=1)
    h0r = h0_re.astype(F32)[:, None]
    h0i = h0_im.astype(F32)[:, None]
    hr = hr + acr * h0r - aci * h0i
    hi = hi + acr * h0i + aci * h0r
    y = (jnp.einsum('gcp,blgp->blgc', c_re.astype(F32), hr)
         - jnp.einsum('gcp,blgp->blgc', c_im.astype(F32), hi))
    y = y.reshape(bsz, L, S5_WIDTH) + d_skip.astype(F32) * uf
    g = jax.nn.gelu(y)
    out = g * jax.nn.sigmoid(g @ w_glu.astype(F32))
    return out.astype(u.dtype), hr[:, -1].astype(h0_re.dtype), hi[:, -1].astype(h0_im.dtype)

def causal_dwconv(xbc, buf, w, b):
    full = jnp.concatenate([buf.astype(xbc.dtype), xbc], axis=1)
    y = lax.conv_general_dilated(full, w.astype(full.dtype)[:, None, :], window_strides=(1,),
                                 padding='VALID', dimension_numbers=('NWC', 'WIO', 'NWC'),
                                 feature_group_count=M2_CONV_DIM)
    return jax.nn.silu(y + b.astype(y.dtype)), full[:, full.shape[1] - (M2_CONV - 1):]

def ssd_chunked(x, dt, A, B, C, h0):
    bsz, L = x.shape[0], x.shape[1]
    chunk = min(M2_CHUNK, L)
    pad = (-L) % chunk
    if pad:
        padf = lambda t: jnp.pad(t, [(0, 0), (0, pad)] + [(0, 0)] * (t.ndim - 2))
        x, dt, B, C = padf(x), padf(dt), padf(B), padf(C)
    nc = (L + pad) // chunk
    xc = x.reshape(bsz, nc, chunk, M2_GROUPS, M2_HPG, M2_HEAD_DIM)
    dtc = dt.reshape(bsz, nc, chunk, M2_GROUPS, M2_HPG)
    Bc = B.reshape(bsz, nc, chunk, M2_GROUPS, M2_D_STATE)
    Cc = C.reshape(bsz, nc, chunk, M2_GROUPS, M2_D_STATE)
    acs = jnp.cumsum(dtc * A, axis=2)
    seg = acs[:, :, :, None] - acs[:, :, None, :]
    causal = jnp.tril(jnp.ones((chunk, chunk), bool))[:, :, None, None]
    decay = jnp.exp(jnp.where(causal, seg, -jnp.inf))
    cb = jnp.einsum('bclgn,bcsgn->bclsg', Cc, Bc)
    wts = cb[..., None] * decay * dtc[:, :, None]
    y_diag = jnp.einsum('bclsgr,bcsgrp->bclgrp', wts, xc)
    decay_st = jnp.exp(acs[:, :, -1:] - acs) * dtc
    st = jnp.einsum('bclgn,bclgr,bclgrp->bcgrpn', Bc, decay_st, xc)
    chunk_decay = jnp.exp(acs[:, :, -1])

    def step(h, inp):
        st_c, dec_c = inp
        return dec_c[..., None, None] * h + st_c, h

    h_last, h_in = lax.scan(step, h0, (jnp.moveaxis(st, 1, 0), jnp.moveaxis(chunk_decay, 1, 0)))
    h_in = jnp.moveaxis(h_in, 0, 1)
    y_off = jnp.einsum('bclgn,bcgrpn,bclgr->bclgrp', Cc, h_in, jnp.exp(acs))
    y = (y_diag + y_off).reshape(bsz, nc * chunk, M2_GROUPS, M2_HPG, M2_HEAD_DIM)[:, :L]
    return y, h_last

def mamba2_mixer(z, xbc, dt_raw, conv_buf, ssm0, segs, conv_w, conv_b, dt_bias, a_log, d_skip, norm_w):
    bsz, L, _ = z.shape
    xbc, new_buf = causal_dwconv(xbc, conv_buf, conv_w, conv_b)
    xbc = xbc.astype(F32)
    gn = M2_GROUPS * M2_D_STATE
    xs = xbc[..., :M2_WIDTH].reshape(bsz, L, M2_GROUPS, M2_HPG, M2_HEAD_DIM)
    Bm = xbc[..., M2_WIDTH:M2_WIDTH + gn].reshape(bsz, L, M2_GROUPS, M2_D_STATE)
    Cm = xbc[..., M2_WIDTH + gn:].reshape(bsz, L, M2_GROUPS, M2_D_STATE)
    dt = jax.nn.softplus(dt_raw.astype(F32) + dt_bias.astype(F32)).reshape(bsz, L, M2_GROUPS, M2_HPG)
    A = -jnp.exp(a_log.astype(F32)).reshape(M2_GROUPS, M2_HPG)
    h = ssm0.astype(F32).reshape(bsz, M2_GROUPS, M2_HPG, M2_HEAD_DIM, M2_D_STATE)
    ys = []
    start = 0
    for seg_len in segs:
        y_seg, h = ssd_chunked(xs[:, start:start + seg_len], dt[:, start:start + seg_len], A,
                               Bm[:, start:start + seg_len], Cm[:, start:start + seg_len], h)
        ys.append(y_seg)
        start += seg_len
    y = jnp.concatenate(ys, axis=1)
    y = y + d_skip.astype(F32).reshape(M2_GROUPS, M2_HPG)[:, :, None] * xs
    y = y.reshape(bsz, L, M2_WIDTH) * jax.nn.silu(z.astype(F32))
    yg = y.reshape(bsz, L, M2_GROUPS, M2_WIDTH // M2_GROUPS)
    yg = yg * lax.rsqrt(jnp.mean(yg * yg, axis=-1, keepdims=True) + EPS)
    y = yg.reshape(bsz, L, M2_WIDTH) * norm_w.astype(F32)
    h_out = h.reshape(bsz, M2_HEADS, M2_HEAD_DIM, M2_D_STATE).astype(ssm0.dtype)
    return y.astype(z.dtype), h_out, new_buf.astype(conv_buf.dtype)

def peer_ffn(h, w_q, sub_keys, u_tab, v_tab):
    bsz, L, D = h.shape
    T = bsz * L
    xt = h.reshape(T, D)
    q = (xt @ w_q).astype(F32).reshape(T, PEER_HEADS, 2, PEER_HALF)
    s = jnp.einsum('thid,hikd->thik', q, sub_keys.astype(F32))
    sv, si = lax.top_k(s, PEER_TOPK)
    cand = sv[:, :, 0, :, None] + sv[:, :, 1, None, :]
    cv, cpos = lax.top_k(cand.reshape(T, PEER_HEADS, PEER_TOPK * PEER_TOPK), PEER_TOPK)
    i1 = jnp.take_along_axis(si[:, :, 0], cpos // PEER_TOPK, axis=-1)
    i2 = jnp.take_along_axis(si[:, :, 1], cpos % PEER_TOPK, axis=-1)
    idx = i1 * PEER_N_KEYS + i2
    g = jax.nn.softmax(cv, axis=-1)
    pad = (-T) % PEER_BLOCK
    xt_p = jnp.pad(xt, ((0, pad), (0, 0)))
    idx_p = jnp.pad(idx, ((0, pad), (0, 0), (0, 0)))
    g_p = jnp.pad(g, ((0, pad), (0, 0), (0, 0)))
    nb = (T + pad) // PEER_BLOCK

    def block(args):
        xb, ib, gb = args
        u = u_tab[ib]
        act = jax.nn.gelu(jnp.einsum('thkd,td->thk', u, xb).astype(F32))
        v = v_tab[ib]
        return jnp.einsum('thk,thkd->td', (gb * act).astype(v.dtype), v)

    out = lax.map(block, (xt_p.reshape(nb, PEER_BLOCK, D),
                          idx_p.reshape(nb, PEER_BLOCK, PEER_HEADS, PEER_TOPK),
                          g_p.reshape(nb, PEER_BLOCK, PEER_HEADS, PEER_TOPK)))
    return out.reshape(nb * PEER_BLOCK, D)[:T].reshape(bsz, L, D).astype(h.dtype)

def decoder_layer(x, s5_re, s5_im, ssm0, conv_buf, segs, l, prm):
    hn = rmsnorm(x, prm['norm_mix_w'][l])
    proj = hn @ prm['w_in'][l]
    o1 = S5_WIDTH
    o2 = o1 + M2_WIDTH
    o3 = o2 + M2_CONV_DIM
    u = proj[..., :o1]
    z = proj[..., o1:o2]
    xbc = proj[..., o2:o3]
    dt_raw = proj[..., o3:]
    y_s5, s5_re_n, s5_im_n = s5_mixer(u, s5_re, s5_im, prm['s5_lambda_re'][l], prm['s5_lambda_im'][l],
                                      prm['s5_log_step'][l], prm['s5_b_re'][l], prm['s5_b_im'][l],
                                      prm['s5_c_re'][l], prm['s5_c_im'][l], prm['s5_d'][l], prm['s5_w_glu'][l])
    y_s5 = rmsnorm(y_s5, prm['s5_norm_w'][l])
    y_m2, ssm_n, conv_n = mamba2_mixer(z, xbc, dt_raw, conv_buf, ssm0, segs, prm['m2_conv_w'][l],
                                       prm['m2_conv_b'][l], prm['m2_dt_bias'][l], prm['m2_a_log'][l],
                                       prm['m2_d'][l], prm['m2_norm_w'][l])
    x = x + jnp.concatenate([y_s5, y_m2], axis=-1) @ prm['w_out'][l]
    x = x + peer_ffn(rmsnorm(x, prm['norm_ffn_w'][l]), prm['peer_w_q'][l], prm['peer_sub_keys'][l],
                     prm['peer_u'][l], prm['peer_v'][l])
    return x, (s5_re_n, s5_im_n, ssm_n, conv_n)

def run_trunk(x, init_states, segs, prm):
    bsz = x.shape[0]
    new = ([], [], [], [])
    for l in range(DEPTH):
        if init_states is None:
            s5r = jnp.zeros((bsz, S5_GROUPS, S5_STATE), x.dtype)
            s5i = jnp.zeros((bsz, S5_GROUPS, S5_STATE), x.dtype)
            ssm0 = jnp.zeros((bsz, M2_HEADS, M2_HEAD_DIM, M2_D_STATE), x.dtype)
            cbuf = jnp.zeros((bsz, M2_CONV - 1, M2_CONV_DIM), x.dtype)
        else:
            s5r = init_states[0][l]
            s5i = init_states[1][l]
            ssm0 = init_states[2][l]
            cbuf = init_states[3][l]
        x, st = decoder_layer(x, s5r, s5i, ssm0, cbuf, segs, l, prm)
        for lst, s in zip(new, st):
            lst.append(s)
    y = rmsnorm(x, prm['final_norm_w'])
    return y, [jnp.stack(lst) for lst in new]

def setup_inputs(seed: int = 0) -> dict:
    key = jax.random.key(seed)
    ks = jax.random.split(key, 32)

    def nrm(k, shape, scale):
        return scale * jax.random.normal(k, shape, F32)

    n_idx = jnp.arange(S5_STATE, dtype=F32)
    gp = (DEPTH, S5_GROUPS, S5_STATE)
    dt0 = jnp.exp(jax.random.uniform(ks[17], (DEPTH, M2_HEADS), F32, math.log(1e-3), math.log(1e-1)))
    return {
        'x_prompt': nrm(ks[0], (BATCH, SEQ, D_MODEL), 1.0),
        'x_sample': nrm(ks[1], (DEC_BATCH, DEC_SEQ, D_MODEL), 1.0),
        'state_s5_re': nrm(ks[2], (DEPTH, DEC_BATCH, S5_GROUPS, S5_STATE), 0.1),
        'state_s5_im': nrm(ks[3], (DEPTH, DEC_BATCH, S5_GROUPS, S5_STATE), 0.1),
        'state_ssm': nrm(ks[4], (DEPTH, DEC_BATCH, M2_HEADS, M2_HEAD_DIM, M2_D_STATE), 0.1),
        'state_conv': nrm(ks[5], (DEPTH, DEC_BATCH, M2_CONV - 1, M2_CONV_DIM), 1.0),
        'meta_tokens': nrm(ks[6], (N_META, D_MODEL), 1.0),
        'norm_mix_w': 1.0 + nrm(ks[7], (DEPTH, D_MODEL), 0.02),
        'w_in': nrm(ks[8], (DEPTH, D_MODEL, IN_PROJ), D_MODEL ** -0.5),
        's5_lambda_re': -0.5 * jnp.exp(nrm(ks[9], gp, 0.05)),
        's5_lambda_im': jnp.pi * n_idx + nrm(ks[10], gp, 0.01),
        's5_log_step': jax.random.uniform(ks[11], (DEPTH, S5_GROUPS), F32, math.log(1e-3), math.log(1e-1)),
        's5_b_re': nrm(ks[12], (DEPTH, S5_GROUPS, S5_STATE, S5_CH_PER_GROUP), (2 * S5_CH_PER_GROUP) ** -0.5),
        's5_b_im': nrm(ks[13], (DEPTH, S5_GROUPS, S5_STATE, S5_CH_PER_GROUP), (2 * S5_CH_PER_GROUP) ** -0.5),
        's5_c_re': nrm(ks[14], (DEPTH, S5_GROUPS, S5_CH_PER_GROUP, S5_STATE), (2 * S5_STATE) ** -0.5),
        's5_c_im': nrm(ks[15], (DEPTH, S5_GROUPS, S5_CH_PER_GROUP, S5_STATE), (2 * S5_STATE) ** -0.5),
        's5_d': nrm(ks[16], (DEPTH, S5_WIDTH), 1.0),
        's5_w_glu': nrm(ks[18], (DEPTH, S5_WIDTH, S5_WIDTH), S5_WIDTH ** -0.5),
        's5_norm_w': 1.0 + nrm(ks[19], (DEPTH, S5_WIDTH), 0.02),
        'm2_conv_w': nrm(ks[20], (DEPTH, M2_CONV, M2_CONV_DIM), 0.5),
        'm2_conv_b': nrm(ks[21], (DEPTH, M2_CONV_DIM), 0.01),
        'm2_dt_bias': dt0 + jnp.log(-jnp.expm1(-dt0)),
        'm2_a_log': jnp.log(jax.random.uniform(ks[22], (DEPTH, M2_HEADS), F32, 1.0, 16.0)),
        'm2_d': 1.0 + nrm(ks[23], (DEPTH, M2_HEADS), 0.1),
        'm2_norm_w': 1.0 + nrm(ks[24], (DEPTH, M2_WIDTH), 0.02),
        'w_out': nrm(ks[25], (DEPTH, MIX_WIDTH, D_MODEL), MIX_WIDTH ** -0.5),
        'norm_ffn_w': 1.0 + nrm(ks[26], (DEPTH, D_MODEL), 0.02),
        'peer_w_q': nrm(ks[27], (DEPTH, D_MODEL, PEER_HEADS * PEER_KEY_DIM), D_MODEL ** -0.5),
        'peer_sub_keys': nrm(ks[28], (DEPTH, PEER_HEADS, 2, PEER_N_KEYS, PEER_HALF), PEER_HALF ** -0.5),
        'peer_u': nrm(ks[29], (DEPTH, PEER_EXPERTS, D_MODEL), D_MODEL ** -0.5),
        'peer_v': nrm(ks[30], (DEPTH, PEER_EXPERTS, D_MODEL), PEER_HEADS ** -0.5),
        'final_norm_w': 1.0 + nrm(ks[31], (D_MODEL,), 0.02),
    }

def reference(x_prompt, x_sample, state_s5_re, state_s5_im, state_ssm, state_conv, meta_tokens,
              norm_mix_w, w_in, s5_lambda_re, s5_lambda_im, s5_log_step, s5_b_re, s5_b_im, s5_c_re,
              s5_c_im, s5_d, s5_w_glu, s5_norm_w, m2_conv_w, m2_conv_b, m2_dt_bias, m2_a_log, m2_d,
              m2_norm_w, w_out, norm_ffn_w, peer_w_q, peer_sub_keys, peer_u, peer_v, final_norm_w):
    prm = {
        'norm_mix_w': norm_mix_w, 'w_in': w_in, 's5_lambda_re': s5_lambda_re, 's5_lambda_im': s5_lambda_im,
        's5_log_step': s5_log_step, 's5_b_re': s5_b_re, 's5_b_im': s5_b_im, 's5_c_re': s5_c_re,
        's5_c_im': s5_c_im, 's5_d': s5_d, 's5_w_glu': s5_w_glu, 's5_norm_w': s5_norm_w,
        'm2_conv_w': m2_conv_w, 'm2_conv_b': m2_conv_b, 'm2_dt_bias': m2_dt_bias, 'm2_a_log': m2_a_log,
        'm2_d': m2_d, 'm2_norm_w': m2_norm_w, 'w_out': w_out, 'norm_ffn_w': norm_ffn_w,
        'peer_w_q': peer_w_q, 'peer_sub_keys': peer_sub_keys, 'peer_u': peer_u, 'peer_v': peer_v,
        'final_norm_w': final_norm_w,
    }
    bp, sp = x_prompt.shape[0], x_prompt.shape[1]
    meta = jnp.broadcast_to(meta_tokens.astype(x_prompt.dtype)[None], (bp, N_META, D_MODEL))
    xp = jnp.concatenate([meta, x_prompt], axis=1)
    yp, pst = run_trunk(xp, None, (N_META, sp), prm)
    y_prompt = yp[:, N_META:]
    y_sample, sst = run_trunk(x_sample, (state_s5_re, state_s5_im, state_ssm, state_conv),
                              (x_sample.shape[1],), prm)
    return (y_prompt, y_sample, pst[0], pst[1], pst[2], pst[3], sst[0], sst[1], sst[2], sst[3])


_drawn_inputs = setup_inputs


def setup_inputs(seed=0):
    import zlib

    import numpy as np

    out = dict(_drawn_inputs(seed))
    spreads = {}
    factors = {'s5_norm_w': 10.624,
     'm2_conv_b': 3.088,
     'm2_norm_w': 10.551,
     'norm_ffn_w': 9.65,
     'final_norm_w': 8.375}
    for name, (base, spread) in spreads.items():
        noise = np.random.default_rng([zlib.crc32(name.encode()), seed]).standard_normal(out[name].shape)
        drawn = base * np.exp(spread * noise) if base else spread * noise
        out[name] = __import__('jax').numpy.asarray(drawn.astype(out[name].dtype))
    for name, factor in factors.items():
        out[name] = (out[name] * factor).astype(out[name].dtype)
    return out
```

```python
import numpy as np
import concourse.bass as bass
from concourse import mybir
from contextlib import ExitStack, contextmanager

F32 = mybir.dt.float32
I32 = mybir.dt.int32
U32 = mybir.dt.uint32
ALU = mybir.AluOpType
ACT = mybir.ActivationFunctionType
AX = mybir.AxisListType

P = 128
D_MODEL = 1024
KT = D_MODEL // P
SEQ = 1024
N_META = 16
SEQS = 8
STEPS = 8
SAMPLE = SEQS * STEPS
MAIN_TILES = SEQ // P
TILES = MAIN_TILES + 1
ROWS = TILES * P
REST = SAMPLE + N_META
EPS = 1e-6

S5_CH = 16
S5_GROUPS = 64
S5_STATE = 64
PAIRS = S5_GROUPS // 2
Q = 8
CH_MAIN = SEQ // Q
CH_META = N_META // Q
CH_REST = SEQS + CH_META
CHUNKS = CH_REST + CH_MAIN
CH_PROMPT = CH_META + CH_MAIN
SCAN = 10
BLOCKS = CH_PROMPT // SCAN
assert BLOCKS * SCAN == CH_PROMPT

HEADS = 16
HPG = 8
HD = 64
NS = 128
XBC = 1536
XB = XBC // P
TAPS = 4
TOKW = 2 * D_MODEL + HEADS
IN_PROJ = TOKW + XBC
XCOLS = N_META + SEQ + SAMPLE

PH = 8
NK = 128
TOPK = 16
SLOTS = PH * TOPK
EXPERTS = NK * NK


class Chain:

    def __init__(self, eng, sem):
        self.eng, self.sem, self.base, self.n = eng, sem, 0, 0

    def link(self, ins):
        self.n += 1
        ins.then_inc(self.sem, 1)
        self.eng.wait_ge(self.sem, self.base + self.n)

    def start(self, base):
        self.base, self.n = base, 0


def settle(eng, sem):
    eng.sem_inc(sem, 1)


def bc(ap, dims):
    return bass.AP(tensor=ap.tensor, offset=ap.offset, ap=[list(ap.ap[0])] + [list(d) for d in dims])


@contextmanager
def stage_semaphores(nc, prefix):
    held = []

    def new(name):
        held.append(nc.alloc_semaphore(prefix + name))
        return held[-1]

    yield new
    nc.clear_and_free_semaphores(held)
    nc.all_engine_barrier()


def project_tokens(nc, D):
    with ExitStack() as ctx:
        sb = lambda n, s, d=F32: ctx.enter_context(nc.sbuf_tensor("pj_" + n, s, d))
        ident = sb("ident", [P, P])
        norm_w = sb("norm_w", [P, KT])
        w_in = sb("w_in", [P, KT, IN_PROJ])
        x = sb("x", [P, D_MODEL])
        square = sb("square", [P, D_MODEL])
        stat = sb("stat", [P, 4])
        normed = sb("normed", [P, D_MODEL])
        normed_t = sb("normed_t", [P, KT, P])
        token_out = sb("token_out", [P, TOKW])
        chan_out = sb("chan_out", [P, XB, P])
        t_psum = ctx.enter_context(nc.psum_tensor("pj_t_psum", [P, KT, P], F32))
        bank = ctx.enter_context(nc.psum_tensor("pj_bank", [P, 4, 512], F32))
        sem = ctx.enter_context(stage_semaphores(nc, "pj_"))
        consts_in, x_in, x_free = sem("consts_in"), sem("x_in"), sem("x_free")
        w_part_in = [sem(f"w_in{j}") for j in range(3)]
        root_ready, square_ready, normed_ready = sem("root_ready"), sem("square_ready"), sem("normed_ready")
        transposed, t_copied = sem("transposed"), sem("t_copied")
        even_done, odd_done = sem("even_done"), sem("odd_done")
        even_free, odd_free = sem("even_free"), sem("odd_free")
        stored, padded, dve_step = sem("stored"), sem("padded"), sem("dve_step")
        ITEMS = 8
        W_CUT = [0, 2 * 512, TOKW, IN_PROJ]
        block = ctx.enter_context(nc.Block())

        @block.sync
        def _(sp):
            sp.dma_start(ident[:], D["ident"]).then_inc(consts_in, 16)
            sp.dma_start(norm_w[:], D["norm_mix_w"]).then_inc(consts_in, 16)
            sp.dma_start(D["y5"][SEQ + REST:ROWS, :], D["x_all"][SEQ + REST:ROWS, :]).then_inc(padded, 16)
            sp.dma_start(x[:], D["x_all"][0:P, :]).then_inc(x_in, 16)
            for j in range(3):
                a, b = W_CUT[j], W_CUT[j + 1]
                sp.dma_start(w_in[:, :, a:b], D["w_in"][:, :, a:b]).then_inc(w_part_in[j], 16)

            def store(i, col, width, dst_cols):
                sp.wait_ge(even_free, i * 4 + 2 + 4)
                sp.wait_ge(odd_free, i * 4 + 2 + 4)
                rows = bass.ds(i * P, P)
                sp.dma_start(D["u"][rows, :], token_out[:, 0:D_MODEL]).then_inc(stored, 16)
                sp.dma_start(D["z"][rows, :], token_out[:, D_MODEL:2 * D_MODEL]).then_inc(stored, 16)
                sp.dma_start(D["dt"][rows, :], token_out[:, 2 * D_MODEL:TOKW]).then_inc(stored, 16)
                sp.dma_start(D["xbc"][:, :, dst_cols], chan_out[:, :, col:col + width]).then_inc(stored, 16)

            with sp.Fori(0, MAIN_TILES) as i:
                sp.wait_ge(x_free, i + 1)
                sp.dma_start(x[:], D["x_all"][bass.ds(i * P + P, P), :]).then_inc(x_in, 16)
                store(i, 0, P, bass.ds(i * P + N_META, P))
            store(MAIN_TILES, 0, SAMPLE, bass.ds(N_META + SEQ, SAMPLE))
            sp.dma_start(D["xbc"][:, :, 0:N_META], chan_out[:, :, SAMPLE:REST]).then_inc(stored, 16)
            sp.wait_ge(stored, 16 * (4 * TILES + 2))
            sp.wait_ge(padded, 16)

        @block.scalar
        def _(act):
            act.sem_inc(even_free, 2)
            act.wait_ge(square_ready, 1)

            def norm(i):
                act.wait_ge(x_in, 16 * (i + 1))
                act.wait_ge(normed_ready, i + 1)
                nc.scalar.activation(square[:], x[:], ACT.Square, accum_out=stat[:, 0:1]).then_inc(square_ready, 1)
                act.wait_ge(square_ready, i + 2)
                nc.scalar.activation(stat[:, 1:2], stat[:, 0:1], ACT.Sqrt, bias=stat[:, 3:4],
                                     scale=1.0 / D_MODEL).then_inc(root_ready, 1)

            def copy_out(i):
                for n, j in enumerate((0, 2, 4, 6)):
                    act.wait_ge(even_done, i * 4 + n + 1)
                    if j == 0:
                        act.wait_ge(stored, i * 64 + 16)
                    dst = (token_out[:, j * 512:(j + 1) * 512] if j < 4 else
                           token_out[:, 2048:TOKW] if j == 4 else chan_out[:, 4:8, :])
                    src = (bank[:, j % 4, :] if j < 4 else bank[:, 0, 0:HEADS] if j == 4 else
                           bank[:, 2, :].rearrange("p (b t) -> p b t", b=4))
                    nc.scalar.activation(dst, src, ACT.Copy).then_inc(even_free, 1)

            norm(0)
            with act.Fori(0, MAIN_TILES) as i:
                norm(i + 1)
                copy_out(i)
            copy_out(MAIN_TILES)

        @block.vector
        def _(dve):
            chain = Chain(dve, dve_step)
            dve.sem_inc(odd_free, 2)
            dve.sem_inc(t_copied, 1)
            dve.sem_inc(stored, 16)
            nc.vector.memset(stat[:, 3:4], EPS).then_inc(square_ready, 1)
            dve.sem_inc(normed_ready, 1)

            def norm(i):
                dve.wait_ge(root_ready, i + 1)
                chain.link(nc.vector.reciprocal(stat[:, 2:3], stat[:, 1:2]))
                dve.wait_ge(transposed, i + 1)
                nc.vector.tensor_scalar(normed[:], x[:], stat[:, 2:3], None, ALU.mult).then_inc(normed_ready, 1)
                dve.wait_ge(normed_ready, i + 2)
                dve.sem_inc(x_free, 1)

            def copy_out(i):
                for n, j in enumerate((1, 3, 5, 7)):
                    dve.wait_ge(odd_done, i * 4 + n + 1)
                    if j == 1:
                        dve.wait_ge(stored, i * 64 + 16)
                    dst = (token_out[:, j * 512:(j + 1) * 512] if j < 4 else
                           chan_out[:, 0:4, :] if j == 5 else chan_out[:, 8:12, :])
                    src = bank[:, j % 4, :] if j < 4 else bank[:, j % 4, :].rearrange("p (b t) -> p b t", b=4)
                    nc.vector.tensor_copy(dst, src).then_inc(odd_free, 1)

            def copy_transposed(i):
                dve.wait_ge(transposed, i + 2)
                nc.vector.tensor_tensor(out=normed_t[:], in0=t_psum[:],
                                        in1=norm_w[:].unsqueeze(2).to_broadcast([P, KT, P]),
                                        op=ALU.mult).then_inc(t_copied, 1)

            dve.wait_ge(consts_in, 32)
            dve.sem_inc(transposed, 1)
            norm(0)
            with dve.Fori(0, MAIN_TILES) as i:
                chain.start(i + 1)
                copy_transposed(i)
                norm(i + 1)
                copy_out(i)
            copy_transposed(MAIN_TILES)
            copy_out(MAIN_TILES)

        @block.tensor
        def _(pe):
            pe.wait_ge(consts_in, 32)

            def tile(i, first):
                pe.wait_ge(normed_ready, i + 2)
                pe.wait_ge(t_copied, i + 1)
                for k in range(KT):
                    last = nc.tensor.transpose(t_psum[:, k, :], normed[:, k * P:(k + 1) * P], ident[:])
                last.then_inc(transposed, 1)
                pe.wait_ge(t_copied, i + 2)
                for j in range(ITEMS):
                    even = j % 2 == 0
                    pe.wait_ge(even_free if even else odd_free, i * 4 + j // 2 + 1)
                    if first:
                        pe.wait_ge(w_part_in[0 if j < 2 else 1 if j < 5 else 2], 16)
                    b = bank[:, j % 4, :]
                    if j < 5:
                        a, w = j * 512, 512 if j < 4 else HEADS
                        for k in range(KT):
                            last = nc.tensor.matmul(b[:, 0:w], normed_t[:, k, :], w_in[:, k, a:a + w],
                                                    start=k == 0, stop=k == KT - 1)
                    else:
                        for c in range(4):
                            a = TOKW + ((j - 5) * 4 + c) * P
                            for k in range(KT):
                                last = nc.tensor.matmul(b[:, c * P:(c + 1) * P], w_in[:, k, a:a + P],
                                                        normed_t[:, k, :], start=k == 0, stop=k == KT - 1)
                    last.then_inc(even_done if even else odd_done, 1)

            tile(0, True)
            with pe.Fori(1, TILES) as i:
                tile(i, False)


def s5_scan(nc, D):
    G2 = 2 * S5_CH
    LAG = Q + 1
    TWO_PI = 2.0 * np.pi
    PI_HI = 6.28125
    PI_LO = float(np.float32(TWO_PI - PI_HI))
    ROUND = 1.5 * 2.0 ** 23
    HALF_MAX = 1.5707963
    with ExitStack() as ctx:
        cur = lambda c: (lambda n, s, d=F32: c.enter_context(nc.sbuf_tensor("s5s_" + n, s, d)))
        sb = cur(ctx)
        sem = ctx.enter_context(stage_semaphores(nc, "s5_"))
        ident = sb("ident", [P, P])
        out_w = sb("out_w", [P, PAIRS, 2, LAG * S5_CH])
        in_w = sb("in_w", [P, PAIRS, 2, Q * S5_CH])
        toep = sb("toep", [P, S5_GROUPS, Q * S5_CH])
        b_bar = sb("b_bar", [P, PAIRS, 2, S5_CH])
        jump = sb("jump", [P, SCAN, 3, PAIRS])
        consts_in, u_in = sem("consts_in"), sem("u_in")

        with ExitStack() as c2:
            sb2 = cur(c2)
            par = sb2("par", [P, 3, PAIRS])
            b_in = sb2("b_in", [P, 2, PAIRS, S5_CH])
            c_in = sb2("c_in", [P, 2, PAIRS, S5_CH])
            skip = sb2("skip", [S5_CH, S5_GROUPS])
            tmp = sb2("tmp", [P, 16, PAIRS])
            power = sb2("power", [P, 2, PAIRS, LAG])
            down = sb2("down", [P, 2, PAIRS, Q])
            prod = sb2("prod", [P, PAIRS, LAG, S5_CH])
            prod2 = sb2("prod2", [P, PAIRS, LAG, S5_CH])
            skip_eye = sb2("skip_eye", [S5_CH, S5_GROUPS, S5_CH])
            kernels = sb2("kernels", [S5_CH, S5_GROUPS, Q * S5_CH])
            b_apart = sb2("b_apart", [P, 4, 2, 2, S5_CH])
            k_psum = c2.enter_context(nc.psum_tensor("s5_k_psum", [S5_CH, 8, Q * S5_CH], F32))
            act_done, dve_for_act, dve_step = sem("act_done"), sem("dve_for_act"), sem("p_dve_step")
            toep_zero, b_ready, k_made, k_copied, k_ready, toep_in = (sem("toep_zero"), sem("b_ready"),
                sem("k_made"), sem("k_copied"), sem("k_ready"), sem("toep_in"))
            w_ready = sem("w_ready")
            block = c2.enter_context(nc.Block())

            @block.sync
            def _(sp):
                for t, n in ((par, "s5_par"), (b_in, "s5_b"), (c_in, "s5_c"), (skip, "s5_d"), (ident, "ident")):
                    sp.dma_start(t[:], D[n]).then_inc(consts_in, 16)
                sp.wait_ge(toep_zero, 1)
                sp.wait_ge(k_ready, 1)
                for s in range(Q):
                    sp.dma_start(toep[s * S5_CH:(s + 1) * S5_CH, :, s * S5_CH:],
                                 kernels[:, :, 0:(Q - s) * S5_CH]).then_inc(toep_in, 16)
                sp.wait_ge(toep_in, 16 * Q)

            @block.gpsimd
            def _(pool):
                nc.gpsimd.memset(toep[:], 0.0).then_inc(toep_zero, 1)

            @block.scalar
            def _(act):
                act.wait_ge(consts_in, 80)
                nc.scalar.activation(tmp[:, 0, :], par[:, 2, :], ACT.Exp).then_inc(act_done, 1)
                act.wait_ge(dve_for_act, 1)
                nc.scalar.activation(tmp[:, 3, :], tmp[:, 1, :], ACT.Exp).then_inc(act_done, 1)
                act.wait_ge(dve_for_act, 2)
                nc.scalar.activation(tmp[:, 5, :], tmp[:, 4, :], ACT.Sin).then_inc(act_done, 1)
                act.wait_ge(dve_for_act, 3)
                nc.scalar.activation(tmp[:, 7, :], tmp[:, 6, :], ACT.Sin).then_inc(act_done, 1)
                with act.Fori(0, PAIRS // 4) as r:
                    act.wait_ge(k_made, r + 1)
                    nc.scalar.activation(kernels[:, bass.ds(r * 8, 8), :], k_psum[:], ACT.Copy).then_inc(k_copied, 1)

            @block.vector
            def _(dve):
                chain = Chain(dve, dve_step)
                V = nc.vector
                tt = lambda o, a, b, op: chain.link(V.tensor_tensor(out=o, in0=a, in1=b, op=op))
                T = lambda j: tmp[:, j, :]
                dve.wait_ge(act_done, 1)
                tt(T(2), par[:, 1, :], T(0), ALU.mult)
                V.tensor_tensor(out=T(1), in0=par[:, 0, :], in1=T(0), op=ALU.mult).then_inc(dve_for_act, 1)
                chain.link(V.tensor_scalar(T(8), T(2), 1.0 / TWO_PI, ROUND, ALU.mult, ALU.add))
                chain.link(V.tensor_scalar(T(8), T(8), ROUND, None, ALU.subtract))
                chain.link(V.scalar_tensor_tensor(out=T(9), in0=T(8), scalar=-PI_HI, in1=T(2), op0=ALU.mult, op1=ALU.add))
                chain.link(V.scalar_tensor_tensor(out=T(9), in0=T(8), scalar=-PI_LO, in1=T(9), op0=ALU.mult, op1=ALU.add))
                chain.link(V.tensor_scalar(T(9), T(9), 0.5, HALF_MAX, ALU.mult, ALU.min))
                V.tensor_scalar(T(4), T(9), -HALF_MAX, None, ALU.max).then_inc(dve_for_act, 1)
                dve.wait_ge(dve_for_act, 2)
                chain.link(V.tensor_scalar(T(10), T(4), -1.0, None, ALU.mult))
                tt(T(10), T(10), T(4), ALU.max)
                V.tensor_scalar(T(6), T(10), -1.0, float(np.pi / 2), ALU.mult, ALU.add).then_inc(dve_for_act, 1)
                dve.wait_ge(act_done, 4)
                a_re, a_im = power[:, 0, :, 1], power[:, 1, :, 1]
                tt(T(8), T(5), T(5), ALU.mult)
                chain.link(V.tensor_scalar(T(8), T(8), -2.0, 1.0, ALU.mult, ALU.add))
                tt(a_re, T(8), T(3), ALU.mult)
                tt(T(9), T(5), T(7), ALU.mult)
                chain.link(V.tensor_scalar(T(9), T(9), 2.0, None, ALU.mult))
                tt(a_im, T(9), T(3), ALU.mult)
                chain.link(V.memset(power[:, 0, :, 0], 1.0))
                chain.link(V.memset(power[:, 1, :, 0], 0.0))

                def complex_mult(o_re, o_im, x_re, x_im, y_re, y_im, t0, t1):
                    tt(t0, x_re, y_re, ALU.mult)
                    tt(t1, x_im, y_im, ALU.mult)
                    tt(o_re, t0, t1, ALU.subtract)
                    tt(t0, x_re, y_im, ALU.mult)
                    tt(t1, x_im, y_re, ALU.mult)
                    tt(o_im, t0, t1, ALU.add)

                for n in range(2, LAG):
                    complex_mult(power[:, 0, :, n], power[:, 1, :, n], power[:, 0, :, n - 1],
                                 power[:, 1, :, n - 1], a_re, a_im, T(8), T(9))
                for s in range(Q):
                    chain.link(V.tensor_copy(down[:, :, :, s], power[:, :, :, Q - 1 - s]))
                for h in range(2):
                    chain.link(V.tensor_copy(jump[:, 0, 1 + h, :], power[:, h, :, Q]))
                for j in range(1, SCAN):
                    complex_mult(jump[:, j, 1, :], jump[:, j, 2, :], jump[:, j - 1, 1, :], jump[:, j - 1, 2, :],
                                 jump[:, 0, 1, :], jump[:, 0, 2, :], T(8), T(9))
                chain.link(V.tensor_scalar(jump[:, :, 0, :], jump[:, :, 2, :], -1.0, None, ALU.mult))
                lre, lim = par[:, 0, :], par[:, 1, :]
                tt(T(8), lre, lre, ALU.mult)
                tt(T(9), lim, lim, ALU.mult)
                tt(T(8), T(8), T(9), ALU.add)
                chain.link(V.reciprocal(T(10), T(8)))
                chain.link(V.tensor_scalar(T(11), a_re, -1.0, None, ALU.add))
                tt(T(8), T(11), lre, ALU.mult)
                tt(T(9), a_im, lim, ALU.mult)
                tt(T(8), T(8), T(9), ALU.add)
                tt(T(12), T(8), T(10), ALU.mult)
                tt(T(8), a_im, lre, ALU.mult)
                tt(T(9), T(11), lim, ALU.mult)
                tt(T(8), T(8), T(9), ALU.subtract)
                tt(T(13), T(8), T(10), ALU.mult)
                f = lambda j: T(j).unsqueeze(2).to_broadcast([P, PAIRS, S5_CH])
                p0, p1 = prod[:, :, 0, :], prod2[:, :, 0, :]
                complex_mult(b_bar[:, :, 0, :], b_bar[:, :, 1, :], f(12), f(13), b_in[:, 0], b_in[:, 1], p0, p1)
                lagged = lambda t: t.unsqueeze(3).to_broadcast([P, PAIRS, LAG, S5_CH])
                chans = lambda t: t.unsqueeze(2).to_broadcast([P, PAIRS, LAG, S5_CH])
                o = lambda h: out_w[:, :, h, :].rearrange("p g (l c) -> p g l c", c=S5_CH)
                tt(prod[:], chans(c_in[:, 0]), lagged(power[:, 0]), ALU.mult)
                tt(prod2[:], chans(c_in[:, 1]), lagged(power[:, 1]), ALU.mult)
                tt(o(0), prod[:], prod2[:], ALU.subtract)
                tt(prod[:], chans(c_in[:, 0]), lagged(power[:, 1]), ALU.mult)
                tt(prod2[:], chans(c_in[:, 1]), lagged(power[:, 0]), ALU.mult)
                chain.link(V.scalar_tensor_tensor(
                    out=o(1).rearrange("p g l c -> p g (l c)"), in0=prod[:].rearrange("p g l c -> p g (l c)"),
                    scalar=-1.0, in1=prod2[:].rearrange("p g l c -> p g (l c)"), op0=ALU.mult, op1=ALU.subtract))
                chain.link(V.memset(b_apart[:], 0.0))
                dve.sem_inc(w_ready, 1)
                stepped = lambda t: t.unsqueeze(3).to_broadcast([P, PAIRS, Q, S5_CH])
                chans8 = lambda t: t.unsqueeze(2).to_broadcast([P, PAIRS, Q, S5_CH])
                iw = lambda h: in_w[:, :, h, :].rearrange("p g (l c) -> p g l c", c=S5_CH)
                base = chain.n
                with dve.Fori(0, PAIRS // 4) as r:
                    chain.start(base + 2 * r)
                    dve.wait_ge(k_copied, r + 1)
                    for g in range(2):
                        rows = slice(g * 64, g * 64 + 64)
                        chain.link(V.tensor_copy(b_apart[rows, :, g, :, :], b_bar[rows, bass.ds(r * 4, 4), :, :]))
                    dve.sem_inc(b_ready, 1)
                chain.start(base + PAIRS // 2)
                complex_mult(iw(0), iw(1), stepped(down[:, 0]), stepped(down[:, 1]), chans8(b_bar[:, :, 0, :]),
                             chans8(b_bar[:, :, 1, :]), prod[:, :, 0:Q, :], prod2[:, :, 0:Q, :])
                tt(skip_eye[:], skip[:].unsqueeze(2).to_broadcast([S5_CH, S5_GROUPS, S5_CH]),
                   ident[0:S5_CH, 0:S5_CH].unsqueeze(1).to_broadcast([S5_CH, S5_GROUPS, S5_CH]), ALU.mult)
                dve.wait_ge(k_copied, PAIRS // 4 + 1)
                V.tensor_tensor(out=kernels[:, :, 0:S5_CH], in0=kernels[:, :, 0:S5_CH], in1=skip_eye[:],
                                op=ALU.add).then_inc(k_ready, 1)

            @block.tensor
            def _(pe):
                pe.sem_inc(k_copied, 1)
                pe.wait_ge(w_ready, 1)
                with pe.Fori(0, PAIRS // 4) as r:
                    pe.wait_ge(b_ready, r + 1)
                    pe.wait_ge(k_copied, r + 1)
                    for j in range(4):
                        for g in range(2):
                            for h in range(2):
                                last = nc.tensor.matmul(k_psum[:, 2 * j + g, :], b_apart[:, j, g, h, :],
                                                        out_w[:, bass.ds(r * 4 + j, 1), h, 0:Q * S5_CH],
                                                        start=h == 0, stop=h == 1)
                    last.then_inc(k_made, 1)

        state = sb("state", [P, PAIRS, 2, CHUNKS])
        u = sb("u", [P, Q, D_MODEL])

        with ExitStack() as c2:
            sb2 = cur(c2)
            u_pair = sb2("u_pair", [P, 2, Q, S5_CH])
            u_rest = sb2("u_rest", [CH_REST, 2, Q, S5_CH])
            in_pair = sb2("in_pair", [P, 2, P])
            u_t = sb2("u_t", [P, 2, CHUNKS])
            in_t = sb2("in_t", [P, 2, P])
            ps = lambda n, s: c2.enter_context(nc.psum_tensor("s5p_" + n, s, F32))
            u_psum, in_psum = ps("u_psum", [P, 512]), ps("in_psum", [P, 2, P])
            v_psum, y_psum = ps("v_psum", [P, 2, CHUNKS]), ps("y_psum", [P, 2, Q, S5_CH])
            u_picked, in_picked, rest_in = sem("u_picked"), sem("in_picked"), sem("rest_in")
            u_turned, in_turned, u_t_ready, in_t_ready = sem("u_turned"), sem("in_turned"), sem("u_t_ready"), sem("in_t_ready")
            v_made, v_kept, y_made, y_kept = sem("v_made"), sem("v_kept"), sem("y_made"), sem("y_kept")
            block = c2.enter_context(nc.Block())
            rest_rows = D["u"][SEQ:SEQ + REST, :].rearrange("(k s) c -> k s c", s=Q)

            @block.sync
            def _(sp):
                sp.dma_start(u[:], D["u"][0:SEQ, :].rearrange("(k s) c -> k s c", s=Q)).then_inc(u_in, 16)
                sp.sem_inc(u_turned, 1)
                with sp.Fori(0, PAIRS) as r:
                    sp.wait_ge(u_turned, r + 1)
                    for g in range(2):
                        sp.dma_start(u_rest[:, g, :, :], rest_rows[:, :, bass.ds(r * G2 + g * S5_CH, S5_CH)]).then_inc(rest_in, 16)

            @block.gpsimd
            def _(pool):
                pool.wait_ge(u_in, 16)
                with pool.Fori(0, PAIRS) as r:
                    pool.wait_ge(u_turned, r + 1)
                    for g in range(2):
                        last = nc.gpsimd.tensor_copy(u_pair[:, g, :, :], u[:, :, bass.ds(r * G2 + g * S5_CH, S5_CH)])
                    last.then_inc(u_picked, 1)
                    pool.wait_ge(in_turned, r + 1)
                    nc.gpsimd.tensor_copy(in_pair[:].unsqueeze(1), in_w[:, bass.ds(r, 1), :, :]).then_inc(in_picked, 1)

            @block.tensor
            def _(pe):
                pe.sem_inc(in_turned, 1)
                with pe.Fori(0, PAIRS) as r:
                    pe.wait_ge(u_picked, r + 1)
                    pe.wait_ge(rest_in, 32 * r + 32)
                    pe.wait_ge(u_t_ready, r + 1)
                    for g in range(2):
                        nc.tensor.transpose(u_psum[:, g * P:(g + 1) * P], u_pair[:, g].rearrange("p s c -> p (s c)"), ident[:])
                        last = nc.tensor.transpose(u_psum[:, 2 * P + g * CH_REST:2 * P + (g + 1) * CH_REST],
                                                   u_rest[:, g].rearrange("p s c -> p (s c)"), ident[0:CH_REST, 0:CH_REST])
                    last.then_inc(u_turned, 1)
                    pe.wait_ge(in_picked, r + 1)
                    pe.wait_ge(in_t_ready, r + 1)
                    for h in range(2):
                        last = nc.tensor.transpose(in_psum[:, h, :], in_pair[:, h, :], ident[:])
                    last.then_inc(in_turned, 1)
                    pe.wait_ge(u_t_ready, r + 2)
                    pe.wait_ge(in_t_ready, r + 2)
                    pe.wait_ge(v_kept, r + 1)
                    for h in range(2):
                        for g in range(2):
                            last = nc.tensor.matmul(v_psum[g * 64:g * 64 + 64, h, :], in_t[:, h, g * 64:g * 64 + 64],
                                                    u_t[:, g, :], start=True, stop=True)
                    last.then_inc(v_made, 1)
                    pe.wait_ge(y_kept, r + 1)
                    for g in range(2):
                        last = nc.tensor.matmul(y_psum[:, g].rearrange("p t c -> p (t c)"), u_t[:, g, CH_REST:],
                                                toep[:, bass.ds(r * 2 + g, 1), :], start=True, stop=True)
                    last.then_inc(y_made, 1)

            @block.scalar
            def _(act):
                act.sem_inc(u_t_ready, 1)
                act.sem_inc(y_kept, 1)
                with act.Fori(0, PAIRS) as r:
                    act.wait_ge(u_turned, r + 2)
                    act.wait_ge(y_made, r + 1)
                    nc.scalar.activation(u_t[:, :, CH_REST:], u_psum[:, 0:2 * P].rearrange("p (g k) -> p g k", g=2), ACT.Copy)
                    nc.scalar.activation(u_t[:, :, 0:CH_REST],
                                         u_psum[:, 2 * P:2 * P + 2 * CH_REST].rearrange("p (g k) -> p g k", g=2),
                                         ACT.Copy).then_inc(u_t_ready, 1)
                    act.wait_ge(y_made, r + 2)
                    for g in range(2):
                        last = nc.scalar.activation(u[:, :, bass.ds(r * G2 + g * S5_CH, S5_CH)], y_psum[:, g], ACT.Copy)
                    last.then_inc(y_kept, 1)

            @block.vector
            def _(dve):
                dve.sem_inc(in_t_ready, 1)
                dve.sem_inc(v_kept, 1)
                dve.sem_inc(y_made, 1)
                with dve.Fori(0, PAIRS) as r:
                    dve.wait_ge(in_turned, r + 2)
                    dve.wait_ge(v_kept, r + 1)
                    nc.vector.tensor_copy(in_t[:], in_psum[:]).then_inc(in_t_ready, 1)
                    dve.wait_ge(v_made, r + 1)
                    nc.vector.tensor_copy(state[:, bass.ds(r, 1), :, :], v_psum[:].unsqueeze(1)).then_inc(v_kept, 1)

        rest_start = sb("rest_start", [P, PAIRS, 2, CH_REST])
        with ExitStack() as c2:
            sb2 = cur(c2)
            end = sb2("end", [P, PAIRS, 2, SEQS])
            last_prompt = sb2("last_prompt", [P, PAIRS, 2])
            t0 = sb2("t0", [P, PAIRS, 2, BLOCKS])
            t1 = sb2("t1", [P, PAIRS, 2, BLOCKS])
            h0_in, ends_ready, ends_out, sc_step = sem("h0_in"), sem("ends_ready"), sem("ends_out"), sem("sc_step")
            block = c2.enter_context(nc.Block())

            @block.sync
            def _(sp):
                sp.dma_start(rest_start[:, :, :, 0:SEQS], D["s5_h0"]).then_inc(h0_in, 16)
                sp.wait_ge(ends_ready, 1)
                sp.dma_start(D["s5_end_sample"], end[:]).then_inc(ends_out, 16)
                sp.dma_start(D["s5_end_prompt"], last_prompt[:]).then_inc(ends_out, 16)
                sp.wait_ge(ends_out, 32)

            @block.vector
            def _(dve):
                chain = Chain(dve, sc_step)
                V = nc.vector
                tt = lambda o, a, b, op: chain.link(V.tensor_tensor(out=o, in0=a, in1=b, op=op))

                def advance(dst, src, j, n, out=None):
                    a, b = t0[:, :, :, 0:n], t1[:, :, :, 0:n]
                    tab = lambda c: jump[:, j, c, :].unsqueeze(2).to_broadcast([P, PAIRS, n])
                    for h in range(2):
                        V.tensor_tensor(out=b[:, :, h], in0=src[:, :, 1 - h], in1=tab(2 * h), op=ALU.mult)
                        last = V.tensor_tensor(out=a[:, :, h], in0=src[:, :, h], in1=tab(1), op=ALU.mult)
                    chain.link(last)
                    tt(a, a, b, ALU.add)
                    tt(dst if out is None else out, dst, a, ALU.add)

                prompt = state[:, :, :, SEQS:].rearrange("p g h (b j) -> p g h b j", j=SCAN)
                for j in range(1, SCAN):
                    advance(prompt[:, :, :, :, j], prompt[:, :, :, :, j - 1], 0, BLOCKS)
                for b in range(1, BLOCKS):
                    advance(prompt[:, :, :, b:b + 1, SCAN - 1], prompt[:, :, :, b - 1:b, SCAN - 1], SCAN - 1, 1)
                for j in range(SCAN - 1):
                    advance(prompt[:, :, :, 1:, j], prompt[:, :, :, :BLOCKS - 1, SCAN - 1], j, BLOCKS - 1)
                dve.wait_ge(h0_in, 16)
                advance(state[:, :, :, 0:SEQS], rest_start[:, :, :, 0:SEQS], 0, SEQS, out=end[:])
                chain.link(V.tensor_copy(last_prompt[:], state[:, :, :, CHUNKS - 1]))
                chain.link(V.memset(rest_start[:, :, :, SEQS], 0.0))
                V.tensor_copy(rest_start[:, :, :, SEQS + 1], state[:, :, :, SEQS]).then_inc(ends_ready, 1)

        with ExitStack() as c2:
            sb2 = cur(c2)
            start = sb2("start", [P, 2, 2, CHUNKS])
            u_rest = sb2("u_rest2", [P, 2, Q, S5_CH])
            u_t = sb2("u_t2", [P, 2, P])
            y_rest = sb2("y_rest", [CH_REST, 2, Q, S5_CH])
            ps = lambda n, s: c2.enter_context(nc.psum_tensor("s5p_" + n, s, F32))
            u_psum = ps("u_psum2", [P, 2, P])
            y_psum, r_psum = ps("y_psum2", [P, 2, Q, S5_CH]), ps("r_psum", [P, 2, Q, S5_CH])
            rest_in, u_turned, u_t_ready = sem("rest_in2"), sem("u_turned2"), sem("u_t_ready2")
            zeroed, start_ready, y_made, y_kept, r_made, r_kept, r_out, y_out = (sem(n) for n in (
                "zeroed", "start_ready", "y_made2", "y_kept2", "r_made", "r_kept", "r_out", "y_out"))
            block = c2.enter_context(nc.Block())
            rest_u = D["u"][SEQ:SEQ + REST, :].rearrange("(k s) c -> k s c", s=Q)
            rest_y = D["y5"][SEQ:SEQ + REST, :].rearrange("(k s) c -> k s c", s=Q)

            @block.sync
            def _(sp):
                sp.sem_inc(u_turned, 1)
                sp.wait_ge(zeroed, 2)
                with sp.Fori(0, PAIRS) as r:
                    sp.wait_ge(u_turned, r + 1)
                    for g in range(2):
                        sp.dma_start(u_rest[0:CH_REST, g, :, :], rest_u[:, :, bass.ds(r * G2 + g * S5_CH, S5_CH)]).then_inc(rest_in, 16)
                    sp.wait_ge(r_kept, r + 2)
                    for g in range(2):
                        sp.dma_start(rest_y[:, :, bass.ds(r * G2 + g * S5_CH, S5_CH)], y_rest[:, g, :, :]).then_inc(r_out, 16)
                sp.wait_ge(y_kept, PAIRS + 1)
                sp.dma_start(D["y5"][0:SEQ, :].rearrange("(k s) c -> k s c", s=Q), u[:]).then_inc(y_out, 16)
                sp.wait_ge(r_out, 32 * PAIRS + 32)
                sp.wait_ge(y_out, 16)

            @block.gpsimd
            def _(pool):
                nc.gpsimd.memset(start[:], 0.0).then_inc(zeroed, 1)
                nc.gpsimd.memset(u_rest[:], 0.0).then_inc(zeroed, 1)
                pool.sem_inc(r_out, 32)

            @block.scalar
            def _(act):
                act.sem_inc(u_t_ready, 1)
                act.sem_inc(r_kept, 1)
                with act.Fori(0, PAIRS) as r:
                    act.wait_ge(u_turned, r + 2)
                    nc.scalar.activation(u_t[:], u_psum[:], ACT.Copy).then_inc(u_t_ready, 1)
                    act.wait_ge(r_made, r + 1)
                    act.wait_ge(r_out, 32 * r + 32)
                    nc.scalar.activation(y_rest[:], r_psum[0:CH_REST], ACT.Copy).then_inc(r_kept, 1)

            @block.vector
            def _(dve):
                dve.wait_ge(zeroed, 2)
                dve.sem_inc(y_kept, 1)
                with dve.Fori(0, PAIRS) as r:
                    dve.wait_ge(r_kept, r + 1)
                    for g in range(2):
                        rows = slice(g * 64, g * 64 + 64)
                        nc.vector.tensor_copy(start[rows, g, :, 0:CH_REST].unsqueeze(1), rest_start[rows, bass.ds(r, 1), :, :])
                        last = nc.vector.tensor_copy(start[rows, g, :, CH_REST:].unsqueeze(1),
                                                     state[rows, bass.ds(r, 1), :, CH_REST - 1:CHUNKS - 1])
                    last.then_inc(start_ready, 1)
                    dve.wait_ge(y_made, r + 1)
                    for g in range(2):
                        cols = u[:, :, bass.ds(r * G2 + g * S5_CH, S5_CH)]
                        last = nc.vector.tensor_tensor(out=cols, in0=cols, in1=y_psum[:, g], op=ALU.add)
                    last.then_inc(y_kept, 1)

            @block.tensor
            def _(pe):
                with pe.Fori(0, PAIRS) as r:
                    pe.wait_ge(rest_in, 32 * r + 32)
                    pe.wait_ge(u_t_ready, r + 1)
                    for g in range(2):
                        last = nc.tensor.transpose(u_psum[:, g, :], u_rest[:, g].rearrange("p s c -> p (s c)"), ident[:])
                    last.then_inc(u_turned, 1)
                    pe.wait_ge(start_ready, r + 1)
                    pe.wait_ge(y_kept, r + 1)
                    for g in range(2):
                        for h in range(2):
                            last = nc.tensor.matmul(y_psum[:, g].rearrange("p t c -> p (t c)"), start[:, g, h, CH_REST:],
                                                    out_w[:, bass.ds(r, 1), h, S5_CH:], start=h == 0, stop=h == 1)
                    last.then_inc(y_made, 1)
                    pe.wait_ge(r_kept, r + 1)
                    pe.wait_ge(u_t_ready, r + 2)
                    for g in range(2):
                        o = r_psum[:, g].rearrange("p t c -> p (t c)")
                        nc.tensor.matmul(o, u_t[:, g, :], toep[:, bass.ds(r * 2 + g, 1), :], start=True, stop=False)
                        for h in range(2):
                            last = nc.tensor.matmul(o, start[:, g, h, 0:P], out_w[:, bass.ds(r, 1), h, S5_CH:],
                                                    start=False, stop=h == 1)
                    last.then_inc(r_made, 1)


def mamba_scan(nc, D):
    SEGS = SEQS + 1
    with ExitStack() as ctx:
        sb = lambda n, s, d=F32: ctx.enter_context(nc.sbuf_tensor("m2s_" + n, s, d))
        sem = ctx.enter_context(stage_semaphores(nc, "m2_"))
        ident = sb("ident", [P, P])
        after = sb("after", [P, P])
        upto = sb("upto", [P, P])
        ones = sb("ones", [P, P])
        after_seg = sb("after_seg", [P, P])
        upto_seg = sb("upto_seg", [P, P])
        in_seg = sb("in_seg", [P, SEGS, P])
        conv_w = sb("conv_w", [P, XB, TAPS])
        conv_b = sb("conv_b", [P, XB])
        head_par = sb("head_par", [P, 3, HEADS])
        a_neg = sb("a_neg", [P, HEADS])
        window = sb("window", [P, XB, P + TAPS - 1])
        conv = sb("conv", [P, XB, P])
        tap = sb("tap", [P, XB, P])
        xbc = sb("xbc", [P, XB, P])
        dt_raw = sb("dt_raw", [P, HEADS])
        small = sb("small", [P, 6, HEADS])
        dt = sb("dt", [P, HEADS])
        da = sb("da", [P, HEADS])
        e_acs = sb("e_acs", [P, HEADS])
        e_rev = sb("e_rev", [P, HEADS])
        e_tot = sb("e_tot", [P, HEADS])
        x_tok = sb("x_tok", [P, HEADS, HD])
        b_tok = sb("b_tok", [P, 2, NS])
        x_dt = sb("x_dt", [P, HEADS, HD])
        x_w = sb("x_w", [P, HEADS, HD])
        x_skip = sb("x_skip", [P, HEADS, HD])
        da_upto = sb("da_upto", [P, HEADS, P])
        decay = sb("decay", [P, HEADS, P])
        cb_masked = sb("cb_masked", [P, 2, P])
        y = sb("y", [P, HEADS, HD])
        state = sb("state", [P, HEADS, HD])
        ps_a = ctx.enter_context(nc.psum_tensor("m2p_a", [P, 4, 512], F32))
        ps_b = ctx.enter_context(nc.psum_tensor("m2p_b", [P, 3, 512], F32))
        ps_c = ctx.enter_context(nc.psum_tensor("m2p_c", [P, 512], F32))
        CB = 256

        consts_in, tile_in, conv_done, xbc_ready = sem("consts_in"), sem("tile_in"), sem("conv_done"), sem("xbc_ready")
        turned, tok_ready, b_ready = sem("turned"), sem("tok_ready"), sem("b_ready")
        abs_ready, soft_ready, dt_ready, a_ready = sem("abs_ready"), sem("soft_ready"), sem("dt_ready"), sem("a_ready")
        upto_ready, sums_made, sums_ready = sem("upto_ready"), sem("sums_made"), sem("sums_ready")
        seg_made, decay_ready, w_ready = sem("seg_made"), sem("decay_ready"), sem("w_ready")
        xw_ready, skip_ready, y_made, y_ready, st_made = sem("xw_ready"), sem("skip_ready"), sem("y_made"), sem("y_ready"), sem("st_made")
        state_ready, y_out, dve_step, act_step, pool_step = sem("state_ready"), sem("y_out"), sem("dve_step"), sem("act_step"), sem("pool_step")
        heads = lambda t: t.unsqueeze(2).to_broadcast([P, HEADS, HD])
        tt = lambda e, o, a, b, op: e.tensor_tensor(out=o, in0=a, in1=b, op=op)

        def dve_front(dve, chain, k, views):
            V = nc.vector
            dve.wait_ge(tile_in, 32 * k + 32)
            dve.wait_ge(xbc_ready, k + 1)
            for w_in, o in views:
                dims = list(o(conv).shape)
                wt = lambda j: (conv_w[:, :, j].unsqueeze(2).to_broadcast(dims) if len(dims) == 3 else
                                conv_w[:, :, j].unsqueeze(2).unsqueeze(3).to_broadcast(dims))
                bias = (conv_b[:].unsqueeze(2).to_broadcast(dims) if len(dims) == 3 else
                        conv_b[:].unsqueeze(2).unsqueeze(3).to_broadcast(dims))
                chain.link(tt(V, o(conv), w_in(0), wt(0), ALU.mult))
                for j in range(1, TAPS):
                    chain.link(tt(V, o(tap), w_in(j), wt(j), ALU.mult))
                    chain.link(tt(V, o(conv), o(conv), o(tap), ALU.add))
                chain.link(tt(V, o(conv), o(conv), bias, ALU.add))
            dve.sem_inc(conv_done, 1)
            chain.link(tt(V, small[:, 0, :], dt_raw[:], head_par[:, 0, :], ALU.add))
            chain.link(V.tensor_scalar(small[:, 1, :], small[:, 0, :], -1.0, None, ALU.mult))
            tt(V, small[:, 1, :], small[:, 0, :], small[:, 1, :], ALU.max).then_inc(abs_ready, 1)
            chain.link(V.tensor_scalar(small[:, 4, :], small[:, 0, :], 0.0, None, ALU.max))
            dve.wait_ge(soft_ready, k + 1)
            chain.link(tt(V, dt[:], small[:, 4, :], small[:, 3, :], ALU.add))
            tt(V, da[:], dt[:], a_neg[:], ALU.mult).then_inc(dt_ready, 1)

        def dve_middle(dve, chain, k, cb_mask):
            V = nc.vector
            dve.wait_ge(turned, k + 1)
            chain.link(V.tensor_copy(x_tok[:], ps_b[:, 0:2, :].rearrange("p b (h d) -> p (b h) d", d=HD)))
            dve.sem_inc(tok_ready, 1)
            chain.link(tt(V, x_dt[:], x_tok[:], heads(dt[:]), ALU.mult))
            dve.wait_ge(sums_ready, k + 2)
            chain.link(tt(V, cb_masked[:], ps_c[:, CB:CB + 2 * P].rearrange("p (g l) -> p g l", g=2),
                          cb_mask.unsqueeze(1).to_broadcast([P, 2, P]), ALU.mult))
            dve.wait_ge(decay_ready, k + 1)
            for g in range(2):
                part = decay[:, g * HPG:(g + 1) * HPG, :]
                last = tt(V, part, part, cb_masked[:, g, :].unsqueeze(1).to_broadcast([P, HPG, P]), ALU.mult)
            last.then_inc(w_ready, 1)
            tt(V, x_w[:], x_dt[:], heads(e_rev[:]), ALU.mult).then_inc(xw_ready, 1)

        def dve_y(dve, chain, k):
            V = nc.vector
            dve.wait_ge(y_made, k + 1)
            dve.wait_ge(y_out, 16 * k + 16)
            chain.link(tt(V, y[:], ps_a[:, 2:4, :].rearrange("p b (h d) -> p (b h) d", d=HD), heads(e_acs[:]), ALU.mult))
            chain.link(tt(V, y[:], y[:], ps_a[:, 0:2, :].rearrange("p b (h d) -> p (b h) d", d=HD), ALU.add))
            dve.wait_ge(skip_ready, k + 1)
            tt(V, y[:], y[:], x_skip[:], ALU.add).then_inc(y_ready, 1)

        def pool_tile(pool, k, mask):
            G = nc.gpsimd
            pool.wait_ge(dt_ready, k + 1)
            pool.wait_ge(seg_made, k + 1)
            tt(G, da_upto[:], da[:].unsqueeze(2).to_broadcast([P, HEADS, P]),
               mask.unsqueeze(1).to_broadcast([P, HEADS, P]), ALU.mult).then_inc(upto_ready, 1)
            pool.wait_ge(tok_ready, k + 1)
            pool.wait_ge(y_ready, k + 1)
            tt(G, x_skip[:], x_tok[:], heads(head_par[:, 2, :]), ALU.mult).then_inc(skip_ready, 1)

        def pe_front(pe, k, m_after, m_upto):
            T = nc.tensor
            pe.wait_ge(xbc_ready, k + 2)
            pe.wait_ge(state_ready, k + 1)
            pe.wait_ge(b_ready, k + 1)
            for c in range(10):
                last = T.transpose(ps_b[:, c // 4, (c % 4) * P:(c % 4 + 1) * P], xbc[:, c, :], ident[:])
            last.then_inc(turned, 1)
            pe.wait_ge(dt_ready, k + 1)
            pe.wait_ge(sums_ready, k + 1)
            pe.wait_ge(w_ready, k + 1)
            for n, m in enumerate((m_upto, m_after, ones)):
                T.matmul(ps_c[:, n * HEADS:(n + 1) * HEADS], m[:], da[:], start=True, stop=True)
            for g in range(2):
                last = T.matmul(ps_c[:, CB + g * P:CB + (g + 1) * P], xbc[:, 8 + g, :], xbc[:, 10 + g, :], start=True, stop=True)
            last.then_inc(sums_made, 1)
            pe.wait_ge(upto_ready, k + 1)
            pe.wait_ge(y_ready, k + 1)
            for n in range(4):
                last = T.matmul(ps_a[:, n, :], m_after[:], da_upto[:, 4 * n:4 * n + 4, :].rearrange("p h l -> p (h l)"), start=True, stop=True)
            last.then_inc(seg_made, 1)

        def pe_inside(pe, k):
            pe.wait_ge(w_ready, k + 2)
            for h in range(HEADS):
                last = nc.tensor.matmul(ps_a[:, h // HPG, (h % HPG) * HD:(h % HPG + 1) * HD], decay[:, h, :], x_dt[:, h, :],
                                        start=True, stop=True)
            return last

        rest_steps = []

        with ExitStack() as c2:
            sb2 = lambda n, s, d=F32: c2.enter_context(nc.sbuf_tensor("m2r_" + n, s, d))
            sem2 = c2.enter_context(stage_semaphores(nc, "m2r_"))
            win_s = sb2("win_s", [P, XB, SEQS, STEPS + TAPS - 1])
            win_m = sb2("win_m", [P, XB, N_META + TAPS - 1])
            tail = sb2("tail", [P, XB, SEQS, TAPS - 1])
            start = sb2("start", [P, SEQS, HEADS, HD])
            c_apart = sb2("c_apart", [P, 2, SEQS, P])
            x_seg = sb2("x_seg", [P, HEADS, HD])
            e_seg = sb2("e_seg", [P, SEGS, HEADS])
            xbc_raw_in, zeroed, c_ready, start_in, tail_ready, tail_out = (sem2(n) for n in (
                "xbc_raw_in", "zeroed", "c_ready", "start_in", "tail_ready", "tail_out"))
            seg_sum_made, seg_sum_ready, x_seg_ready, seg_state_made, seg_state_ready, ends_out = (sem2(n) for n in (
                "seg_sum_made", "seg_sum_ready", "x_seg_ready", "seg_state_made", "seg_state_ready", "ends_out"))
            block = c2.enter_context(nc.Block())

            @block.sync
            def _(sp):
                for t, n in ((ident, "ident"), (after, "after"), (upto, "upto"), (ones, "ones"), (after_seg, "after_seg"),
                             (upto_seg, "upto_seg"), (in_seg, "in_seg"), (conv_w, "conv_w"), (conv_b, "conv_b"), (head_par, "head_par")):
                    sp.dma_start(t[:], D[n]).then_inc(consts_in, 16)
                rest = SEQ + N_META
                sp.dma_start(tail[:], D["conv_past"]).then_inc(xbc_raw_in, 16)
                sp.dma_start(window[:, :, 0:SAMPLE], D["xbc"][:, :, rest:rest + SAMPLE]).then_inc(xbc_raw_in, 16)
                sp.wait_ge(zeroed, 1)
                sp.dma_start(win_m[:, :, TAPS - 1:], D["xbc"][:, :, 0:N_META]).then_inc(tile_in, 16)
                sp.dma_start(dt_raw[:], D["dt"][SEQ:ROWS, :]).then_inc(tile_in, 16)
                sp.dma_start(start[:], D["ssm_h0"]).then_inc(start_in, 16)
                sp.wait_ge(tail_ready, 1)
                sp.dma_start(D["conv_end_sample"], tail[:]).then_inc(tail_out, 16)
                sp.wait_ge(y_ready, 2)
                sp.dma_start(D["ym"][SEQ:ROWS, :], y[:].rearrange("p h d -> p (h d)")).then_inc(y_out, 16)
                sp.wait_ge(seg_state_ready, SEQS)
                sp.dma_start(D["ssm_end_sample"], start[:]).then_inc(ends_out, 16)
                sp.wait_ge(ends_out, 16)
                sp.wait_ge(tail_out, 16)
                sp.wait_ge(y_out, 32)

            @block.gpsimd
            def _(pool):
                G = nc.gpsimd
                G.memset(win_m[:, :, 0:TAPS - 1], 0.0).then_inc(zeroed, 1)
                G.memset(conv[:], 0.0).then_inc(zeroed, 1)
                G.memset(c_apart[:], 0.0).then_inc(zeroed, 1)
                pool.sem_inc(seg_made, 1)
                pool.sem_inc(y_ready, 1)
                pool_tile(pool, 0, upto_seg[:])

            @block.scalar
            def _(act):
                act.wait_ge(consts_in, 160)
                act.sem_inc(xbc_ready, 1)
                act.sem_inc(b_ready, 1)
                act.sem_inc(sums_ready, 1)
                nc.scalar.activation(small[:, 5, :], head_par[:, 1, :], ACT.Exp).then_inc(a_ready, 1)
                act.wait_ge(conv_done, 1)
                nc.scalar.activation(xbc[:], conv[:], ACT.Silu).then_inc(xbc_ready, 1)
                act.wait_ge(abs_ready, 1)
                nc.scalar.activation(small[:, 2, :], small[:, 1, :], ACT.Exp, scale=-1.0).then_inc(act_step, 1)
                act.wait_ge(act_step, 1)
                nc.scalar.activation(small[:, 3, :], small[:, 2, :], ACT.Ln, bias=ones[:, 0:1]).then_inc(soft_ready, 1)
                act.wait_ge(turned, 1)
                nc.scalar.activation(b_tok[:], ps_b[:, 2, 0:2 * NS].rearrange("p (g n) -> p g n", g=2), ACT.Copy).then_inc(b_ready, 1)
                act.wait_ge(sums_made, 1)
                nc.scalar.activation(e_acs[:], ps_c[:, 0:HEADS], ACT.Exp)
                nc.scalar.activation(e_rev[:], ps_c[:, HEADS:2 * HEADS], ACT.Exp).then_inc(sums_ready, 1)
                act.wait_ge(seg_made, 2)
                nc.scalar.activation(decay[:], ps_a[:].rearrange("p b (h l) -> p (b h) l", l=P), ACT.Exp).then_inc(decay_ready, 1)
                act.wait_ge(seg_sum_made, 1)
                nc.scalar.activation(e_seg[:], ps_c[:, 0:SEGS * HEADS].rearrange("p (b h) -> p b h", h=HEADS), ACT.Exp).then_inc(seg_sum_ready, 1)

            @block.vector
            def _(dve):
                V = nc.vector
                chain = Chain(dve, dve_step)
                dve.sem_inc(y_out, 16)
                dve.sem_inc(w_ready, 1)
                dve.sem_inc(state_ready, 1)
                dve.wait_ge(a_ready, 1)
                chain.link(V.tensor_scalar(a_neg[:], small[:, 5, :], -1.0, None, ALU.mult))
                dve.wait_ge(xbc_raw_in, 32)
                chain.link(V.tensor_copy(win_s[:, :, :, 0:TAPS - 1], tail[:]))
                chain.link(V.tensor_copy(win_s[:, :, :, TAPS - 1:], window[:, :, 0:SAMPLE].rearrange("p x (b t) -> p x b t", b=SEQS)))
                V.tensor_copy(tail[:], win_s[:, :, :, STEPS:]).then_inc(tail_ready, 1)
                dve.wait_ge(zeroed, 3)
                dve_front(dve, chain, 0, [
                    (lambda j: win_s[:, :, :, j:j + STEPS], lambda t: t[:, :, 0:SAMPLE].rearrange("p x (b t) -> p x b t", b=SEQS)),
                    (lambda j: win_m[:, :, j:j + N_META], lambda t: t[:, :, SAMPLE:REST])])
                dve.wait_ge(xbc_ready, 2)
                for g in range(2):
                    c = c_apart[:, g]
                    diag = bass.AP(tensor=c.tensor, offset=c.offset, ap=[list(c.ap[0]), [P + STEPS, SEQS], [1, STEPS]])
                    last = V.tensor_copy(diag, xbc[:, 10 + g, 0:SAMPLE].rearrange("p (b t) -> p b t", b=SEQS))
                last.then_inc(c_ready, 1)
                dve_middle(dve, chain, 0, upto_seg[:])
                dve.wait_ge(xw_ready, 1)
                dve_y(dve, chain, 0)
                dve.wait_ge(seg_sum_ready, 1)
                dve.wait_ge(start_in, 16)
                for b in range(SEGS):
                    if b:
                        dve.wait_ge(seg_state_made, b)
                    V.tensor_scalar(x_seg[:], x_w[:], in_seg[:, b, 0:1], None, ALU.mult).then_inc(x_seg_ready, 1)
                    e = e_seg[:, b, :].unsqueeze(2).to_broadcast([P, HEADS, HD])
                    new = ps_b[:, 0:2, :].rearrange("p b (h d) -> p (b h) d", d=HD)
                    if b < SEQS:
                        chain.link(tt(V, start[:, b], start[:, b], e, ALU.mult))
                        dve.wait_ge(seg_state_made, b + 1)
                        tt(V, start[:, b], start[:, b], new, ALU.add).then_inc(seg_state_ready, 1)
                    else:
                        dve.wait_ge(seg_state_made, b + 1)
                        V.tensor_copy(state[:], new).then_inc(state_ready, 1)
                rest_steps.append(chain.n)

            @block.tensor
            def _(pe):
                T = nc.tensor
                pe.wait_ge(consts_in, 160)
                pe_front(pe, 0, after_seg, upto_seg)
                last = pe_inside(pe, 0)
                pe.wait_ge(c_ready, 1)
                pe.wait_ge(start_in, 16)
                for g in range(2):
                    for b in range(SEQS):
                        last = T.matmul(ps_a[:, 2 + g, :], c_apart[:, g, b, :], start[:, b, g * HPG:(g + 1) * HPG, :].rearrange("p h d -> p (h d)"),
                                        start=b == 0, stop=b == SEQS - 1)
                last.then_inc(y_made, 1)
                pe.wait_ge(sums_ready, 2)
                pe.wait_ge(w_ready, 2)
                for b in range(SEGS):
                    last = T.matmul(ps_c[:, b * HEADS:(b + 1) * HEADS], in_seg[:, b, :], da[:], start=True, stop=True)
                last.then_inc(seg_sum_made, 1)
                pe.wait_ge(b_ready, 2)
                for b in range(SEGS):
                    pe.wait_ge(x_seg_ready, b + 1)
                    if b:
                        pe.wait_ge(seg_state_ready, b)
                    for g in range(2):
                        last = T.matmul(ps_b[:, g, :], b_tok[:, g, :], x_seg[:, g * HPG:(g + 1) * HPG, :].rearrange("p h d -> p (h d)"), start=True, stop=True)
                    last.then_inc(seg_state_made, 1)

        with ExitStack() as c2:
            conv_tail = c2.enter_context(nc.sbuf_tensor("m2m_conv_tail", [P, XB, TAPS - 1], F32))
            prompt_out, tail_ready, window_free = sem("prompt_out"), sem("tail_ready"), sem("window_free")
            block = c2.enter_context(nc.Block())

            @block.sync
            def _(sp):
                sp.sem_inc(window_free, 1)
                with sp.Fori(0, MAIN_TILES) as i:
                    sp.wait_ge(window_free, i + 1)
                    sp.dma_start(window[:], D["xbc"][:, :, bass.ds(i * P + N_META - TAPS + 1, P + TAPS - 1)]).then_inc(tile_in, 16)
                    sp.dma_start(dt_raw[:], D["dt"][bass.ds(i * P, P), :]).then_inc(tile_in, 16)
                    sp.wait_ge(y_ready, i + 3)
                    sp.dma_start(D["ym"][bass.ds(i * P, P), :], y[:].rearrange("p h d -> p (h d)")).then_inc(y_out, 16)
                sp.wait_ge(state_ready, MAIN_TILES + 2)
                sp.dma_start(D["ssm_end_prompt"], state[:]).then_inc(prompt_out, 16)
                sp.wait_ge(tail_ready, 1)
                sp.dma_start(D["conv_end_prompt"], conv_tail[:]).then_inc(prompt_out, 16)
                sp.wait_ge(prompt_out, 32)
                sp.wait_ge(y_out, 16 * (MAIN_TILES + 2))

            @block.gpsimd
            def _(pool):
                with pool.Fori(1, TILES) as k:
                    pool_tile(pool, k, upto[:])

            @block.scalar
            def _(act):
                with act.Fori(1, TILES) as k:
                    act.wait_ge(conv_done, k + 1)
                    act.wait_ge(y_made, k)
                    nc.scalar.activation(xbc[:], conv[:], ACT.Silu).then_inc(xbc_ready, 1)
                    act.wait_ge(abs_ready, k + 1)
                    nc.scalar.activation(small[:, 2, :], small[:, 1, :], ACT.Exp, scale=-1.0).then_inc(act_step, 1)
                    act.wait_ge(act_step, k + 1)
                    nc.scalar.activation(small[:, 3, :], small[:, 2, :], ACT.Ln, bias=ones[:, 0:1]).then_inc(soft_ready, 1)
                    act.wait_ge(turned, k + 1)
                    nc.scalar.activation(b_tok[:], ps_b[:, 2, 0:2 * NS].rearrange("p (g n) -> p g n", g=2), ACT.Copy).then_inc(b_ready, 1)
                    act.wait_ge(sums_made, k + 1)
                    nc.scalar.activation(e_acs[:], ps_c[:, 0:HEADS], ACT.Exp)
                    nc.scalar.activation(e_rev[:], ps_c[:, HEADS:2 * HEADS], ACT.Exp)
                    nc.scalar.activation(e_tot[:], ps_c[:, 2 * HEADS:3 * HEADS], ACT.Exp).then_inc(sums_ready, 1)
                    act.wait_ge(seg_made, k + 2)
                    nc.scalar.activation(decay[:], ps_a[:].rearrange("p b (h l) -> p (b h) l", l=P), ACT.Exp).then_inc(decay_ready, 1)

            @block.vector
            def _(dve):
                V = nc.vector
                chain = Chain(dve, dve_step)
                STEPS_PER = 19
                begin = rest_steps[0]
                tail_cols = slice(P, P + TAPS - 1)
                with dve.Fori(1, TILES) as k:
                    chain.start(begin + (k - 1) * STEPS_PER)
                    dve_front(dve, chain, k, [(lambda j: window[:, :, j:j + P], lambda t: t[:])])
                    chain.link(V.tensor_copy(conv_tail[:], window[:, :, tail_cols]))
                    dve.sem_inc(window_free, 1)
                    dve_middle(dve, chain, k, upto[:])
                    dve.wait_ge(y_made, k + 1)
                    chain.link(tt(V, state[:], state[:], heads(e_tot[:]), ALU.mult))
                    dve.wait_ge(st_made, k)
                    tt(V, state[:], state[:], ps_b[:, 0:2, :].rearrange("p b (h d) -> p (b h) d", d=HD), ALU.add).then_inc(state_ready, 1)
                    dve_y(dve, chain, k)
                    assert chain.n == STEPS_PER, chain.n
                dve.wait_ge(state_ready, TILES + 1)
                dve.sem_inc(tail_ready, 1)

            @block.tensor
            def _(pe):
                T = nc.tensor
                with pe.Fori(1, TILES) as k:
                    pe_front(pe, k, after, upto)
                    last = pe_inside(pe, k)
                    for g in range(2):
                        last = T.matmul(ps_a[:, 2 + g, :], xbc[:, 10 + g, :], state[:, g * HPG:(g + 1) * HPG, :].rearrange("p h d -> p (h d)"),
                                        start=True, stop=True)
                    last.then_inc(y_made, 1)
                    pe.wait_ge(xw_ready, k + 1)
                    pe.wait_ge(b_ready, k + 2)
                    for g in range(2):
                        last = T.matmul(ps_b[:, g, :], b_tok[:, g, :], x_w[:, g * HPG:(g + 1) * HPG, :].rearrange("p h d -> p (h d)"),
                                        start=True, stop=True)
                    last.then_inc(st_made, 1)


def mix_out(nc, D):
    with ExitStack() as ctx:
        sb = lambda n, s, d=F32: ctx.enter_context(nc.sbuf_tensor("mo_" + n, s, d))
        sem = ctx.enter_context(stage_semaphores(nc, "mo_"))
        ident = sb("ident", [P, P])
        w_glu = sb("w_glu", [P, KT, D_MODEL])
        w_out = sb("w_out", [P, 2 * KT, D_MODEL])
        norm_w = sb("norm_w", [P, 2 * KT])
        eps = sb("eps", [P, 1])
        y5 = sb("y5", [P, D_MODEL])
        z = sb("z", [P, D_MODEL])
        ym = sb("ym", [P, D_MODEL])
        x = sb("x", [P, D_MODEL])
        g = sb("g", [P, D_MODEL])
        g_t = sb("g_t", [P, KT, P])
        sig = sb("sig", [P, D_MODEL])
        z_silu = sb("z_silu", [P, D_MODEL])
        square = sb("square", [P, D_MODEL])
        s5_n = sb("s5_n", [P, D_MODEL])
        m2_n = sb("m2_n", [P, D_MODEL])
        both_t = sb("both_t", [P, 2 * KT, P])
        x_mid = sb("x_mid", [P, D_MODEL])
        stat = sb("stat", [P, 3, 3])
        ps = lambda n: ctx.enter_context(nc.psum_tensor("mo_" + n, [P, KT, P], F32))
        ps_s5, ps_m2, ps_glu, ps_out = ps("ps_s5"), ps("ps_m2"), ps("ps_glu"), ps("ps_out")
        glu_in, out_in, consts_in, y_in, x_in, eps_set = (sem(n) for n in ("glu_in", "out_in", "consts_in", "y_in", "x_in", "eps_set"))
        g_ready, z_ready, m2_gated, m2_summed, m2_root = (sem(n) for n in ("g_ready", "z_ready", "m2_gated", "m2_summed", "m2_root"))
        sig_ready, s5_gated, s5_summed, s5_root = (sem(n) for n in ("sig_ready", "s5_gated", "s5_summed", "s5_root"))
        g_turned, g_t_ready, m2_n_ready, m2_turned, m2_t_ready = (sem(n) for n in ("g_turned", "g_t_ready", "m2_n_ready", "m2_turned", "m2_t_ready"))
        glu_made, s5_n_ready, s5_turned, s5_t_ready = (sem(n) for n in ("glu_made", "s5_n_ready", "s5_turned", "s5_t_ready"))
        out_made, x_mid_ready, x_mid_out, dve_step = (sem(n) for n in ("out_made", "x_mid_ready", "x_mid_out", "dve_step"))
        flat = lambda t: t[:].rearrange("p b c -> p (b c)")
        block = ctx.enter_context(nc.Block())

        @block.sync
        def _(sp):
            def load_y(k):
                for t, n in ((y5, "y5"), (z, "z"), (ym, "ym")):
                    sp.dma_start(t[:], D[n][bass.ds(k * P, P), :]).then_inc(y_in, 16)

            def store(k):
                sp.wait_ge(x_mid_ready, k + 2)
                sp.dma_start(D["x_mid"][bass.ds(k * P, P), :], x_mid[:]).then_inc(x_mid_out, 16)

            load_y(0)
            sp.dma_start(x[:], D["x_all"][0:P, :]).then_inc(x_in, 16)
            sp.dma_start(ident[:], D["ident"]).then_inc(consts_in, 16)
            sp.dma_start(norm_w[:], D["mix_norm_w"]).then_inc(consts_in, 16)
            sp.dma_start(w_glu[:], D["w_glu"]).then_inc(glu_in, 16)
            sp.dma_start(w_out[:], D["w_out"]).then_inc(out_in, 16)
            with sp.Fori(0, MAIN_TILES) as k:
                sp.wait_ge(m2_gated, k + 1)
                sp.wait_ge(g_ready, k + 1)
                load_y(k + 1)
                store(k)
                sp.dma_start(x[:], D["x_all"][bass.ds(k * P + P, P), :]).then_inc(x_in, 16)
            store(MAIN_TILES)
            sp.wait_ge(x_mid_out, 16 * (TILES + 1))

        @block.scalar
        def _(act):
            A = nc.scalar.activation
            act.sem_inc(sig_ready, 1)
            act.wait_ge(eps_set, 1)
            with act.Fori(0, TILES) as k:
                act.wait_ge(y_in, 48 * k + 48)
                act.wait_ge(s5_gated, k + 1)
                A(g[:], y5[:], ACT.Gelu_apprx_tanh).then_inc(g_ready, 1)
                A(z_silu[:], z[:], ACT.Silu).then_inc(z_ready, 1)
                act.wait_ge(m2_gated, k + 1)
                for h in range(2):
                    half = slice(h * 512, h * 512 + 512)
                    last = A(square[:, half], m2_n[:, half], ACT.Square, accum_out=stat[:, 0, 1 + h:2 + h])
                last.then_inc(m2_summed, 1)
                act.wait_ge(m2_summed, k + 1)
                A(stat[:, 1, 1:3], stat[:, 0, 1:3], ACT.Sqrt, bias=eps[:], scale=2.0 / D_MODEL).then_inc(m2_root, 1)
                act.wait_ge(glu_made, k + 1)
                A(sig[:], flat(ps_glu), ACT.Sigmoid).then_inc(sig_ready, 1)
                act.wait_ge(s5_gated, k + 2)
                A(square[:], s5_n[:], ACT.Square, accum_out=stat[:, 0, 0:1]).then_inc(s5_summed, 1)
                act.wait_ge(s5_summed, k + 1)
                A(stat[:, 1, 0:1], stat[:, 0, 0:1], ACT.Sqrt, bias=eps[:], scale=1.0 / D_MODEL).then_inc(s5_root, 1)

        @block.vector
        def _(dve):
            V = nc.vector
            chain = Chain(dve, dve_step)
            STEPS_PER = 2
            dve.sem_inc(s5_gated, 1)
            dve.sem_inc(x_mid_out, 16)
            dve.sem_inc(x_mid_ready, 1)
            dve.sem_inc(s5_t_ready, 1)
            V.memset(eps[:], EPS).then_inc(eps_set, 1)
            dve.wait_ge(consts_in, 32)
            weigh = lambda o, src, w: V.tensor_tensor(out=o, in0=src[:], in1=w.unsqueeze(2).to_broadcast([P, KT, P]), op=ALU.mult)
            with dve.Fori(0, TILES) as k:
                chain.start(STEPS_PER * k)
                dve.wait_ge(z_ready, k + 1)
                V.tensor_tensor(out=m2_n[:], in0=ym[:], in1=z_silu[:], op=ALU.mult).then_inc(m2_gated, 1)
                dve.wait_ge(g_turned, k + 1)
                V.tensor_copy(g_t[:], ps_s5[:]).then_inc(g_t_ready, 1)
                dve.wait_ge(m2_root, k + 1)
                chain.link(V.reciprocal(stat[:, 2, 1:3], stat[:, 1, 1:3]))
                for h in range(2):
                    half = slice(h * 512, h * 512 + 512)
                    last = V.tensor_scalar(m2_n[:, half], m2_n[:, half], stat[:, 2, 1 + h:2 + h], None, ALU.mult)
                last.then_inc(m2_n_ready, 1)
                dve.wait_ge(m2_turned, k + 1)
                weigh(both_t[:, KT:, :], ps_m2, norm_w[:, KT:]).then_inc(m2_t_ready, 1)
                dve.wait_ge(sig_ready, k + 2)
                V.tensor_tensor(out=s5_n[:], in0=g[:], in1=sig[:], op=ALU.mult).then_inc(s5_gated, 1)
                dve.wait_ge(s5_root, k + 1)
                chain.link(V.reciprocal(stat[:, 2, 0:1], stat[:, 1, 0:1]))
                V.tensor_scalar(s5_n[:], s5_n[:], stat[:, 2, 0:1], None, ALU.mult).then_inc(s5_n_ready, 1)
                dve.wait_ge(s5_turned, k + 1)
                weigh(both_t[:, 0:KT, :], ps_s5, norm_w[:, 0:KT]).then_inc(s5_t_ready, 1)
                dve.wait_ge(out_made, k + 1)
                dve.wait_ge(x_in, 16 * k + 16)
                dve.wait_ge(x_mid_out, 16 * k + 16)
                V.tensor_tensor(out=x_mid[:], in0=x[:], in1=flat(ps_out), op=ALU.add).then_inc(x_mid_ready, 1)

        @block.tensor
        def _(pe):
            T = nc.tensor

            def turn(dst, src):
                for c in range(KT):
                    last = T.transpose(dst[:, c, :], src[:, c * P:(c + 1) * P], ident[:])
                return last

            def project(dst, src_t, w, c0, n, first, final):
                for half in range(2):
                    for c in range(c0, c0 + n):
                        last = T.matmul(flat(dst)[:, half * 512:half * 512 + 512], src_t[:, c, :], w[:, c, half * 512:half * 512 + 512],
                                        start=first and c == c0, stop=final and c == c0 + n - 1)
                return last

            pe.wait_ge(consts_in, 32)
            pe.wait_ge(glu_in, 16)
            pe.wait_ge(out_in, 16)
            with pe.Fori(0, TILES) as k:
                pe.wait_ge(g_ready, k + 1)
                pe.wait_ge(s5_t_ready, k + 1)
                turn(ps_s5, g).then_inc(g_turned, 1)
                pe.wait_ge(g_t_ready, k + 1)
                pe.wait_ge(sig_ready, k + 1)
                project(ps_glu, g_t, w_glu, 0, KT, True, True).then_inc(glu_made, 1)
                pe.wait_ge(m2_n_ready, k + 1)
                turn(ps_m2, m2_n).then_inc(m2_turned, 1)
                pe.wait_ge(m2_t_ready, k + 1)
                pe.wait_ge(x_mid_ready, k + 1)
                project(ps_out, both_t, w_out, KT, KT, True, False)
                pe.wait_ge(s5_n_ready, k + 1)
                turn(ps_s5, s5_n).then_inc(s5_turned, 1)
                pe.wait_ge(s5_t_ready, k + 2)
                project(ps_out, both_t, w_out, 0, KT, False, True).then_inc(out_made, 1)


def route(nc, D):
    PAIR = 2 * PH
    LEAST = -3.0e38
    with ExitStack() as ctx:
        sb = lambda n, s, d=F32: ctx.enter_context(nc.sbuf_tensor("rt_" + n, s, d))
        sem = ctx.enter_context(stage_semaphores(nc, "rt_"))
        ident = sb("ident", [P, P])
        w_q = sb("w_q", [P, KT, PAIR * P])
        keys_t = sb("keys_t", [P, PAIR, NK])
        ffn_w = sb("ffn_w", [P, D_MODEL])
        count16 = sb("count16", [P, TOPK])
        eps = sb("eps", [P, 1])
        x = sb("x", [P, D_MODEL])
        square = sb("square", [P, D_MODEL])
        stat = sb("stat", [P, 3])
        h = sb("h", [P, D_MODEL])
        h_t = sb("h_t", [P, KT, P])
        q_t = sb("q_t", [P, PAIR, P])
        score = sb("score", [P, PAIR, NK])
        rest = sb("rest", [P, PAIR, NK])
        best = sb("best", [P, PH, 2, TOPK])
        best_i = sb("best_i", [P, PH, 2, TOPK], U32)
        best_f = sb("best_f", [P, PH, 2, TOPK])
        cand = sb("cand", [P, PH, TOPK, TOPK])
        cand2 = sb("cand2", [P, PH, TOPK * TOPK])
        top = sb("top", [P, PH, TOPK])
        pos = sb("pos", [P, PH, TOPK], U32)
        pos_ab = sb("pos_ab", [P, 2, SLOTS], U32)
        pos_f = sb("pos_f", [P, 2, SLOTS])
        hit = sb("hit", [P, SLOTS, TOPK])
        picked = sb("picked", [P, 2, SLOTS])
        index = sb("index", [P, SLOTS], I32)
        e = sb("e", [P, PH, TOPK])
        total = sb("total", [P, 2, PH])
        gate = sb("gate", [P, PH, TOPK])
        ps_t = ctx.enter_context(nc.psum_tensor("rt_ps_t", [P, KT, P], F32))
        ps_q = ctx.enter_context(nc.psum_tensor("rt_ps_q", [P, 2, 4, P], F32))
        ps_s = ctx.enter_context(nc.psum_tensor("rt_ps_s", [P, 2, 4, P], F32))
        consts_in, x_in, w_q_in, eps_set, summed, root, h_ready, h_out = (sem(n) for n in (
            "consts_in", "x_in", "w_q_in", "eps_set", "summed", "root", "h_ready", "h_out"))
        h_turned, h_t_ready, q_made, q_ready, s_made, s_ready, topped = (sem(n) for n in (
            "h_turned", "h_t_ready", "q_made", "q_ready", "s_made", "s_ready", "topped"))
        shifted, e_ready, choice_ready, choice_out, dve_step, settled = (sem(n) for n in (
            "shifted", "e_ready", "choice_ready", "choice_out", "dve_step", "settled"))
        UNITS = PAIR // 4
        block = ctx.enter_context(nc.Block())

        @block.sync
        def _(sp):
            sp.dma_start(x[:], D["x_mid"][0:P, :]).then_inc(x_in, 16)
            for t, n in ((ident, "ident"), (ffn_w, "norm_ffn_w"), (count16, "count16"), (keys_t, "keys_t")):
                sp.dma_start(t[:], D[n]).then_inc(consts_in, 16)
            sp.dma_start(w_q[:], D["w_q"]).then_inc(w_q_in, 16)

            def store(k):
                sp.wait_ge(h_ready, k + 2)
                sp.dma_start(D["h"][bass.ds(k * P, P), :], h[:]).then_inc(h_out, 16)
                sp.wait_ge(choice_ready, k + 1)
                settle(sp, settled)
                sp.dma_start(D["index"][:, bass.ds(k, 1), :], index[:].unsqueeze(1)).then_inc(choice_out, 16)
                sp.dma_start(D["gate"][:, bass.ds(k, 1), :], gate[:].rearrange("p h c -> p (h c)").unsqueeze(1)).then_inc(choice_out, 16)

            with sp.Fori(0, MAIN_TILES) as k:
                sp.wait_ge(h_ready, k + 2)
                sp.dma_start(x[:], D["x_mid"][bass.ds(k * P + P, P), :]).then_inc(x_in, 16)
                store(k)
            store(MAIN_TILES)
            sp.wait_ge(h_out, 16 * (TILES + 1))
            sp.wait_ge(choice_out, 32 * (TILES + 1))

        @block.scalar
        def _(act):
            A = nc.scalar.activation
            act.sem_inc(q_ready, 2)
            act.sem_inc(s_ready, 2)
            act.wait_ge(eps_set, 1)
            with act.Fori(0, TILES) as k:
                act.wait_ge(x_in, 16 * k + 16)
                act.wait_ge(h_ready, k + 1)
                A(square[:], x[:], ACT.Square, accum_out=stat[:, 0:1]).then_inc(summed, 1)
                act.wait_ge(summed, k + 1)
                A(stat[:, 1:2], stat[:, 0:1], ACT.Sqrt, bias=eps[:], scale=1.0 / D_MODEL).then_inc(root, 1)
                for n in range(UNITS + 1):
                    if n < UNITS:
                        act.wait_ge(q_made, UNITS * k + n + 1)
                        A(q_t[:, 4 * n:4 * n + 4, :], ps_q[:, n % 2], ACT.Copy).then_inc(q_ready, 1)
                    if n:
                        act.wait_ge(s_made, UNITS * k + n)
                        if n == 1:
                            act.wait_ge(topped, k + 1)
                        A(score[:, 4 * n - 4:4 * n, :], ps_s[:, (n - 1) % 2], ACT.Copy).then_inc(s_ready, 1)
                act.wait_ge(shifted, k + 1)
                A(e[:], e[:], ACT.Exp).then_inc(e_ready, 1)

        @block.vector
        def _(dve):
            V = nc.vector
            chain = Chain(dve, dve_step)
            STEPS_PER = 25
            tt = lambda o, a, b, op: V.tensor_tensor(out=o, in0=a, in1=b, op=op)
            dve.sem_inc(h_ready, 1)
            dve.sem_inc(h_out, 16)
            dve.sem_inc(topped, 1)
            dve.sem_inc(choice_out, 32)
            V.memset(eps[:], EPS).then_inc(eps_set, 1)
            dve.wait_ge(consts_in, 64)
            pairs = [(a, b) for a in range(PH) for b in range(2)]

            with dve.Fori(0, TILES) as k:
                chain.start(STEPS_PER * k)
                dve.wait_ge(root, k + 1)
                chain.link(V.reciprocal(stat[:, 2:3], stat[:, 1:2]))
                dve.wait_ge(h_out, 16 * k + 16)
                chain.link(V.tensor_scalar(h[:], x[:], stat[:, 2:3], None, ALU.mult))
                tt(h[:], h[:], ffn_w[:], ALU.mult).then_inc(h_ready, 1)
                dve.wait_ge(h_turned, k + 1)
                V.tensor_copy(h_t[:], ps_t[:]).then_inc(h_t_ready, 1)

                dve.wait_ge(s_ready, UNITS * k + UNITS + 2)
                settle(dve, settled)
                for j, (a, b) in enumerate(pairs):
                    last = V.max(out=best[:, a, b, 0:8], in_=score[:, j, :])
                chain.link(last)
                settle(dve, settled)
                for j, (a, b) in enumerate(pairs):
                    V.max_index(out=best_i[:, a, b, 0:8], in_max=best[:, a, b, 0:8], in_values=score[:, j, :])
                    last = V.match_replace(out=rest[:, j, :], in_to_replace=best[:, a, b, 0:8], in_values=score[:, j, :], imm_value=LEAST)
                chain.link(last)
                dve.sem_inc(topped, 1)
                for j, (a, b) in enumerate(pairs):
                    last = V.max(out=best[:, a, b, 8:16], in_=rest[:, j, :])
                chain.link(last)
                settle(dve, settled)
                for j, (a, b) in enumerate(pairs):
                    last = V.max_index(out=best_i[:, a, b, 8:16], in_max=best[:, a, b, 8:16], in_values=rest[:, j, :])
                chain.link(last)
                chain.link(V.tensor_copy(best_f[:], best_i[:]))
                chain.link(tt(cand[:], best[:, :, 0, :].unsqueeze(3).to_broadcast([P, PH, TOPK, TOPK]),
                              best[:, :, 1, :].unsqueeze(2).to_broadcast([P, PH, TOPK, TOPK]), ALU.add))
                sums = cand[:].rearrange("p h a b -> p h (a b)")
                settle(dve, settled)
                for a in range(PH):
                    last = V.max(out=top[:, a, 0:8], in_=sums[:, a, :])
                chain.link(last)
                settle(dve, settled)
                for a in range(PH):
                    V.max_index(out=pos[:, a, 0:8], in_max=top[:, a, 0:8], in_values=sums[:, a, :])
                    last = V.match_replace(out=cand2[:, a, :], in_to_replace=top[:, a, 0:8], in_values=sums[:, a, :], imm_value=LEAST)
                chain.link(last)
                settle(dve, settled)
                for a in range(PH):
                    last = V.max(out=top[:, a, 8:16], in_=cand2[:, a, :])
                chain.link(last)
                settle(dve, settled)
                for a in range(PH):
                    last = V.max_index(out=pos[:, a, 8:16], in_max=top[:, a, 8:16], in_values=cand2[:, a, :])
                chain.link(last)
                dve.wait_ge(choice_out, 32 * k + 32)
                tt(e[:], top[:], top[:, :, 0:1].to_broadcast([P, PH, TOPK]), ALU.subtract).then_inc(shifted, 1)
                flat_pos = pos[:].rearrange("p h c -> p (h c)")
                chain.link(V.tensor_scalar(pos_ab[:, 0, :], flat_pos, 4, None, ALU.logical_shift_right))
                chain.link(V.tensor_scalar(pos_ab[:, 1, :], flat_pos, TOPK - 1, None, ALU.bitwise_and))
                chain.link(V.tensor_copy(pos_f[:], pos_ab[:]))
                for b in range(2):
                    chain.link(tt(hit[:], pos_f[:, b, :].unsqueeze(2).to_broadcast([P, SLOTS, TOPK]),
                                  count16[:].unsqueeze(1).to_broadcast([P, SLOTS, TOPK]), ALU.is_equal))
                    by_head = hit[:].rearrange("p (h c) j -> p h c j", h=PH)
                    chain.link(tt(by_head, by_head, best_f[:, :, b, :].unsqueeze(2).to_broadcast([P, PH, TOPK, TOPK]), ALU.mult))
                    chain.link(V.tensor_reduce(out=picked[:, b, :], in_=hit[:], axis=AX.X, op=ALU.add))
                chain.link(V.scalar_tensor_tensor(out=pos_f[:, 0, :], in0=picked[:, 0, :], scalar=float(NK), in1=picked[:, 1, :],
                                                  op0=ALU.mult, op1=ALU.add))
                chain.link(V.tensor_copy(index[:], pos_f[:, 0, :]))
                dve.wait_ge(e_ready, k + 1)
                chain.link(V.tensor_reduce(out=total[:, 0, :], in_=e[:], axis=AX.X, op=ALU.add))
                chain.link(V.reciprocal(total[:, 1, :], total[:, 0, :]))
                tt(gate[:], e[:], total[:, 1, :].unsqueeze(2).to_broadcast([P, PH, TOPK]), ALU.mult).then_inc(choice_ready, 1)
                assert chain.n == STEPS_PER, chain.n

        @block.tensor
        def _(pe):
            T = nc.tensor
            pe.wait_ge(consts_in, 64)
            pe.wait_ge(w_q_in, 16)
            with pe.Fori(0, TILES) as k:
                pe.wait_ge(h_ready, k + 2)
                for c in range(KT):
                    last = T.transpose(ps_t[:, c, :], h[:, c * P:(c + 1) * P], ident[:])
                last.then_inc(h_turned, 1)
                pe.wait_ge(h_t_ready, k + 1)
                for n in range(UNITS + 1):
                    if n < UNITS:
                        pe.wait_ge(q_ready, UNITS * k + n + 1)
                        for j in range(4):
                            for c in range(KT):
                                last = T.matmul(ps_q[:, n % 2, j, :], w_q[:, c, (4 * n + j) * P:(4 * n + j + 1) * P], h_t[:, c, :],
                                                start=c == 0, stop=c == KT - 1)
                        last.then_inc(q_made, 1)
                    if n:
                        pe.wait_ge(q_ready, UNITS * k + n + 2)
                        pe.wait_ge(s_ready, UNITS * k + n)
                        for j in range(4):
                            m = 4 * (n - 1) + j
                            last = T.matmul(ps_s[:, (n - 1) % 2, j, :], q_t[:, m, :], keys_t[:, m, :], start=True, stop=True)
                        last.then_inc(s_made, 1)


def experts(nc, D):
    RING, GROUP = 16, 4
    GROUPS = RING // GROUP
    ROUNDS = SLOTS // RING
    with ExitStack() as ctx:
        sb = lambda n, s, d=F32: ctx.enter_context(nc.sbuf_tensor("ex_" + n, s, d))
        sem = ctx.enter_context(stage_semaphores(nc, "ex_"))
        ident = sb("ident", [P, P])
        half_ident = sb("half_ident", [P, 2, P])
        final_w = sb("final_w", [P, D_MODEL])
        eps = sb("eps", [P, 1])
        index = sb("index", [P, TILES, SLOTS], I32)
        gate = sb("gate", [P, TILES, SLOTS])
        ring = sb("ring", [P, RING, 2 * D_MODEL])
        round_i = sb("round_i", [P, RING], I32)
        h_next = sb("h_next", [P, D_MODEL])
        h = sb("h", [P, D_MODEL])
        x = sb("x", [P, D_MODEL])
        dot = sb("dot", [P, RING])
        act_v = sb("act_v", [P, RING])
        diag = sb("diag", [P, RING, P])
        out = sb("out", [P, D_MODEL])
        square = sb("square", [P, D_MODEL])
        stat = sb("stat", [P, 3])
        acc = ctx.enter_context(nc.psum_tensor("ex_acc", [P, 2, 512], F32))
        consts_in, h_in, x_in, eps_set = (sem(n) for n in ("consts_in", "h_in", "x_in", "eps_set"))
        h_taken, indices_ready = sem("h_taken"), sem("indices_ready")
        row_in = [sem(f"row_in{s}") for s in range(RING)]
        dots_ready = [sem(f"dots_ready{g}") for g in range(GROUPS)]
        act_ready = [sem(f"act_ready{g}") for g in range(GROUPS)]
        diag_ready = [sem(f"diag_ready{g}") for g in range(GROUPS)]
        group_done = [sem(f"group_done{g}") for g in range(GROUPS)]
        tile_done, copied, summed, root, y_ready, y_out, dve_step = (sem(n) for n in (
            "tile_done", "copied", "summed", "root", "y_ready", "y_out", "dve_step"))
        settled = sem("settled")
        block = ctx.enter_context(nc.Block())

        @block.sync
        def _(sp):
            sp.dma_start(index[:], D["index"]).then_inc(consts_in, 16)
            for t, n in ((gate, "gate"), (ident, "ident"), (half_ident, "half_ident"), (final_w, "final_norm_w")):
                sp.dma_start(t[:], D[n]).then_inc(consts_in, 16)
            sp.dma_start(h_next[:], D["h"][0:P, :]).then_inc(h_in, 16)
            sp.dma_start(x[:], D["x_mid"][0:P, :]).then_inc(x_in, 16)
            with sp.Fori(0, MAIN_TILES) as k:
                sp.wait_ge(h_taken, k + 1)
                sp.dma_start(h_next[:], D["h"][bass.ds(k * P + P, P), :]).then_inc(h_in, 16)
                sp.wait_ge(tile_done, k + 1)
                sp.dma_start(x[:], D["x_mid"][bass.ds(k * P + P, P), :]).then_inc(x_in, 16)
                sp.wait_ge(y_ready, k + 1)
                sp.dma_start(D["y"][bass.ds(k * P, P), :], out[:]).then_inc(y_out, 16)
            sp.wait_ge(y_ready, TILES)
            sp.dma_start(D["y"][SEQ:SEQ + SAMPLE, :], out[0:SAMPLE, :]).then_inc(y_out, 16)
            sp.wait_ge(y_out, 16 * (TILES + 1))

        @block.gpsimd
        def _(pool):
            pool.wait_ge(consts_in, 80)
            for g in range(GROUPS):
                pool.sem_inc(group_done[g], 1)

            def gather(k, rows):
                with pool.Fori(0, ROUNDS) as r:
                    n = k * ROUNDS + r
                    for g in range(GROUPS):
                        pool.wait_ge(group_done[g], n + 1)
                        part = round_i[:, g * GROUP:(g + 1) * GROUP]
                        nc.gpsimd.tensor_copy(part.unsqueeze(1), index[:, bass.ds(k, 1), bass.ds(r * RING + g * GROUP, GROUP)]).then_inc(indices_ready, 1)
                        pool.wait_ge(indices_ready, GROUPS * n + g + 1)
                        settle(pool, settled)
                        for s in range(g * GROUP, (g + 1) * GROUP):
                            nc.gpsimd.indirect_dma_start(
                                out=ring[0:rows, s, :], out_offset=None, in_=D["uv"],
                                in_offset=bass.IndirectOffsetOnAxis(ap=round_i[0:rows, s:s + 1], axis=0)).then_inc(row_in[s], 16)

            with pool.Fori(0, MAIN_TILES) as k:
                gather(k, P)
            gather(MAIN_TILES, SAMPLE)

        @block.vector
        def _(dve):
            V = nc.vector
            chain = Chain(dve, dve_step)
            STEPS_PER = 3
            V.memset(eps[:], EPS).then_inc(eps_set, 1)
            dve.sem_inc(y_out, 16)
            dve.sem_inc(copied, 1)
            dve.wait_ge(consts_in, 80)

            def tile(k, rows):
                chain.start(STEPS_PER * k)
                dve.wait_ge(h_in, 16 * k + 16)
                chain.link(V.tensor_copy(h[:], h_next[:]))
                dve.sem_inc(h_taken, 1)
                with dve.Fori(0, ROUNDS) as r:
                    n = k * ROUNDS + r
                    for g in range(GROUPS):
                        for s in range(g * GROUP, (g + 1) * GROUP):
                            dve.wait_ge(row_in[s], 16 * n + 16)
                            last = V.tensor_tensor_reduce(out=ring[0:rows, s, 0:D_MODEL], in0=ring[0:rows, s, 0:D_MODEL], in1=h[0:rows, :],
                                                          scale=1.0, scalar=0.0, op0=ALU.mult, op1=ALU.add, accum_out=dot[0:rows, s:s + 1])
                        last.then_inc(dots_ready[g], 1)
                        dve.wait_ge(act_ready[g], n + 1)
                        for s in range(g * GROUP, (g + 1) * GROUP):
                            last = V.tensor_scalar(diag[0:rows, s, :], ident[0:rows, :], act_v[0:rows, s:s + 1],
                                                   gate[0:rows, bass.ds(k, 1), bass.ds(r * RING + s, 1)].rearrange("p a b -> p (a b)"), ALU.mult, ALU.mult)
                        last.then_inc(diag_ready[g], 1)
                dve.wait_ge(tile_done, k + 1)
                dve.wait_ge(y_out, 16 * k + 16)
                V.tensor_copy(out[:], acc[:].rearrange("p b c -> p (b c)")).then_inc(copied, 1)
                dve.wait_ge(root, k + 1)
                chain.link(V.reciprocal(stat[:, 2:3], stat[:, 1:2]))
                chain.link(V.tensor_scalar(out[:], out[:], stat[:, 2:3], None, ALU.mult))
                V.tensor_tensor(out=out[:], in0=out[:], in1=final_w[:], op=ALU.mult).then_inc(y_ready, 1)

            with dve.Fori(0, MAIN_TILES) as k:
                tile(k, P)
            tile(MAIN_TILES, SAMPLE)

        @block.scalar
        def _(act):
            A = nc.scalar.activation
            act.wait_ge(eps_set, 1)

            def tile(k, rows):
                with act.Fori(0, ROUNDS) as r:
                    for g in range(GROUPS):
                        cols = slice(g * GROUP, (g + 1) * GROUP)
                        act.wait_ge(dots_ready[g], k * ROUNDS + r + 1)
                        A(act_v[0:rows, cols], dot[0:rows, cols], ACT.Gelu_apprx_tanh).then_inc(act_ready[g], 1)
                act.wait_ge(copied, k + 2)
                A(square[:], out[:], ACT.Square, accum_out=stat[:, 0:1]).then_inc(summed, 1)
                act.wait_ge(summed, k + 1)
                A(stat[:, 1:2], stat[:, 0:1], ACT.Sqrt, bias=eps[:], scale=1.0 / D_MODEL).then_inc(root, 1)

            with act.Fori(0, MAIN_TILES) as k:
                tile(k, P)
            tile(MAIN_TILES, SAMPLE)

        @block.tensor
        def _(pe):
            T = nc.tensor
            pe.wait_ge(consts_in, 80)

            def tile(k, rows):
                pe.wait_ge(x_in, 16 * k + 16)
                pe.wait_ge(copied, k + 1)
                def add_x(half):
                    for b in range(2):
                        last = T.matmul(acc[:, b, :], half_ident[:, half, :], x[:, b * 512:b * 512 + 512], start=half == 0, stop=half == 1)
                    return last

                add_x(0)
                with pe.Fori(0, ROUNDS) as r:
                    n = k * ROUNDS + r
                    for g in range(GROUPS):
                        pe.wait_ge(diag_ready[g], n + 1)
                        for s in range(g * GROUP, (g + 1) * GROUP):
                            for b in range(2):
                                last = T.matmul(acc[:, b, :], diag[0:rows, s, :], ring[0:rows, s, D_MODEL + b * 512:D_MODEL + b * 512 + 512],
                                                start=False, stop=False)
                        last.then_inc(group_done[g], 1)
                pe.wait_ge(group_done[GROUPS - 1], k * ROUNDS + ROUNDS + 1)
                add_x(1).then_inc(tile_done, 1)

            with pe.Fori(0, MAIN_TILES) as k:
                tile(k, P)
            tile(MAIN_TILES, SAMPLE)


def lay_out(x):
    r = lambda a: np.ascontiguousarray(a, np.float32)
    pairs = lambda a, *tail: a.reshape(PAIRS, 2, S5_STATE, *tail).transpose(1, 2, 0, *range(3, 3 + len(tail))).reshape(P, PAIRS, *tail)
    d = {}
    d["x_all"] = np.concatenate([x["x_prompt"][0], x["x_sample"].reshape(SAMPLE, D_MODEL), x["meta_tokens"],
                                 np.zeros((P - REST, D_MODEL), np.float32)])
    d["ident"] = np.eye(P, dtype=np.float32)
    d["half_ident"] = np.stack([np.diag(np.arange(P) < P // 2), np.diag(np.arange(P) >= P // 2)], 1)
    d["norm_mix_w"] = x["norm_mix_w"][0].reshape(KT, P).T
    w = x["w_in"][0]
    w = np.concatenate([w[:, :2 * D_MODEL], w[:, 2 * D_MODEL + XBC:], w[:, 2 * D_MODEL:2 * D_MODEL + XBC]], 1)
    d["w_in"] = w.reshape(KT, P, IN_PROJ).transpose(1, 0, 2)
    d["s5_par"] = np.stack([pairs(x["s5_lambda_re"][0]), pairs(x["s5_lambda_im"][0]),
                            pairs(np.repeat(x["s5_log_step"][0][:, None], S5_STATE, 1))], 1)
    d["s5_b"] = np.stack([pairs(x["s5_b_re"][0], S5_CH), pairs(x["s5_b_im"][0], S5_CH)], 1)
    d["s5_c"] = np.stack([pairs(x["s5_c_re"][0].transpose(0, 2, 1), S5_CH), pairs(x["s5_c_im"][0].transpose(0, 2, 1), S5_CH)], 1)
    d["s5_d"] = x["s5_d"][0].reshape(S5_GROUPS, S5_CH).T
    j = np.arange(P)
    seg = np.where(j < SAMPLE, j // STEPS, np.where(j < REST, SEQS, SEQS + 1 + j))
    same = seg[:, None] == seg[None, :]
    real = (j < REST)[:, None]
    d["after"], d["upto"], d["ones"] = j[:, None] > j[None, :], j[:, None] <= j[None, :], np.ones((P, P))
    d["after_seg"], d["upto_seg"] = d["after"] & same & real, d["upto"] & same & real
    d["in_seg"] = np.repeat((seg[:, None] == np.arange(SEQS + 1)[None, :])[:, :, None], P, 2)
    chan = lambda a: a.reshape(*a.shape[:-1], XB, P)
    d["conv_w"] = chan(x["m2_conv_w"][0]).transpose(2, 1, 0)
    d["conv_b"] = chan(x["m2_conv_b"][0]).T
    d["conv_past"] = chan(x["state_conv"][0]).transpose(3, 2, 0, 1)
    d["head_par"] = np.broadcast_to(np.stack([x["m2_dt_bias"][0], x["m2_a_log"][0], x["m2_d"][0]]), (P, 3, HEADS))
    d["ssm_h0"] = x["state_ssm"][0].transpose(3, 0, 1, 2)
    rows = lambda w: w.reshape(-1, P, w.shape[1]).transpose(1, 0, 2)
    d["w_glu"], d["w_out"], d["w_q"] = rows(x["s5_w_glu"][0]), rows(x["w_out"][0]), rows(x["peer_w_q"][0])
    d["mix_norm_w"] = np.concatenate([x["s5_norm_w"][0], x["m2_norm_w"][0]]).reshape(2 * KT, P).T
    d["keys_t"] = x["peer_sub_keys"][0].reshape(2 * PH, NK, P).transpose(2, 0, 1)
    d["norm_ffn_w"] = np.broadcast_to(x["norm_ffn_w"][0], (P, D_MODEL))
    d["final_norm_w"] = np.broadcast_to(x["final_norm_w"], (P, D_MODEL))
    d["count16"] = np.broadcast_to(np.arange(TOPK), (P, TOPK))
    d["uv"] = np.concatenate([x["peer_u"][0], x["peer_v"][0]], 1)
    h0 = np.stack([x["state_s5_re"][0], x["state_s5_im"][0]])
    d["s5_h0"] = h0.reshape(2, SEQS, PAIRS, 2, S5_STATE).transpose(3, 4, 2, 0, 1).reshape(P, PAIRS, 2, SEQS)
    return {k: r(v) for k, v in d.items()}


SCRATCH = {"u": (ROWS, D_MODEL), "z": (ROWS, D_MODEL), "dt": (ROWS, HEADS), "xbc": (P, XB, XCOLS), "y5": (ROWS, D_MODEL), "ym": (ROWS, D_MODEL),
           "x_mid": (ROWS, D_MODEL), "h": (ROWS, D_MODEL), "gate": (P, TILES, SLOTS), "index": (P, TILES, SLOTS)}
OUTPUTS = {"y": (SEQ + SAMPLE, D_MODEL), "s5_end_sample": (P, PAIRS, 2, SEQS), "s5_end_prompt": (P, PAIRS, 2),
           "conv_end_sample": (P, XB, SEQS, TAPS - 1), "conv_end_prompt": (P, XB, TAPS - 1),
           "ssm_end_sample": (P, SEQS, HEADS, HD), "ssm_end_prompt": (P, HEADS, HD)}


def write_program(nc, D):
    project_tokens(nc, D)
    s5_scan(nc, D)
    mamba_scan(nc, D)
    mix_out(nc, D)
    route(nc, D)
    experts(nc, D)


def kernel(**inputs):
    import concourse.bacc as bacc
    from concourse.bass_utils import run_bass_kernel_spmd

    x = {name: np.asarray(a) for name, a in inputs.items()}
    nc = bacc.Bacc("TRN2", target_bir_lowering=False, num_devices=1)
    arrays = lay_out(x)
    D = {name: nc.dram_tensor("in_" + name, a.shape, F32, kind="ExternalInput").ap() for name, a in arrays.items()}
    for name, shape in SCRATCH.items():
        D[name] = nc.dram_tensor("scratch_" + name, shape, I32 if name == "index" else F32).ap()
    for name, shape in OUTPUTS.items():
        D[name] = nc.dram_tensor("out_" + name, shape, F32, kind="ExternalOutput").ap()
    write_program(nc, D)
    got = run_bass_kernel_spmd(nc, [{"in_" + n: a for n, a in arrays.items()}], core_ids=[0]).results[0]
    out = {name: np.asarray(got["out_" + name]) for name in OUTPUTS}

    s5 = lambda a, part: a[:, :, part].reshape(2, S5_STATE, PAIRS, -1).transpose(3, 2, 0, 1).reshape(1, -1, S5_GROUPS, S5_STATE)
    ssm = lambda a: a.reshape(NS, -1, HEADS, HD).transpose(1, 2, 3, 0)[None]
    conv = lambda a: a.reshape(P, XB, -1, TAPS - 1).transpose(2, 3, 1, 0).reshape(1, -1, TAPS - 1, XBC)
    r = np.ascontiguousarray
    return (r(out["y"][:SEQ].reshape(1, SEQ, D_MODEL)), r(out["y"][SEQ:].reshape(SEQS, STEPS, D_MODEL)),
            r(s5(out["s5_end_prompt"], 0)), r(s5(out["s5_end_prompt"], 1)), r(ssm(out["ssm_end_prompt"])), r(conv(out["conv_end_prompt"])),
            r(s5(out["s5_end_sample"], 0)), r(s5(out["s5_end_sample"], 1)), r(ssm(out["ssm_end_sample"])), r(conv(out["conv_end_sample"])))
```

```python
import numpy as np
import concourse.bass as bass
from concourse import mybir
from contextlib import ExitStack, contextmanager

F32 = mybir.dt.float32
I32 = mybir.dt.int32
U32 = mybir.dt.uint32
ALU = mybir.AluOpType
ACT = mybir.ActivationFunctionType
AX = mybir.AxisListType

P = 128
D_MODEL = 1024
KT = D_MODEL // P
SEQ = 1024
N_META = 16
SEQS = 8
STEPS = 8
SAMPLE = SEQS * STEPS
MAIN_TILES = SEQ // P
TILES = MAIN_TILES + 1
ROWS = TILES * P
REST = SAMPLE + N_META
EPS = 1e-6

S5_CH = 16
S5_GROUPS = 64
S5_STATE = 64
PAIRS = S5_GROUPS // 2
Q = 8
CH_MAIN = SEQ // Q
CH_META = N_META // Q
CH_REST = SEQS + CH_META
CHUNKS = CH_REST + CH_MAIN
CH_PROMPT = CH_META + CH_MAIN
SCAN = 10
BLOCKS = CH_PROMPT // SCAN
assert BLOCKS * SCAN == CH_PROMPT

HEADS = 16
HPG = 8
HD = 64
NS = 128
XBC = 1536
XB = XBC // P
TAPS = 4
TOKW = 2 * D_MODEL + HEADS
IN_PROJ = TOKW + XBC
XCOLS = N_META + SEQ + SAMPLE

PH = 8
NK = 128
TOPK = 16
SLOTS = PH * TOPK
EXPERTS = NK * NK


class Chain:

    def __init__(self, eng, sem):
        self.eng, self.sem, self.base, self.n = eng, sem, 0, 0

    def link(self, ins):
        self.n += 1
        ins.then_inc(self.sem, 1)
        self.eng.wait_ge(self.sem, self.base + self.n)

    def start(self, base):
        self.base, self.n = base, 0


def settle(eng, sem):
    eng.sem_inc(sem, 1)


def bc(ap, dims):
    return bass.AP(tensor=ap.tensor, offset=ap.offset, ap=[list(ap.ap[0])] + [list(d) for d in dims])


@contextmanager
def stage_semaphores(nc, prefix):
    held = []

    def new(name):
        held.append(nc.alloc_semaphore(prefix + name))
        return held[-1]

    yield new
    nc.clear_and_free_semaphores(held)
    nc.all_engine_barrier()


def project_tokens(nc, D):
    with ExitStack() as ctx:
        sb = lambda n, s, d=F32: ctx.enter_context(nc.sbuf_tensor("pj_" + n, s, d))
        ident = sb("ident", [P, P])
        norm_w = sb("norm_w", [P, KT])
        w_in = sb("w_in", [P, KT, IN_PROJ])
        x = sb("x", [P, D_MODEL])
        square = sb("square", [P, D_MODEL])
        stat = sb("stat", [P, 4])
        normed = sb("normed", [P, D_MODEL])
        normed_t = sb("normed_t", [P, KT, P])
        token_out = sb("token_out", [P, TOKW])
        chan_out = sb("chan_out", [P, XB, P])
        t_psum = ctx.enter_context(nc.psum_tensor("pj_t_psum", [P, KT, P], F32))
        bank = ctx.enter_context(nc.psum_tensor("pj_bank", [P, 4, 512], F32))
        sem = ctx.enter_context(stage_semaphores(nc, "pj_"))
        consts_in, x_in, x_free = sem("consts_in"), sem("x_in"), sem("x_free")
        w_part_in = [sem(f"w_in{j}") for j in range(3)]
        root_ready, square_ready, normed_ready = sem("root_ready"), sem("square_ready"), sem("normed_ready")
        transposed, t_copied = sem("transposed"), sem("t_copied")
        even_done, odd_done = sem("even_done"), sem("odd_done")
        even_free, odd_free = sem("even_free"), sem("odd_free")
        stored, padded, dve_step = sem("stored"), sem("padded"), sem("dve_step")
        ITEMS = 8
        W_CUT = [0, 2 * 512, TOKW, IN_PROJ]
        block = ctx.enter_context(nc.Block())

        @block.sync
        def _(sp):
            sp.dma_start(ident[:], D["ident"]).then_inc(consts_in, 16)
            sp.dma_start(norm_w[:], D["norm_mix_w"]).then_inc(consts_in, 16)
            sp.dma_start(D["y5"][SEQ + REST:ROWS, :], D["x_all"][SEQ + REST:ROWS, :]).then_inc(padded, 16)
            sp.dma_start(x[:], D["x_all"][0:P, :]).then_inc(x_in, 16)
            for j in range(3):
                a, b = W_CUT[j], W_CUT[j + 1]
                sp.dma_start(w_in[:, :, a:b], D["w_in"][:, :, a:b]).then_inc(w_part_in[j], 16)

            def store(i, col, width, dst_cols):
                sp.wait_ge(even_free, i * 4 + 2 + 4)
                sp.wait_ge(odd_free, i * 4 + 2 + 4)
                rows = bass.ds(i * P, P)
                sp.dma_start(D["u"][rows, :], token_out[:, 0:D_MODEL]).then_inc(stored, 16)
                sp.dma_start(D["z"][rows, :], token_out[:, D_MODEL:2 * D_MODEL]).then_inc(stored, 16)
                sp.dma_start(D["dt"][rows, :], token_out[:, 2 * D_MODEL:TOKW]).then_inc(stored, 16)
                sp.dma_start(D["xbc"][:, :, dst_cols], chan_out[:, :, col:col + width]).then_inc(stored, 16)

            with sp.Fori(0, MAIN_TILES) as i:
                sp.wait_ge(x_free, i + 1)
                sp.dma_start(x[:], D["x_all"][bass.ds(i * P + P, P), :]).then_inc(x_in, 16)
                store(i, 0, P, bass.ds(i * P + N_META, P))
            store(MAIN_TILES, 0, SAMPLE, bass.ds(N_META + SEQ, SAMPLE))
            sp.dma_start(D["xbc"][:, :, 0:N_META], chan_out[:, :, SAMPLE:REST]).then_inc(stored, 16)
            sp.wait_ge(stored, 16 * (4 * TILES + 2))
            sp.wait_ge(padded, 16)

        @block.scalar
        def _(act):
            act.sem_inc(even_free, 2)
            act.wait_ge(square_ready, 1)

            def norm(i):
                act.wait_ge(x_in, 16 * (i + 1))
                act.wait_ge(normed_ready, i + 1)
                nc.scalar.activation(square[:], x[:], ACT.Square, accum_out=stat[:, 0:1]).then_inc(square_ready, 1)
                act.wait_ge(square_ready, i + 2)
                nc.scalar.activation(stat[:, 1:2], stat[:, 0:1], ACT.Sqrt, bias=stat[:, 3:4],
                                     scale=1.0 / D_MODEL).then_inc(root_ready, 1)

            def copy_out(i):
                for n, j in enumerate((0, 2, 4, 6)):
                    act.wait_ge(even_done, i * 4 + n + 1)
                    if j == 0:
                        act.wait_ge(stored, i * 64 + 16)
                    dst = (token_out[:, j * 512:(j + 1) * 512] if j < 4 else
                           token_out[:, 2048:TOKW] if j == 4 else chan_out[:, 4:8, :])
                    src = (bank[:, j % 4, :] if j < 4 else bank[:, 0, 0:HEADS] if j == 4 else
                           bank[:, 2, :].rearrange("p (b t) -> p b t", b=4))
                    nc.scalar.activation(dst, src, ACT.Copy).then_inc(even_free, 1)

            norm(0)
            with act.Fori(0, MAIN_TILES) as i:
                norm(i + 1)
                copy_out(i)
            copy_out(MAIN_TILES)

        @block.vector
        def _(dve):
            chain = Chain(dve, dve_step)
            dve.sem_inc(odd_free, 2)
            dve.sem_inc(t_copied, 1)
            dve.sem_inc(stored, 16)
            nc.vector.memset(stat[:, 3:4], EPS).then_inc(square_ready, 1)
            dve.sem_inc(normed_ready, 1)

            def norm(i):
                dve.wait_ge(root_ready, i + 1)
                chain.link(nc.vector.reciprocal(stat[:, 2:3], stat[:, 1:2]))
                dve.wait_ge(transposed, i + 1)
                nc.vector.tensor_scalar(normed[:], x[:], stat[:, 2:3], None, ALU.mult).then_inc(normed_ready, 1)
                dve.wait_ge(normed_ready, i + 2)
                dve.sem_inc(x_free, 1)

            def copy_out(i):
                for n, j in enumerate((1, 3, 5, 7)):
                    dve.wait_ge(odd_done, i * 4 + n + 1)
                    if j == 1:
                        dve.wait_ge(stored, i * 64 + 16)
                    dst = (token_out[:, j * 512:(j + 1) * 512] if j < 4 else
                           chan_out[:, 0:4, :] if j == 5 else chan_out[:, 8:12, :])
                    src = bank[:, j % 4, :] if j < 4 else bank[:, j % 4, :].rearrange("p (b t) -> p b t", b=4)
                    nc.vector.tensor_copy(dst, src).then_inc(odd_free, 1)

            def copy_transposed(i):
                dve.wait_ge(transposed, i + 2)
                nc.vector.tensor_tensor(out=normed_t[:], in0=t_psum[:],
                                        in1=norm_w[:].unsqueeze(2).to_broadcast([P, KT, P]),
                                        op=ALU.mult).then_inc(t_copied, 1)

            dve.wait_ge(consts_in, 32)
            dve.sem_inc(transposed, 1)
            norm(0)
            with dve.Fori(0, MAIN_TILES) as i:
                chain.start(i + 1)
                copy_transposed(i)
                norm(i + 1)
                copy_out(i)
            copy_transposed(MAIN_TILES)
            copy_out(MAIN_TILES)

        @block.tensor
        def _(pe):
            pe.wait_ge(consts_in, 32)

            def tile(i, first):
                pe.wait_ge(normed_ready, i + 2)
                pe.wait_ge(t_copied, i + 1)
                for k in range(KT):
                    last = nc.tensor.transpose(t_psum[:, k, :], normed[:, k * P:(k + 1) * P], ident[:])
                last.then_inc(transposed, 1)
                pe.wait_ge(t_copied, i + 2)
                for j in range(ITEMS):
                    even = j % 2 == 0
                    pe.wait_ge(even_free if even else odd_free, i * 4 + j // 2 + 1)
                    if first:
                        pe.wait_ge(w_part_in[0 if j < 2 else 1 if j < 5 else 2], 16)
                    b = bank[:, j % 4, :]
                    if j < 5:
                        a, w = j * 512, 512 if j < 4 else HEADS
                        for k in range(KT):
                            last = nc.tensor.matmul(b[:, 0:w], normed_t[:, k, :], w_in[:, k, a:a + w],
                                                    start=k == 0, stop=k == KT - 1)
                    else:
                        for c in range(4):
                            a = TOKW + ((j - 5) * 4 + c) * P
                            for k in range(KT):
                                last = nc.tensor.matmul(b[:, c * P:(c + 1) * P], w_in[:, k, a:a + P],
                                                        normed_t[:, k, :], start=k == 0, stop=k == KT - 1)
                    last.then_inc(even_done if even else odd_done, 1)

            tile(0, True)
            with pe.Fori(1, TILES) as i:
                tile(i, False)


def s5_scan(nc, D):
    G2 = 2 * S5_CH
    LAG = Q + 1
    TWO_PI = 2.0 * np.pi
    PI_HI = 6.28125
    PI_LO = float(np.float32(TWO_PI - PI_HI))
    ROUND = 1.5 * 2.0 ** 23
    HALF_MAX = 1.5707963
    with ExitStack() as ctx:
        cur = lambda c: (lambda n, s, d=F32: c.enter_context(nc.sbuf_tensor("s5s_" + n, s, d)))
        sb = cur(ctx)
        sem = ctx.enter_context(stage_semaphores(nc, "s5_"))
        ident = sb("ident", [P, P])
        out_w = sb("out_w", [P, PAIRS, 2, LAG * S5_CH])
        in_w = sb("in_w", [P, PAIRS, 2, Q * S5_CH])
        toep = sb("toep", [P, S5_GROUPS, Q * S5_CH])
        b_bar = sb("b_bar", [P, PAIRS, 2, S5_CH])
        jump = sb("jump", [P, SCAN, 3, PAIRS])
        consts_in, u_in = sem("consts_in"), sem("u_in")

        with ExitStack() as c2:
            sb2 = cur(c2)
            par = sb2("par", [P, 3, PAIRS])
            b_in = sb2("b_in", [P, 2, PAIRS, S5_CH])
            c_in = sb2("c_in", [P, 2, PAIRS, S5_CH])
            skip = sb2("skip", [S5_CH, S5_GROUPS])
            tmp = sb2("tmp", [P, 16, PAIRS])
            power = sb2("power", [P, 2, PAIRS, LAG])
            down = sb2("down", [P, 2, PAIRS, Q])
            prod = sb2("prod", [P, PAIRS, LAG, S5_CH])
            prod2 = sb2("prod2", [P, PAIRS, LAG, S5_CH])
            skip_eye = sb2("skip_eye", [S5_CH, S5_GROUPS, S5_CH])
            kernels = sb2("kernels", [S5_CH, S5_GROUPS, Q * S5_CH])
            b_apart = sb2("b_apart", [P, 4, 2, 2, S5_CH])
            k_psum = c2.enter_context(nc.psum_tensor("s5_k_psum", [S5_CH, 8, Q * S5_CH], F32))
            act_done, dve_for_act, dve_step = sem("act_done"), sem("dve_for_act"), sem("p_dve_step")
            toep_zero, b_ready, k_made, k_copied, k_ready, toep_in = (sem("toep_zero"), sem("b_ready"),
                sem("k_made"), sem("k_copied"), sem("k_ready"), sem("toep_in"))
            w_ready = sem("w_ready")
            block = c2.enter_context(nc.Block())

            @block.sync
            def _(sp):
                for t, n in ((par, "s5_par"), (b_in, "s5_b"), (c_in, "s5_c"), (skip, "s5_d"), (ident, "ident")):
                    sp.dma_start(t[:], D[n]).then_inc(consts_in, 16)
                sp.wait_ge(toep_zero, 1)
                sp.wait_ge(k_ready, 1)
                for s in range(Q):
                    sp.dma_start(toep[s * S5_CH:(s + 1) * S5_CH, :, s * S5_CH:],
                                 kernels[:, :, 0:(Q - s) * S5_CH]).then_inc(toep_in, 16)
                sp.wait_ge(toep_in, 16 * Q)

            @block.gpsimd
            def _(pool):
                nc.gpsimd.memset(toep[:], 0.0).then_inc(toep_zero, 1)

            @block.scalar
            def _(act):
                act.wait_ge(consts_in, 80)
                nc.scalar.activation(tmp[:, 0, :], par[:, 2, :], ACT.Exp).then_inc(act_done, 1)
                act.wait_ge(dve_for_act, 1)
                nc.scalar.activation(tmp[:, 3, :], tmp[:, 1, :], ACT.Exp).then_inc(act_done, 1)
                act.wait_ge(dve_for_act, 2)
                nc.scalar.activation(tmp[:, 5, :], tmp[:, 4, :], ACT.Sin).then_inc(act_done, 1)
                act.wait_ge(dve_for_act, 3)
                nc.scalar.activation(tmp[:, 7, :], tmp[:, 6, :], ACT.Sin).then_inc(act_done, 1)
                with act.Fori(0, PAIRS // 4) as r:
                    act.wait_ge(k_made, r + 1)
                    nc.scalar.activation(kernels[:, bass.ds(r * 8, 8), :], k_psum[:], ACT.Copy).then_inc(k_copied, 1)

            @block.vector
            def _(dve):
                chain = Chain(dve, dve_step)
                V = nc.vector
                tt = lambda o, a, b, op: chain.link(V.tensor_tensor(out=o, in0=a, in1=b, op=op))
                T = lambda j: tmp[:, j, :]
                dve.wait_ge(act_done, 1)
                tt(T(2), par[:, 1, :], T(0), ALU.mult)
                V.tensor_tensor(out=T(1), in0=par[:, 0, :], in1=T(0), op=ALU.mult).then_inc(dve_for_act, 1)
                chain.link(V.tensor_scalar(T(8), T(2), 1.0 / TWO_PI, ROUND, ALU.mult, ALU.add))
                chain.link(V.tensor_scalar(T(8), T(8), ROUND, None, ALU.subtract))
                chain.link(V.scalar_tensor_tensor(out=T(9), in0=T(8), scalar=-PI_HI, in1=T(2), op0=ALU.mult, op1=ALU.add))
                chain.link(V.scalar_tensor_tensor(out=T(9), in0=T(8), scalar=-PI_LO, in1=T(9), op0=ALU.mult, op1=ALU.add))
                chain.link(V.tensor_scalar(T(9), T(9), 0.5, HALF_MAX, ALU.mult, ALU.min))
                V.tensor_scalar(T(4), T(9), -HALF_MAX, None, ALU.max).then_inc(dve_for_act, 1)
                dve.wait_ge(dve_for_act, 2)
                chain.link(V.tensor_scalar(T(10), T(4), -1.0, None, ALU.mult))
                tt(T(10), T(10), T(4), ALU.max)
                V.tensor_scalar(T(6), T(10), -1.0, float(np.pi / 2), ALU.mult, ALU.add).then_inc(dve_for_act, 1)
                dve.wait_ge(act_done, 4)
                a_re, a_im = power[:, 0, :, 1], power[:, 1, :, 1]
                tt(T(8), T(5), T(5), ALU.mult)
                chain.link(V.tensor_scalar(T(8), T(8), -2.0, 1.0, ALU.mult, ALU.add))
                tt(a_re, T(8), T(3), ALU.mult)
                tt(T(9), T(5), T(7), ALU.mult)
                chain.link(V.tensor_scalar(T(9), T(9), 2.0, None, ALU.mult))
                tt(a_im, T(9), T(3), ALU.mult)
                chain.link(V.memset(power[:, 0, :, 0], 1.0))
                chain.link(V.memset(power[:, 1, :, 0], 0.0))

                def complex_mult(o_re, o_im, x_re, x_im, y_re, y_im, t0, t1):
                    tt(t0, x_re, y_re, ALU.mult)
                    tt(t1, x_im, y_im, ALU.mult)
                    tt(o_re, t0, t1, ALU.subtract)
                    tt(t0, x_re, y_im, ALU.mult)
                    tt(t1, x_im, y_re, ALU.mult)
                    tt(o_im, t0, t1, ALU.add)

                for n in range(2, LAG):
                    complex_mult(power[:, 0, :, n], power[:, 1, :, n], power[:, 0, :, n - 1],
                                 power[:, 1, :, n - 1], a_re, a_im, T(8), T(9))
                for s in range(Q):
                    chain.link(V.tensor_copy(down[:, :, :, s], power[:, :, :, Q - 1 - s]))
                for h in range(2):
                    chain.link(V.tensor_copy(jump[:, 0, 1 + h, :], power[:, h, :, Q]))
                for j in range(1, SCAN):
                    complex_mult(jump[:, j, 1, :], jump[:, j, 2, :], jump[:, j - 1, 1, :], jump[:, j - 1, 2, :],
                                 jump[:, 0, 1, :], jump[:, 0, 2, :], T(8), T(9))
                chain.link(V.tensor_scalar(jump[:, :, 0, :], jump[:, :, 2, :], -1.0, None, ALU.mult))
                lre, lim = par[:, 0, :], par[:, 1, :]
                tt(T(8), lre, lre, ALU.mult)
                tt(T(9), lim, lim, ALU.mult)
                tt(T(8), T(8), T(9), ALU.add)
                chain.link(V.reciprocal(T(10), T(8)))
                chain.link(V.tensor_scalar(T(11), a_re, -1.0, None, ALU.add))
                tt(T(8), T(11), lre, ALU.mult)
                tt(T(9), a_im, lim, ALU.mult)
                tt(T(8), T(8), T(9), ALU.add)
                tt(T(12), T(8), T(10), ALU.mult)
                tt(T(8), a_im, lre, ALU.mult)
                tt(T(9), T(11), lim, ALU.mult)
                tt(T(8), T(8), T(9), ALU.subtract)
                tt(T(13), T(8), T(10), ALU.mult)
                f = lambda j: T(j).unsqueeze(2).to_broadcast([P, PAIRS, S5_CH])
                p0, p1 = prod[:, :, 0, :], prod2[:, :, 0, :]
                complex_mult(b_bar[:, :, 0, :], b_bar[:, :, 1, :], f(12), f(13), b_in[:, 0], b_in[:, 1], p0, p1)
                lagged = lambda t: t.unsqueeze(3).to_broadcast([P, PAIRS, LAG, S5_CH])
                chans = lambda t: t.unsqueeze(2).to_broadcast([P, PAIRS, LAG, S5_CH])
                o = lambda h: out_w[:, :, h, :].rearrange("p g (l c) -> p g l c", c=S5_CH)
                tt(prod[:], chans(c_in[:, 0]), lagged(power[:, 0]), ALU.mult)
                tt(prod2[:], chans(c_in[:, 1]), lagged(power[:, 1]), ALU.mult)
                tt(o(0), prod[:], prod2[:], ALU.subtract)
                tt(prod[:], chans(c_in[:, 0]), lagged(power[:, 1]), ALU.mult)
                tt(prod2[:], chans(c_in[:, 1]), lagged(power[:, 0]), ALU.mult)
                chain.link(V.scalar_tensor_tensor(
                    out=o(1).rearrange("p g l c -> p g (l c)"), in0=prod[:].rearrange("p g l c -> p g (l c)"),
                    scalar=-1.0, in1=prod2[:].rearrange("p g l c -> p g (l c)"), op0=ALU.mult, op1=ALU.subtract))
                chain.link(V.memset(b_apart[:], 0.0))
                dve.sem_inc(w_ready, 1)
                stepped = lambda t: t.unsqueeze(3).to_broadcast([P, PAIRS, Q, S5_CH])
                chans8 = lambda t: t.unsqueeze(2).to_broadcast([P, PAIRS, Q, S5_CH])
                iw = lambda h: in_w[:, :, h, :].rearrange("p g (l c) -> p g l c", c=S5_CH)
                base = chain.n
                with dve.Fori(0, PAIRS // 4) as r:
                    chain.start(base + 2 * r)
                    dve.wait_ge(k_copied, r + 1)
                    for g in range(2):
                        rows = slice(g * 64, g * 64 + 64)
                        chain.link(V.tensor_copy(b_apart[rows, :, g, :, :], b_bar[rows, bass.ds(r * 4, 4), :, :]))
                    dve.sem_inc(b_ready, 1)
                chain.start(base + PAIRS // 2)
                complex_mult(iw(0), iw(1), stepped(down[:, 0]), stepped(down[:, 1]), chans8(b_bar[:, :, 0, :]),
                             chans8(b_bar[:, :, 1, :]), prod[:, :, 0:Q, :], prod2[:, :, 0:Q, :])
                tt(skip_eye[:], skip[:].unsqueeze(2).to_broadcast([S5_CH, S5_GROUPS, S5_CH]),
                   ident[0:S5_CH, 0:S5_CH].unsqueeze(1).to_broadcast([S5_CH, S5_GROUPS, S5_CH]), ALU.mult)
                dve.wait_ge(k_copied, PAIRS // 4 + 1)
                V.tensor_tensor(out=kernels[:, :, 0:S5_CH], in0=kernels[:, :, 0:S5_CH], in1=skip_eye[:],
                                op=ALU.add).then_inc(k_ready, 1)

            @block.tensor
            def _(pe):
                pe.sem_inc(k_copied, 1)
                pe.wait_ge(w_ready, 1)
                with pe.Fori(0, PAIRS // 4) as r:
                    pe.wait_ge(b_ready, r + 1)
                    pe.wait_ge(k_copied, r + 1)
                    for j in range(4):
                        for g in range(2):
                            for h in range(2):
                                last = nc.tensor.matmul(k_psum[:, 2 * j + g, :], b_apart[:, j, g, h, :],
                                                        out_w[:, bass.ds(r * 4 + j, 1), h, 0:Q * S5_CH],
                                                        start=h == 0, stop=h == 1)
                    last.then_inc(k_made, 1)

        state = sb("state", [P, PAIRS, 2, CHUNKS])
        u = sb("u", [P, Q, D_MODEL])

        with ExitStack() as c2:
            sb2 = cur(c2)
            u_pair = sb2("u_pair", [P, 2, Q, S5_CH])
            u_rest = sb2("u_rest", [CH_REST, 2, Q, S5_CH])
            in_pair = sb2("in_pair", [P, 2, P])
            u_t = sb2("u_t", [P, 2, CHUNKS])
            in_t = sb2("in_t", [P, 2, P])
            ps = lambda n, s: c2.enter_context(nc.psum_tensor("s5p_" + n, s, F32))
            u_psum, in_psum = ps("u_psum", [P, 512]), ps("in_psum", [P, 2, P])
            v_psum, y_psum = ps("v_psum", [P, 2, CHUNKS]), ps("y_psum", [P, 2, Q, S5_CH])
            u_picked, in_picked, rest_in = sem("u_picked"), sem("in_picked"), sem("rest_in")
            u_turned, in_turned, u_t_ready, in_t_ready = sem("u_turned"), sem("in_turned"), sem("u_t_ready"), sem("in_t_ready")
            v_made, v_kept, y_made, y_kept = sem("v_made"), sem("v_kept"), sem("y_made"), sem("y_kept")
            block = c2.enter_context(nc.Block())
            rest_rows = D["u"][SEQ:SEQ + REST, :].rearrange("(k s) c -> k s c", s=Q)

            @block.sync
            def _(sp):
                sp.dma_start(u[:], D["u"][0:SEQ, :].rearrange("(k s) c -> k s c", s=Q)).then_inc(u_in, 16)
                sp.sem_inc(u_turned, 1)
                with sp.Fori(0, PAIRS) as r:
                    sp.wait_ge(u_turned, r + 1)
                    for g in range(2):
                        sp.dma_start(u_rest[:, g, :, :], rest_rows[:, :, bass.ds(r * G2 + g * S5_CH, S5_CH)]).then_inc(rest_in, 16)

            @block.gpsimd
            def _(pool):
                pool.wait_ge(u_in, 16)
                with pool.Fori(0, PAIRS) as r:
                    pool.wait_ge(u_turned, r + 1)
                    for g in range(2):
                        last = nc.gpsimd.tensor_copy(u_pair[:, g, :, :], u[:, :, bass.ds(r * G2 + g * S5_CH, S5_CH)])
                    last.then_inc(u_picked, 1)
                    pool.wait_ge(in_turned, r + 1)
                    nc.gpsimd.tensor_copy(in_pair[:].unsqueeze(1), in_w[:, bass.ds(r, 1), :, :]).then_inc(in_picked, 1)

            @block.tensor
            def _(pe):
                pe.sem_inc(in_turned, 1)
                with pe.Fori(0, PAIRS) as r:
                    pe.wait_ge(u_picked, r + 1)
                    pe.wait_ge(rest_in, 32 * r + 32)
                    pe.wait_ge(u_t_ready, r + 1)
                    for g in range(2):
                        nc.tensor.transpose(u_psum[:, g * P:(g + 1) * P], u_pair[:, g].rearrange("p s c -> p (s c)"), ident[:])
                        last = nc.tensor.transpose(u_psum[:, 2 * P + g * CH_REST:2 * P + (g + 1) * CH_REST],
                                                   u_rest[:, g].rearrange("p s c -> p (s c)"), ident[0:CH_REST, 0:CH_REST])
                    last.then_inc(u_turned, 1)
                    pe.wait_ge(in_picked, r + 1)
                    pe.wait_ge(in_t_ready, r + 1)
                    for h in range(2):
                        last = nc.tensor.transpose(in_psum[:, h, :], in_pair[:, h, :], ident[:])
                    last.then_inc(in_turned, 1)
                    pe.wait_ge(u_t_ready, r + 2)
                    pe.wait_ge(in_t_ready, r + 2)
                    pe.wait_ge(v_kept, r + 1)
                    for h in range(2):
                        for g in range(2):
                            last = nc.tensor.matmul(v_psum[g * 64:g * 64 + 64, h, :], in_t[:, h, g * 64:g * 64 + 64],
                                                    u_t[:, g, :], start=True, stop=True)
                    last.then_inc(v_made, 1)
                    pe.wait_ge(y_kept, r + 1)
                    for g in range(2):
                        last = nc.tensor.matmul(y_psum[:, g].rearrange("p t c -> p (t c)"), u_t[:, g, CH_REST:],
                                                toep[:, bass.ds(r * 2 + g, 1), :], start=True, stop=True)
                    last.then_inc(y_made, 1)

            @block.scalar
            def _(act):
                act.sem_inc(u_t_ready, 1)
                act.sem_inc(y_kept, 1)
                with act.Fori(0, PAIRS) as r:
                    act.wait_ge(u_turned, r + 2)
                    act.wait_ge(y_made, r + 1)
                    nc.scalar.activation(u_t[:, :, CH_REST:], u_psum[:, 0:2 * P].rearrange("p (g k) -> p g k", g=2), ACT.Copy)
                    nc.scalar.activation(u_t[:, :, 0:CH_REST],
                                         u_psum[:, 2 * P:2 * P + 2 * CH_REST].rearrange("p (g k) -> p g k", g=2),
                                         ACT.Copy).then_inc(u_t_ready, 1)
                    act.wait_ge(y_made, r + 2)
                    for g in range(2):
                        last = nc.scalar.activation(u[:, :, bass.ds(r * G2 + g * S5_CH, S5_CH)], y_psum[:, g], ACT.Copy)
                    last.then_inc(y_kept, 1)

            @block.vector
            def _(dve):
                dve.sem_inc(in_t_ready, 1)
                dve.sem_inc(v_kept, 1)
                dve.sem_inc(y_made, 1)
                with dve.Fori(0, PAIRS) as r:
                    dve.wait_ge(in_turned, r + 2)
                    dve.wait_ge(v_kept, r + 1)
                    nc.vector.tensor_copy(in_t[:], in_psum[:]).then_inc(in_t_ready, 1)
                    dve.wait_ge(v_made, r + 1)
                    nc.vector.tensor_copy(state[:, bass.ds(r, 1), :, :], v_psum[:].unsqueeze(1)).then_inc(v_kept, 1)

        rest_start = sb("rest_start", [P, PAIRS, 2, CH_REST])
        with ExitStack() as c2:
            sb2 = cur(c2)
            end = sb2("end", [P, PAIRS, 2, SEQS])
            last_prompt = sb2("last_prompt", [P, PAIRS, 2])
            t0 = sb2("t0", [P, PAIRS, 2, BLOCKS])
            t1 = sb2("t1", [P, PAIRS, 2, BLOCKS])
            h0_in, ends_ready, ends_out, sc_step = sem("h0_in"), sem("ends_ready"), sem("ends_out"), sem("sc_step")
            block = c2.enter_context(nc.Block())

            @block.sync
            def _(sp):
                sp.dma_start(rest_start[:, :, :, 0:SEQS], D["s5_h0"]).then_inc(h0_in, 16)
                sp.wait_ge(ends_ready, 1)
                sp.dma_start(D["s5_end_sample"], end[:]).then_inc(ends_out, 16)
                sp.dma_start(D["s5_end_prompt"], last_prompt[:]).then_inc(ends_out, 16)
                sp.wait_ge(ends_out, 32)

            @block.vector
            def _(dve):
                chain = Chain(dve, sc_step)
                V = nc.vector
                tt = lambda o, a, b, op: chain.link(V.tensor_tensor(out=o, in0=a, in1=b, op=op))

                def advance(dst, src, j, n, out=None):
                    a, b = t0[:, :, :, 0:n], t1[:, :, :, 0:n]
                    tab = lambda c: jump[:, j, c, :].unsqueeze(2).to_broadcast([P, PAIRS, n])
                    for h in range(2):
                        V.tensor_tensor(out=b[:, :, h], in0=src[:, :, 1 - h], in1=tab(2 * h), op=ALU.mult)
                        last = V.tensor_tensor(out=a[:, :, h], in0=src[:, :, h], in1=tab(1), op=ALU.mult)
                    chain.link(last)
                    tt(a, a, b, ALU.add)
                    tt(dst if out is None else out, dst, a, ALU.add)

                prompt = state[:, :, :, SEQS:].rearrange("p g h (b j) -> p g h b j", j=SCAN)
                for j in range(1, SCAN):
                    advance(prompt[:, :, :, :, j], prompt[:, :, :, :, j - 1], 0, BLOCKS)
                for b in range(1, BLOCKS):
                    advance(prompt[:, :, :, b:b + 1, SCAN - 1], prompt[:, :, :, b - 1:b, SCAN - 1], SCAN - 1, 1)
                for j in range(SCAN - 1):
                    advance(prompt[:, :, :, 1:, j], prompt[:, :, :, :BLOCKS - 1, SCAN - 1], j, BLOCKS - 1)
                dve.wait_ge(h0_in, 16)
                advance(state[:, :, :, 0:SEQS], rest_start[:, :, :, 0:SEQS], 0, SEQS, out=end[:])
                chain.link(V.tensor_copy(last_prompt[:], state[:, :, :, CHUNKS - 1]))
                chain.link(V.memset(rest_start[:, :, :, SEQS], 0.0))
                V.tensor_copy(rest_start[:, :, :, SEQS + 1], state[:, :, :, SEQS]).then_inc(ends_ready, 1)

        with ExitStack() as c2:
            sb2 = cur(c2)
            start = sb2("start", [P, 2, 2, CHUNKS])
            u_rest = sb2("u_rest2", [P, 2, P])
            u_t = sb2("u_t2", [P, 2, P])
            rest = in_w[0:CH_REST].rearrange("k p g n -> k (p g) n")
            ps = lambda n, s: c2.enter_context(nc.psum_tensor("s5p_" + n, s, F32))
            u_psum = ps("u_psum2", [P, 2, P])
            y_psum, r_psum = ps("y_psum2", [P, 2, Q, S5_CH]), ps("r_psum", [P, 2, Q, S5_CH])
            rest_in, rest_picked, u_turned, u_t_ready = sem("rest_in2"), sem("rest_picked"), sem("u_turned2"), sem("u_t_ready2")
            zeroed, start_ready, y_made, y_kept, r_made, r_kept, r_out, y_out = (sem(n) for n in (
                "zeroed", "start_ready", "y_made2", "y_kept2", "r_made", "r_kept", "r_out", "y_out"))
            block = c2.enter_context(nc.Block())
            rest_u = D["u"][SEQ:SEQ + REST, :].rearrange("(k s) c -> k s c", s=Q)
            rest_y = D["y5"][SEQ:SEQ + REST, :].rearrange("(k s) c -> k s c", s=Q)

            @block.sync
            def _(sp):
                for s in range(Q):
                    sp.dma_start(rest[:, :, s * S5_CH:(s + 1) * S5_CH], rest_u[:, s, :].rearrange("k (g c) -> k g c", c=S5_CH)).then_inc(rest_in, 16)
                sp.wait_ge(y_kept, PAIRS + 1)
                sp.dma_start(D["y5"][0:SEQ, :].rearrange("(k s) c -> k s c", s=Q), u[:]).then_inc(y_out, 16)
                sp.wait_ge(r_kept, PAIRS + 1)
                for s in range(Q):
                    sp.dma_start(rest_y[:, s, :].rearrange("k (g c) -> k g c", c=S5_CH), rest[:, :, s * S5_CH:(s + 1) * S5_CH]).then_inc(r_out, 16)
                sp.wait_ge(r_out, 16 * Q)
                sp.wait_ge(y_out, 16)

            @block.gpsimd
            def _(pool):
                nc.gpsimd.memset(start[:], 0.0).then_inc(zeroed, 1)
                nc.gpsimd.memset(u_rest[:], 0.0).then_inc(zeroed, 1)
                pool.sem_inc(u_turned, 1)
                pool.wait_ge(rest_in, 16 * Q)
                pool.wait_ge(zeroed, 2)
                with pool.Fori(0, PAIRS) as r:
                    pool.wait_ge(u_turned, r + 1)
                    nc.gpsimd.tensor_copy(u_rest[0:CH_REST], rest[:, bass.ds(2 * r, 2), :]).then_inc(rest_picked, 1)

            @block.scalar
            def _(act):
                act.sem_inc(u_t_ready, 1)
                act.sem_inc(r_kept, 1)
                with act.Fori(0, PAIRS) as r:
                    act.wait_ge(u_turned, r + 2)
                    nc.scalar.activation(u_t[:], u_psum[:], ACT.Copy).then_inc(u_t_ready, 1)
                    act.wait_ge(r_made, r + 1)
                    nc.scalar.activation(rest[:, bass.ds(2 * r, 2), :], r_psum[0:CH_REST].rearrange("k g t c -> k g (t c)"), ACT.Copy).then_inc(r_kept, 1)

            @block.vector
            def _(dve):
                dve.wait_ge(zeroed, 2)
                dve.sem_inc(y_kept, 1)
                with dve.Fori(0, PAIRS) as r:
                    dve.wait_ge(r_kept, r + 1)
                    for g in range(2):
                        rows = slice(g * 64, g * 64 + 64)
                        nc.vector.tensor_copy(start[rows, g, :, 0:CH_REST].unsqueeze(1), rest_start[rows, bass.ds(r, 1), :, :])
                        last = nc.vector.tensor_copy(start[rows, g, :, CH_REST:].unsqueeze(1),
                                                     state[rows, bass.ds(r, 1), :, CH_REST - 1:CHUNKS - 1])
                    last.then_inc(start_ready, 1)
                    dve.wait_ge(y_made, r + 1)
                    for g in range(2):
                        cols = u[:, :, bass.ds(r * G2 + g * S5_CH, S5_CH)]
                        last = nc.vector.tensor_tensor(out=cols, in0=cols, in1=y_psum[:, g], op=ALU.add)
                    last.then_inc(y_kept, 1)

            @block.tensor
            def _(pe):
                with pe.Fori(0, PAIRS) as r:
                    pe.wait_ge(rest_picked, r + 1)
                    pe.wait_ge(u_t_ready, r + 1)
                    for g in range(2):
                        last = nc.tensor.transpose(u_psum[:, g, :], u_rest[:, g, :], ident[:])
                    last.then_inc(u_turned, 1)
                    pe.wait_ge(start_ready, r + 1)
                    pe.wait_ge(y_kept, r + 1)
                    for g in range(2):
                        for h in range(2):
                            last = nc.tensor.matmul(y_psum[:, g].rearrange("p t c -> p (t c)"), start[:, g, h, CH_REST:],
                                                    out_w[:, bass.ds(r, 1), h, S5_CH:], start=h == 0, stop=h == 1)
                    last.then_inc(y_made, 1)
                    pe.wait_ge(r_kept, r + 1)
                    pe.wait_ge(u_t_ready, r + 2)
                    for g in range(2):
                        o = r_psum[:, g].rearrange("p t c -> p (t c)")
                        nc.tensor.matmul(o, u_t[:, g, :], toep[:, bass.ds(r * 2 + g, 1), :], start=True, stop=False)
                        for h in range(2):
                            last = nc.tensor.matmul(o, start[:, g, h, 0:P], out_w[:, bass.ds(r, 1), h, S5_CH:],
                                                    start=False, stop=h == 1)
                    last.then_inc(r_made, 1)


def mamba_scan(nc, D):
    SEGS = SEQS + 1
    with ExitStack() as ctx:
        sb = lambda n, s, d=F32: ctx.enter_context(nc.sbuf_tensor("m2s_" + n, s, d))
        sem = ctx.enter_context(stage_semaphores(nc, "m2_"))
        ident = sb("ident", [P, P])
        after = sb("after", [P, P])
        upto = sb("upto", [P, P])
        ones = sb("ones", [P, P])
        after_seg = sb("after_seg", [P, P])
        upto_seg = sb("upto_seg", [P, P])
        in_seg = sb("in_seg", [P, SEGS, P])
        conv_w = sb("conv_w", [P, XB, TAPS])
        conv_b = sb("conv_b", [P, XB])
        head_par = sb("head_par", [P, 3, HEADS])
        a_neg = sb("a_neg", [P, HEADS])
        window = sb("window", [P, XB, P + TAPS - 1])
        conv = sb("conv", [P, XB, P])
        tap = sb("tap", [P, XB, P])
        xbc = sb("xbc", [P, XB, P])
        dt_raw = sb("dt_raw", [P, HEADS])
        small = sb("small", [P, 6, HEADS])
        dt = sb("dt", [P, HEADS])
        da = sb("da", [P, HEADS])
        e_acs = sb("e_acs", [P, HEADS])
        e_rev = sb("e_rev", [P, HEADS])
        e_tot = sb("e_tot", [P, HEADS])
        x_tok = sb("x_tok", [P, HEADS, HD])
        b_tok = sb("b_tok", [P, 2, NS])
        x_dt = sb("x_dt", [P, HEADS, HD])
        x_w = sb("x_w", [P, HEADS, HD])
        x_skip = sb("x_skip", [P, HEADS, HD])
        da_upto = sb("da_upto", [P, HEADS, P])
        decay = sb("decay", [P, HEADS, P])
        cb_masked = sb("cb_masked", [P, 2, P])
        y = sb("y", [P, HEADS, HD])
        state = sb("state", [P, HEADS, HD])
        ps_a = ctx.enter_context(nc.psum_tensor("m2p_a", [P, 4, 512], F32))
        ps_b = ctx.enter_context(nc.psum_tensor("m2p_b", [P, 3, 512], F32))
        ps_c = ctx.enter_context(nc.psum_tensor("m2p_c", [P, 512], F32))
        CB = 256

        consts_in, tile_in, conv_done, xbc_ready = sem("consts_in"), sem("tile_in"), sem("conv_done"), sem("xbc_ready")
        turned, tok_ready, b_ready = sem("turned"), sem("tok_ready"), sem("b_ready")
        abs_ready, soft_ready, dt_ready, a_ready = sem("abs_ready"), sem("soft_ready"), sem("dt_ready"), sem("a_ready")
        upto_ready, sums_made, sums_ready = sem("upto_ready"), sem("sums_made"), sem("sums_ready")
        seg_made, decay_ready, w_ready = sem("seg_made"), sem("decay_ready"), sem("w_ready")
        xw_ready, skip_ready, y_made, y_ready, st_made = sem("xw_ready"), sem("skip_ready"), sem("y_made"), sem("y_ready"), sem("st_made")
        state_ready, y_out, dve_step, act_step, pool_step = sem("state_ready"), sem("y_out"), sem("dve_step"), sem("act_step"), sem("pool_step")
        heads = lambda t: t.unsqueeze(2).to_broadcast([P, HEADS, HD])
        tt = lambda e, o, a, b, op: e.tensor_tensor(out=o, in0=a, in1=b, op=op)

        def dve_conv(dve, chain, k, views):
            V = nc.vector
            dve.wait_ge(tile_in, 32 * k + 32)
            dve.wait_ge(xbc_ready, k + 1)
            for w_in, o in views:
                dims = list(o(conv).shape)
                wt = lambda j: (conv_w[:, :, j].unsqueeze(2).to_broadcast(dims) if len(dims) == 3 else
                                conv_w[:, :, j].unsqueeze(2).unsqueeze(3).to_broadcast(dims))
                bias = (conv_b[:].unsqueeze(2).to_broadcast(dims) if len(dims) == 3 else
                        conv_b[:].unsqueeze(2).unsqueeze(3).to_broadcast(dims))
                chain.link(tt(V, o(conv), w_in(0), wt(0), ALU.mult))
                for j in range(1, TAPS):
                    chain.link(tt(V, o(tap), w_in(j), wt(j), ALU.mult))
                    chain.link(tt(V, o(conv), o(conv), o(tap), ALU.add))
                chain.link(tt(V, o(conv), o(conv), bias, ALU.add))
            dve.sem_inc(conv_done, 1)

        def dve_dt(dve, chain, k):
            V = nc.vector
            chain.link(tt(V, small[:, 0, :], dt_raw[:], head_par[:, 0, :], ALU.add))
            chain.link(V.tensor_scalar(small[:, 1, :], small[:, 0, :], -1.0, None, ALU.mult))
            tt(V, small[:, 1, :], small[:, 0, :], small[:, 1, :], ALU.max).then_inc(abs_ready, 1)

        def dve_da(dve, chain, k):
            V = nc.vector
            chain.link(V.tensor_scalar(small[:, 4, :], small[:, 0, :], 0.0, None, ALU.max))
            dve.wait_ge(soft_ready, k + 1)
            chain.link(tt(V, dt[:], small[:, 4, :], small[:, 3, :], ALU.add))
            tt(V, da[:], dt[:], a_neg[:], ALU.mult).then_inc(dt_ready, 1)

        def dve_tokens(dve, chain, k):
            V = nc.vector
            dve.wait_ge(turned, k + 1)
            chain.link(V.tensor_copy(x_tok[:], ps_b[:, 0:2, :].rearrange("p b (h d) -> p (b h) d", d=HD)))
            dve.sem_inc(tok_ready, 1)
            chain.link(tt(V, x_dt[:], x_tok[:], heads(dt[:]), ALU.mult))

        def dve_decays(dve, chain, k, cb_mask):
            V = nc.vector
            dve.wait_ge(sums_ready, k + 2)
            chain.link(tt(V, cb_masked[:], ps_c[:, CB:CB + 2 * P].rearrange("p (g l) -> p g l", g=2),
                          cb_mask.unsqueeze(1).to_broadcast([P, 2, P]), ALU.mult))
            dve.wait_ge(decay_ready, k + 1)
            for g in range(2):
                part = decay[:, g * HPG:(g + 1) * HPG, :]
                last = tt(V, part, part, cb_masked[:, g, :].unsqueeze(1).to_broadcast([P, HPG, P]), ALU.mult)
            last.then_inc(w_ready, 1)
            tt(V, x_w[:], x_dt[:], heads(e_rev[:]), ALU.mult).then_inc(xw_ready, 1)

        def dve_y(dve, chain, k):
            V = nc.vector
            dve.wait_ge(y_made, k + 1)
            dve.wait_ge(y_out, 16 * k + 16)
            chain.link(tt(V, y[:], ps_a[:, 2:4, :].rearrange("p b (h d) -> p (b h) d", d=HD), heads(e_acs[:]), ALU.mult))
            chain.link(tt(V, y[:], y[:], ps_a[:, 0:2, :].rearrange("p b (h d) -> p (b h) d", d=HD), ALU.add))
            dve.wait_ge(skip_ready, k + 1)
            tt(V, y[:], y[:], x_skip[:], ALU.add).then_inc(y_ready, 1)

        def pool_tile(pool, k, mask):
            G = nc.gpsimd
            pool.wait_ge(dt_ready, k + 1)
            pool.wait_ge(seg_made, k + 1)
            tt(G, da_upto[:], da[:].unsqueeze(2).to_broadcast([P, HEADS, P]),
               mask.unsqueeze(1).to_broadcast([P, HEADS, P]), ALU.mult).then_inc(upto_ready, 1)
            pool.wait_ge(tok_ready, k + 1)
            pool.wait_ge(y_ready, k + 1)
            tt(G, x_skip[:], x_tok[:], heads(head_par[:, 2, :]), ALU.mult).then_inc(skip_ready, 1)

        def pe_front(pe, k, m_after, m_upto):
            T = nc.tensor
            pe.wait_ge(xbc_ready, k + 2)
            pe.wait_ge(state_ready, k + 1)
            pe.wait_ge(b_ready, k + 1)
            for c in range(10):
                last = T.transpose(ps_b[:, c // 4, (c % 4) * P:(c % 4 + 1) * P], xbc[:, c, :], ident[:])
            last.then_inc(turned, 1)
            pe.wait_ge(dt_ready, k + 1)
            pe.wait_ge(sums_ready, k + 1)
            pe.wait_ge(w_ready, k + 1)
            for n, m in enumerate((m_upto, m_after, ones)):
                T.matmul(ps_c[:, n * HEADS:(n + 1) * HEADS], m[:], da[:], start=True, stop=True)
            for g in range(2):
                last = T.matmul(ps_c[:, CB + g * P:CB + (g + 1) * P], xbc[:, 8 + g, :], xbc[:, 10 + g, :], start=True, stop=True)
            last.then_inc(sums_made, 1)
            pe.wait_ge(upto_ready, k + 1)
            pe.wait_ge(y_ready, k + 1)
            for n in range(4):
                last = T.matmul(ps_a[:, n, :], m_after[:], da_upto[:, 4 * n:4 * n + 4, :].rearrange("p h l -> p (h l)"), start=True, stop=True)
            last.then_inc(seg_made, 1)

        def pe_inside(pe, k):
            pe.wait_ge(w_ready, k + 2)
            for h in range(HEADS):
                last = nc.tensor.matmul(ps_a[:, h // HPG, (h % HPG) * HD:(h % HPG + 1) * HD], decay[:, h, :], x_dt[:, h, :],
                                        start=True, stop=True)
            return last

        rest_steps = []

        with ExitStack() as c2:
            sb2 = lambda n, s, d=F32: c2.enter_context(nc.sbuf_tensor("m2r_" + n, s, d))
            sem2 = c2.enter_context(stage_semaphores(nc, "m2r_"))
            win_s = sb2("win_s", [P, XB, SEQS, STEPS + TAPS - 1])
            win_m = sb2("win_m", [P, XB, N_META + TAPS - 1])
            tail = sb2("tail", [P, XB, SEQS, TAPS - 1])
            start = sb2("start", [P, SEQS, HEADS, HD])
            c_apart = sb2("c_apart", [P, 2, SEQS, P])
            x_seg = sb2("x_seg", [P, HEADS, HD])
            e_seg = sb2("e_seg", [P, SEGS, HEADS])
            xbc_raw_in, zeroed, c_ready, start_in, tail_ready, tail_out = (sem2(n) for n in (
                "xbc_raw_in", "zeroed", "c_ready", "start_in", "tail_ready", "tail_out"))
            seg_sum_made, seg_sum_ready, x_seg_ready, seg_state_made, seg_state_ready, ends_out = (sem2(n) for n in (
                "seg_sum_made", "seg_sum_ready", "x_seg_ready", "seg_state_made", "seg_state_ready", "ends_out"))
            block = c2.enter_context(nc.Block())

            @block.sync
            def _(sp):
                for t, n in ((ident, "ident"), (after, "after"), (upto, "upto"), (ones, "ones"), (after_seg, "after_seg"),
                             (upto_seg, "upto_seg"), (in_seg, "in_seg"), (conv_w, "conv_w"), (conv_b, "conv_b"), (head_par, "head_par")):
                    sp.dma_start(t[:], D[n]).then_inc(consts_in, 16)
                rest = SEQ + N_META
                sp.dma_start(tail[:], D["conv_past"]).then_inc(xbc_raw_in, 16)
                sp.dma_start(window[:, :, 0:SAMPLE], D["xbc"][:, :, rest:rest + SAMPLE]).then_inc(xbc_raw_in, 16)
                sp.wait_ge(zeroed, 1)
                sp.dma_start(win_m[:, :, TAPS - 1:], D["xbc"][:, :, 0:N_META]).then_inc(tile_in, 16)
                sp.dma_start(dt_raw[:], D["dt"][SEQ:ROWS, :]).then_inc(tile_in, 16)
                sp.dma_start(start[:], D["ssm_h0"]).then_inc(start_in, 16)
                sp.wait_ge(tail_ready, 1)
                sp.dma_start(D["conv_end_sample"], tail[:]).then_inc(tail_out, 16)
                sp.wait_ge(y_ready, 2)
                sp.dma_start(D["ym"][SEQ:ROWS, :], y[:].rearrange("p h d -> p (h d)")).then_inc(y_out, 16)
                sp.wait_ge(seg_state_ready, SEQS)
                sp.dma_start(D["ssm_end_sample"], start[:]).then_inc(ends_out, 16)
                sp.wait_ge(ends_out, 16)
                sp.wait_ge(tail_out, 16)
                sp.wait_ge(y_out, 32)

            @block.gpsimd
            def _(pool):
                G = nc.gpsimd
                G.memset(win_m[:, :, 0:TAPS - 1], 0.0).then_inc(zeroed, 1)
                G.memset(conv[:], 0.0).then_inc(zeroed, 1)
                G.memset(c_apart[:], 0.0).then_inc(zeroed, 1)
                pool.sem_inc(seg_made, 1)
                pool.sem_inc(y_ready, 1)
                pool_tile(pool, 0, upto_seg[:])

            @block.scalar
            def _(act):
                act.wait_ge(consts_in, 160)
                act.sem_inc(xbc_ready, 1)
                act.sem_inc(b_ready, 1)
                act.sem_inc(sums_ready, 1)
                nc.scalar.activation(small[:, 5, :], head_par[:, 1, :], ACT.Exp).then_inc(a_ready, 1)
                act.wait_ge(conv_done, 1)
                nc.scalar.activation(xbc[:], conv[:], ACT.Silu).then_inc(xbc_ready, 1)
                act.wait_ge(abs_ready, 1)
                nc.scalar.activation(small[:, 2, :], small[:, 1, :], ACT.Exp, scale=-1.0).then_inc(act_step, 1)
                act.wait_ge(act_step, 1)
                nc.scalar.activation(small[:, 3, :], small[:, 2, :], ACT.Ln, bias=ones[:, 0:1]).then_inc(soft_ready, 1)
                act.wait_ge(turned, 1)
                nc.scalar.activation(b_tok[:], ps_b[:, 2, 0:2 * NS].rearrange("p (g n) -> p g n", g=2), ACT.Copy).then_inc(b_ready, 1)
                act.wait_ge(sums_made, 1)
                nc.scalar.activation(e_acs[:], ps_c[:, 0:HEADS], ACT.Exp)
                nc.scalar.activation(e_rev[:], ps_c[:, HEADS:2 * HEADS], ACT.Exp).then_inc(sums_ready, 1)
                act.wait_ge(seg_made, 2)
                nc.scalar.activation(decay[:], ps_a[:].rearrange("p b (h l) -> p (b h) l", l=P), ACT.Exp).then_inc(decay_ready, 1)
                act.wait_ge(seg_sum_made, 1)
                nc.scalar.activation(e_seg[:], ps_c[:, 0:SEGS * HEADS].rearrange("p (b h) -> p b h", h=HEADS), ACT.Exp).then_inc(seg_sum_ready, 1)

            @block.vector
            def _(dve):
                V = nc.vector
                chain = Chain(dve, dve_step)
                dve.sem_inc(y_out, 16)
                dve.sem_inc(w_ready, 1)
                dve.sem_inc(state_ready, 1)
                dve.wait_ge(a_ready, 1)
                chain.link(V.tensor_scalar(a_neg[:], small[:, 5, :], -1.0, None, ALU.mult))
                dve.wait_ge(xbc_raw_in, 32)
                chain.link(V.tensor_copy(win_s[:, :, :, 0:TAPS - 1], tail[:]))
                chain.link(V.tensor_copy(win_s[:, :, :, TAPS - 1:], window[:, :, 0:SAMPLE].rearrange("p x (b t) -> p x b t", b=SEQS)))
                V.tensor_copy(tail[:], win_s[:, :, :, STEPS:]).then_inc(tail_ready, 1)
                dve.wait_ge(zeroed, 3)
                dve_conv(dve, chain, 0, [
                    (lambda j: win_s[:, :, :, j:j + STEPS], lambda t: t[:, :, 0:SAMPLE].rearrange("p x (b t) -> p x b t", b=SEQS)),
                    (lambda j: win_m[:, :, j:j + N_META], lambda t: t[:, :, SAMPLE:REST])])
                dve_dt(dve, chain, 0)
                dve_da(dve, chain, 0)
                dve.wait_ge(xbc_ready, 2)
                for g in range(2):
                    c = c_apart[:, g]
                    diag = bass.AP(tensor=c.tensor, offset=c.offset, ap=[list(c.ap[0]), [P + STEPS, SEQS], [1, STEPS]])
                    last = V.tensor_copy(diag, xbc[:, 10 + g, 0:SAMPLE].rearrange("p (b t) -> p b t", b=SEQS))
                last.then_inc(c_ready, 1)
                dve_tokens(dve, chain, 0)
                dve_decays(dve, chain, 0, upto_seg[:])
                dve.wait_ge(xw_ready, 1)
                dve_y(dve, chain, 0)
                dve.wait_ge(seg_sum_ready, 1)
                dve.wait_ge(start_in, 16)
                for b in range(SEGS):
                    if b:
                        dve.wait_ge(seg_state_made, b)
                    V.tensor_scalar(x_seg[:], x_w[:], in_seg[:, b, 0:1], None, ALU.mult).then_inc(x_seg_ready, 1)
                    e = e_seg[:, b, :].unsqueeze(2).to_broadcast([P, HEADS, HD])
                    new = ps_b[:, 0:2, :].rearrange("p b (h d) -> p (b h) d", d=HD)
                    if b < SEQS:
                        chain.link(tt(V, start[:, b], start[:, b], e, ALU.mult))
                        dve.wait_ge(seg_state_made, b + 1)
                        tt(V, start[:, b], start[:, b], new, ALU.add).then_inc(seg_state_ready, 1)
                    else:
                        dve.wait_ge(seg_state_made, b + 1)
                        V.tensor_copy(state[:], new).then_inc(state_ready, 1)
                rest_steps.append(chain.n)

            @block.tensor
            def _(pe):
                T = nc.tensor
                pe.wait_ge(consts_in, 160)
                pe_front(pe, 0, after_seg, upto_seg)
                last = pe_inside(pe, 0)
                pe.wait_ge(c_ready, 1)
                pe.wait_ge(start_in, 16)
                for g in range(2):
                    for b in range(SEQS):
                        last = T.matmul(ps_a[:, 2 + g, :], c_apart[:, g, b, :], start[:, b, g * HPG:(g + 1) * HPG, :].rearrange("p h d -> p (h d)"),
                                        start=b == 0, stop=b == SEQS - 1)
                last.then_inc(y_made, 1)
                pe.wait_ge(sums_ready, 2)
                pe.wait_ge(w_ready, 2)
                for b in range(SEGS):
                    last = T.matmul(ps_c[:, b * HEADS:(b + 1) * HEADS], in_seg[:, b, :], da[:], start=True, stop=True)
                last.then_inc(seg_sum_made, 1)
                pe.wait_ge(b_ready, 2)
                for b in range(SEGS):
                    pe.wait_ge(x_seg_ready, b + 1)
                    if b:
                        pe.wait_ge(seg_state_ready, b)
                    for g in range(2):
                        last = T.matmul(ps_b[:, g, :], b_tok[:, g, :], x_seg[:, g * HPG:(g + 1) * HPG, :].rearrange("p h d -> p (h d)"), start=True, stop=True)
                    last.then_inc(seg_state_made, 1)

        with ExitStack() as c2:
            conv_tail = c2.enter_context(nc.sbuf_tensor("m2m_conv_tail", [P, XB, TAPS - 1], F32))
            prompt_out, tail_ready, window_free = sem("prompt_out"), sem("tail_ready"), sem("window_free")
            block = c2.enter_context(nc.Block())

            @block.sync
            def _(sp):
                def load(i):
                    sp.dma_start(window[:], D["xbc"][:, :, bass.ds(i * P + N_META - TAPS + 1, P + TAPS - 1)]).then_inc(tile_in, 16)
                    sp.dma_start(dt_raw[:], D["dt"][bass.ds(i * P, P), :]).then_inc(tile_in, 16)

                def store(i):
                    sp.wait_ge(y_ready, i + 3)
                    sp.dma_start(D["ym"][bass.ds(i * P, P), :], y[:].rearrange("p h d -> p (h d)")).then_inc(y_out, 16)

                load(0)
                with sp.Fori(0, MAIN_TILES - 1) as i:
                    sp.wait_ge(window_free, i + 1)
                    load(i + 1)
                    store(i)
                store(MAIN_TILES - 1)
                sp.wait_ge(state_ready, MAIN_TILES + 2)
                sp.dma_start(D["ssm_end_prompt"], state[:]).then_inc(prompt_out, 16)
                sp.wait_ge(tail_ready, 1)
                sp.dma_start(D["conv_end_prompt"], conv_tail[:]).then_inc(prompt_out, 16)
                sp.wait_ge(prompt_out, 32)
                sp.wait_ge(y_out, 16 * (MAIN_TILES + 2))

            @block.gpsimd
            def _(pool):
                with pool.Fori(1, TILES) as k:
                    pool_tile(pool, k, upto[:])

            @block.scalar
            def _(act):
                def soft(k):
                    act.wait_ge(abs_ready, k + 1)
                    nc.scalar.activation(small[:, 2, :], small[:, 1, :], ACT.Exp, scale=-1.0).then_inc(act_step, 1)
                    act.wait_ge(act_step, k + 1)
                    nc.scalar.activation(small[:, 3, :], small[:, 2, :], ACT.Ln, bias=ones[:, 0:1]).then_inc(soft_ready, 1)

                def silu(k):
                    act.wait_ge(conv_done, k + 1)
                    act.wait_ge(y_made, k)
                    nc.scalar.activation(xbc[:], conv[:], ACT.Silu).then_inc(xbc_ready, 1)

                def tile(k, more):
                    act.wait_ge(turned, k + 1)
                    nc.scalar.activation(b_tok[:], ps_b[:, 2, 0:2 * NS].rearrange("p (g n) -> p g n", g=2), ACT.Copy).then_inc(b_ready, 1)
                    act.wait_ge(sums_made, k + 1)
                    act.wait_ge(y_ready, k + 1)
                    nc.scalar.activation(e_acs[:], ps_c[:, 0:HEADS], ACT.Exp)
                    nc.scalar.activation(e_rev[:], ps_c[:, HEADS:2 * HEADS], ACT.Exp)
                    nc.scalar.activation(e_tot[:], ps_c[:, 2 * HEADS:3 * HEADS], ACT.Exp).then_inc(sums_ready, 1)
                    act.wait_ge(seg_made, k + 2)
                    nc.scalar.activation(decay[:], ps_a[:].rearrange("p b (h l) -> p (b h) l", l=P), ACT.Exp).then_inc(decay_ready, 1)
                    if more:
                        soft(k + 1)
                        silu(k + 1)

                soft(1)
                silu(1)
                with act.Fori(1, MAIN_TILES) as k:
                    tile(k, True)
                tile(MAIN_TILES, False)

            @block.vector
            def _(dve):
                V = nc.vector
                chain = Chain(dve, dve_step)
                STEPS_PER = 19
                begin = rest_steps[0]
                tail_cols = slice(P, P + TAPS - 1)

                def prepare(k):
                    dve_conv(dve, chain, k, [(lambda j: window[:, :, j:j + P], lambda t: t[:])])
                    chain.link(V.tensor_copy(conv_tail[:], window[:, :, tail_cols]))
                    dve_dt(dve, chain, k)
                    dve.sem_inc(window_free, 1)

                def tile(k, more):
                    chain.start(front + (k - 1) * STEPS_PER)
                    dve_tokens(dve, chain, k)
                    if more:
                        prepare(k + 1)
                    dve_decays(dve, chain, k, upto[:])
                    if more:
                        dve_da(dve, chain, k + 1)
                    dve.wait_ge(y_made, k + 1)
                    chain.link(tt(V, state[:], state[:], heads(e_tot[:]), ALU.mult))
                    dve.wait_ge(st_made, k)
                    tt(V, state[:], state[:], ps_b[:, 0:2, :].rearrange("p b (h d) -> p (b h) d", d=HD), ALU.add).then_inc(state_ready, 1)
                    dve_y(dve, chain, k)
                    assert chain.n == STEPS_PER or not more, chain.n

                chain.start(begin)
                prepare(1)
                dve_da(dve, chain, 1)
                front = begin + chain.n
                with dve.Fori(1, MAIN_TILES) as k:
                    tile(k, True)
                tile(MAIN_TILES, False)
                dve.wait_ge(state_ready, TILES + 1)
                dve.sem_inc(tail_ready, 1)

            @block.tensor
            def _(pe):
                T = nc.tensor
                with pe.Fori(1, TILES) as k:
                    pe_front(pe, k, after, upto)
                    last = pe_inside(pe, k)
                    for g in range(2):
                        last = T.matmul(ps_a[:, 2 + g, :], xbc[:, 10 + g, :], state[:, g * HPG:(g + 1) * HPG, :].rearrange("p h d -> p (h d)"),
                                        start=True, stop=True)
                    last.then_inc(y_made, 1)
                    pe.wait_ge(xw_ready, k + 1)
                    pe.wait_ge(b_ready, k + 2)
                    for g in range(2):
                        last = T.matmul(ps_b[:, g, :], b_tok[:, g, :], x_w[:, g * HPG:(g + 1) * HPG, :].rearrange("p h d -> p (h d)"),
                                        start=True, stop=True)
                    last.then_inc(st_made, 1)


def mix_out(nc, D):
    with ExitStack() as ctx:
        sb = lambda n, s, d=F32: ctx.enter_context(nc.sbuf_tensor("mo_" + n, s, d))
        sem = ctx.enter_context(stage_semaphores(nc, "mo_"))
        ident = sb("ident", [P, P])
        w_glu = sb("w_glu", [P, KT, D_MODEL])
        w_out = sb("w_out", [P, 2 * KT, D_MODEL])
        norm_w = sb("norm_w", [P, 2 * KT])
        eps = sb("eps", [P, 1])
        y5 = sb("y5", [P, D_MODEL])
        z = sb("z", [P, D_MODEL])
        ym = sb("ym", [P, D_MODEL])
        x = sb("x", [P, D_MODEL])
        g = sb("g", [P, D_MODEL])
        g_t = sb("g_t", [P, KT, P])
        sig = sb("sig", [P, D_MODEL])
        z_silu = sb("z_silu", [P, D_MODEL])
        square = sb("square", [P, D_MODEL])
        s5_n = sb("s5_n", [P, D_MODEL])
        m2_n = sb("m2_n", [P, D_MODEL])
        both_t = sb("both_t", [P, 2 * KT, P])
        x_mid = sb("x_mid", [P, D_MODEL])
        stat = sb("stat", [P, 3, 3])
        ps = lambda n: ctx.enter_context(nc.psum_tensor("mo_" + n, [P, KT, P], F32))
        ps_s5, ps_m2, ps_glu, ps_out = ps("ps_s5"), ps("ps_m2"), ps("ps_glu"), ps("ps_out")
        glu_in, out_in, consts_in, y_in, x_in, eps_set = (sem(n) for n in ("glu_in", "out_in", "consts_in", "y_in", "x_in", "eps_set"))
        g_ready, z_ready, m2_gated, m2_summed, m2_root = (sem(n) for n in ("g_ready", "z_ready", "m2_gated", "m2_summed", "m2_root"))
        sig_ready, s5_gated, s5_summed, s5_root = (sem(n) for n in ("sig_ready", "s5_gated", "s5_summed", "s5_root"))
        g_turned, g_t_ready, m2_n_ready, m2_turned, m2_t_ready = (sem(n) for n in ("g_turned", "g_t_ready", "m2_n_ready", "m2_turned", "m2_t_ready"))
        glu_made, s5_n_ready, s5_turned, s5_t_ready = (sem(n) for n in ("glu_made", "s5_n_ready", "s5_turned", "s5_t_ready"))
        out_made, x_mid_ready, x_mid_out, dve_step = (sem(n) for n in ("out_made", "x_mid_ready", "x_mid_out", "dve_step"))
        flat = lambda t: t[:].rearrange("p b c -> p (b c)")
        block = ctx.enter_context(nc.Block())

        @block.sync
        def _(sp):
            def load_y(k):
                for t, n in ((y5, "y5"), (z, "z"), (ym, "ym")):
                    sp.dma_start(t[:], D[n][bass.ds(k * P, P), :]).then_inc(y_in, 16)

            def store(k):
                sp.wait_ge(x_mid_ready, k + 2)
                sp.dma_start(D["x_mid"][bass.ds(k * P, P), :], x_mid[:]).then_inc(x_mid_out, 16)

            load_y(0)
            sp.dma_start(x[:], D["x_all"][0:P, :]).then_inc(x_in, 16)
            sp.dma_start(ident[:], D["ident"]).then_inc(consts_in, 16)
            sp.dma_start(norm_w[:], D["mix_norm_w"]).then_inc(consts_in, 16)
            sp.dma_start(w_glu[:], D["w_glu"]).then_inc(glu_in, 16)
            sp.dma_start(w_out[:], D["w_out"]).then_inc(out_in, 16)
            with sp.Fori(0, MAIN_TILES) as k:
                sp.wait_ge(m2_gated, k + 1)
                sp.wait_ge(g_ready, k + 1)
                load_y(k + 1)
                store(k)
                sp.dma_start(x[:], D["x_all"][bass.ds(k * P + P, P), :]).then_inc(x_in, 16)
            store(MAIN_TILES)
            sp.wait_ge(x_mid_out, 16 * (TILES + 1))

        @block.scalar
        def _(act):
            A = nc.scalar.activation
            act.sem_inc(sig_ready, 1)
            act.wait_ge(eps_set, 1)
            with act.Fori(0, TILES) as k:
                act.wait_ge(y_in, 48 * k + 48)
                act.wait_ge(s5_gated, k + 1)
                A(g[:], y5[:], ACT.Gelu_apprx_tanh).then_inc(g_ready, 1)
                A(z_silu[:], z[:], ACT.Silu).then_inc(z_ready, 1)
                act.wait_ge(m2_gated, k + 1)
                for h in range(2):
                    half = slice(h * 512, h * 512 + 512)
                    last = A(square[:, half], m2_n[:, half], ACT.Square, accum_out=stat[:, 0, 1 + h:2 + h])
                last.then_inc(m2_summed, 1)
                act.wait_ge(m2_summed, k + 1)
                A(stat[:, 1, 1:3], stat[:, 0, 1:3], ACT.Sqrt, bias=eps[:], scale=2.0 / D_MODEL).then_inc(m2_root, 1)
                act.wait_ge(glu_made, k + 1)
                A(sig[:], flat(ps_glu), ACT.Sigmoid).then_inc(sig_ready, 1)
                act.wait_ge(s5_gated, k + 2)
                A(square[:], s5_n[:], ACT.Square, accum_out=stat[:, 0, 0:1]).then_inc(s5_summed, 1)
                act.wait_ge(s5_summed, k + 1)
                A(stat[:, 1, 0:1], stat[:, 0, 0:1], ACT.Sqrt, bias=eps[:], scale=1.0 / D_MODEL).then_inc(s5_root, 1)

        @block.vector
        def _(dve):
            V = nc.vector
            chain = Chain(dve, dve_step)
            STEPS_PER = 2
            dve.sem_inc(s5_gated, 1)
            dve.sem_inc(x_mid_out, 16)
            dve.sem_inc(x_mid_ready, 1)
            dve.sem_inc(s5_t_ready, 1)
            V.memset(eps[:], EPS).then_inc(eps_set, 1)
            dve.wait_ge(consts_in, 32)
            weigh = lambda o, src, w: V.tensor_tensor(out=o, in0=src[:], in1=w.unsqueeze(2).to_broadcast([P, KT, P]), op=ALU.mult)
            with dve.Fori(0, TILES) as k:
                chain.start(STEPS_PER * k)
                dve.wait_ge(z_ready, k + 1)
                V.tensor_tensor(out=m2_n[:], in0=ym[:], in1=z_silu[:], op=ALU.mult).then_inc(m2_gated, 1)
                dve.wait_ge(g_turned, k + 1)
                V.tensor_copy(g_t[:], ps_s5[:]).then_inc(g_t_ready, 1)
                dve.wait_ge(m2_root, k + 1)
                chain.link(V.reciprocal(stat[:, 2, 1:3], stat[:, 1, 1:3]))
                for h in range(2):
                    half = slice(h * 512, h * 512 + 512)
                    last = V.tensor_scalar(m2_n[:, half], m2_n[:, half], stat[:, 2, 1 + h:2 + h], None, ALU.mult)
                last.then_inc(m2_n_ready, 1)
                dve.wait_ge(m2_turned, k + 1)
                weigh(both_t[:, KT:, :], ps_m2, norm_w[:, KT:]).then_inc(m2_t_ready, 1)
                dve.wait_ge(sig_ready, k + 2)
                V.tensor_tensor(out=s5_n[:], in0=g[:], in1=sig[:], op=ALU.mult).then_inc(s5_gated, 1)
                dve.wait_ge(s5_root, k + 1)
                chain.link(V.reciprocal(stat[:, 2, 0:1], stat[:, 1, 0:1]))
                V.tensor_scalar(s5_n[:], s5_n[:], stat[:, 2, 0:1], None, ALU.mult).then_inc(s5_n_ready, 1)
                dve.wait_ge(s5_turned, k + 1)
                weigh(both_t[:, 0:KT, :], ps_s5, norm_w[:, 0:KT]).then_inc(s5_t_ready, 1)
                dve.wait_ge(out_made, k + 1)
                dve.wait_ge(x_in, 16 * k + 16)
                dve.wait_ge(x_mid_out, 16 * k + 16)
                V.tensor_tensor(out=x_mid[:], in0=x[:], in1=flat(ps_out), op=ALU.add).then_inc(x_mid_ready, 1)

        @block.tensor
        def _(pe):
            T = nc.tensor

            def turn(dst, src):
                for c in range(KT):
                    last = T.transpose(dst[:, c, :], src[:, c * P:(c + 1) * P], ident[:])
                return last

            def project(dst, src_t, w, c0, n, first, final):
                for half in range(2):
                    for c in range(c0, c0 + n):
                        last = T.matmul(flat(dst)[:, half * 512:half * 512 + 512], src_t[:, c, :], w[:, c, half * 512:half * 512 + 512],
                                        start=first and c == c0, stop=final and c == c0 + n - 1)
                return last

            pe.wait_ge(consts_in, 32)
            pe.wait_ge(glu_in, 16)
            pe.wait_ge(out_in, 16)
            with pe.Fori(0, TILES) as k:
                pe.wait_ge(g_ready, k + 1)
                pe.wait_ge(s5_t_ready, k + 1)
                turn(ps_s5, g).then_inc(g_turned, 1)
                pe.wait_ge(g_t_ready, k + 1)
                pe.wait_ge(sig_ready, k + 1)
                project(ps_glu, g_t, w_glu, 0, KT, True, True).then_inc(glu_made, 1)
                pe.wait_ge(m2_n_ready, k + 1)
                turn(ps_m2, m2_n).then_inc(m2_turned, 1)
                pe.wait_ge(m2_t_ready, k + 1)
                pe.wait_ge(x_mid_ready, k + 1)
                project(ps_out, both_t, w_out, KT, KT, True, False)
                pe.wait_ge(s5_n_ready, k + 1)
                turn(ps_s5, s5_n).then_inc(s5_turned, 1)
                pe.wait_ge(s5_t_ready, k + 2)
                project(ps_out, both_t, w_out, 0, KT, False, True).then_inc(out_made, 1)


def route_and_experts(nc, D):
    PAIR = 2 * PH
    LEAST = -3.0e38
    RING, GROUP = 8, 1
    RING_GROUPS = RING // GROUP
    GROUPS = SLOTS // GROUP
    USES = GROUPS // RING_GROUPS
    HALF = SLOTS // 2
    UNITS, UNIT = PAIR // 4, 4
    ROUTE_STEPS = 64
    EVERY = GROUPS // ROUTE_STEPS
    SQUARES, NORM, TURN, H_T, QUERY = 3, 5, 6, 7, 8
    Q_COPY, SCORE, SCORE_COPY, KEYS = QUERY + UNIT + 1, QUERY + UNIT + 2, QUERY + UNIT + 4, QUERY + UNIT + 5
    SUMS = KEYS + UNIT * UNITS
    EXP = SUMS + 16
    assert SUMS + 22 < ROUTE_STEPS - 8
    with ExitStack() as ctx:
        sb = lambda n, s, d=F32: ctx.enter_context(nc.sbuf_tensor("pe_" + n, s, d))
        sem = ctx.enter_context(stage_semaphores(nc, "pe_"))
        ident = sb("ident", [P, P])
        half_ident = sb("half_ident", [P, 2, P])
        ffn_w = sb("ffn_w", [P, D_MODEL])
        final_w = sb("final_w", [P, D_MODEL])
        count16 = sb("count16", [P, TOPK])
        eps = sb("eps", [P, 1])
        square = sb("square", [P, D_MODEL])
        w_q = sb("w_q", [P, KT, PAIR * P])
        keys_t = sb("keys_t", [P, PAIR, NK])
        x = sb("x", [P, D_MODEL])
        stat = sb("stat", [P, 3])
        h = sb("h", [P, D_MODEL])
        h_t = sb("h_t", [P, KT, P])
        q_t = sb("q_t", [P, 2, UNIT, P])
        work_a = sb("work_a", [P, PH * TOPK * TOPK])
        work_b = sb("work_b", [P, PH * TOPK * TOPK])
        rest = work_a[:].rearrange("p (j n) -> p j n", j=PAIR)
        cand = work_a[:].rearrange("p (h a b) -> p h a b", h=PH, a=TOPK)
        hit = work_a[:].rearrange("p (s j) -> p s j", s=SLOTS)
        score = work_b[:].rearrange("p (j n) -> p j n", j=PAIR)
        cand2 = work_b[:].rearrange("p (h c) -> p h c", h=PH)
        best = sb("best", [P, PH, 2, TOPK])
        best_i = sb("best_i", [P, PH, 2, TOPK], U32)
        best_f = sb("best_f", [P, PH, 2, TOPK])
        top = sb("top", [P, PH, TOPK])
        pos = sb("pos", [P, PH, TOPK], U32)
        pos_ab = sb("pos_ab", [P, 2, SLOTS], U32)
        pos_f = sb("pos_f", [P, 2, SLOTS])
        picked = sb("picked", [P, 2, SLOTS])
        index = sb("index", [P, SLOTS], I32)
        e = sb("e", [P, PH, TOPK])
        total = sb("total", [P, 2, PH])
        gate = sb("gate", [P, PH, TOPK])
        ring = sb("ring", [P, RING, 2 * D_MODEL])
        diag = sb("diag", [P, RING, P])
        x_now = sb("x_now", [P, D_MODEL])
        h_now = sb("h_now", [P, D_MODEL])
        gate_now = sb("gate_now", [P, SLOTS])
        index_now = sb("index_now", [P, 2, HALF], I32)
        dot = sb("dot", [P, RING])
        act_v = sb("act_v", [P, RING])
        out = sb("out", [P, D_MODEL])
        end_stat = sb("end_stat", [P, 3])
        acc = ctx.enter_context(nc.psum_tensor("pe_acc", [P, 2, 512], F32))
        ps_t = ctx.enter_context(nc.psum_tensor("pe_ps_t", [P, KT, P], F32))
        ps_q = ctx.enter_context(nc.psum_tensor("pe_ps_q", [P, 2, UNIT, P], F32))
        ps_s = ctx.enter_context(nc.psum_tensor("pe_ps_s", [P, 2, UNIT, P], F32))
        consts_in, x_in, w_q_in, eps_set, summed, root, h_ready = (sem(n) for n in (
            "consts_in", "x_in", "w_q_in", "eps_set", "summed", "root", "h_ready"))
        h_turned, h_t_ready, q_made, q_ready, s_made, s_ready = (sem(n) for n in (
            "h_turned", "h_t_ready", "q_made", "q_ready", "s_made", "s_ready"))
        shifted, e_ready, index_ready, index_taken, route_step, settled = (sem(n) for n in (
            "shifted", "e_ready", "index_ready", "index_taken", "route_step", "settled"))
        dots_ready, act_ready, diag_ready, group_done = sem("dots_ready"), sem("act_ready"), sem("diag_ready"), sem("group_done")
        rows_in = [sem(f"rows_in{g}") for g in range(RING_GROUPS)]
        x_now_ready, h_now_ready, tile_done, end_summed, end_root, end_step, y_ready, y_out = (sem(n) for n in (
            "x_now_ready", "h_now_ready", "tile_done", "end_summed", "end_root", "end_step", "y_ready", "y_out"))
        block = ctx.enter_context(nc.Block())

        def place(g):
            p = g % RING_GROUPS
            return p, range(p * GROUP, (p + 1) * GROUP), g // RING_GROUPS

        @block.sync
        def _(sp):
            sp.dma_start(x[:], D["x_mid"][0:P, :]).then_inc(x_in, 16)
            for t, n in ((ident, "ident"), (ffn_w, "norm_ffn_w"), (count16, "count16"), (keys_t, "keys_t"),
                         (half_ident, "half_ident"), (final_w, "final_norm_w")):
                sp.dma_start(t[:], D[n]).then_inc(consts_in, 16)
            sp.dma_start(w_q[:], D["w_q"]).then_inc(w_q_in, 16)
            with sp.Fori(0, MAIN_TILES) as k:
                sp.wait_ge(x_now_ready, k + 1)
                sp.dma_start(x[:], D["x_mid"][bass.ds(k * P + P, P), :]).then_inc(x_in, 16)
                sp.wait_ge(y_ready, k + 2)
                sp.dma_start(D["y"][bass.ds(k * P, P), :], out[:]).then_inc(y_out, 16)
            sp.wait_ge(y_ready, TILES + 1)
            sp.dma_start(D["y"][SEQ:SEQ + SAMPLE, :], out[0:SAMPLE, :]).then_inc(y_out, 16)
            sp.wait_ge(y_out, 16 * (TILES + 1))

        @block.gpsimd
        def _(pool):
            flat = index[:].rearrange("p (b s) -> p b s", b=2)
            pool.sem_inc(group_done, RING_GROUPS)

            def tile(k, rows, route):
                for g in range(GROUPS):
                    p, slots, use = place(g)
                    pool.wait_ge(group_done, k * GROUPS + g + 1)
                    if g == RING_GROUPS:
                        settle(pool, settled)
                        nc.gpsimd.tensor_copy(index_now[:, 1, :], flat[:, 1, :]).then_inc(index_taken, 1)
                        pool.wait_ge(index_taken, 2 * k + 2)
                    if g == GROUPS - RING_GROUPS and route:
                        pool.wait_ge(index_ready, k + 2)
                        settle(pool, settled)
                        nc.gpsimd.tensor_copy(index_now[:, 0, :], flat[:, 0, :]).then_inc(index_taken, 1)
                        pool.wait_ge(index_taken, 2 * k + 3)
                    settle(pool, settled)
                    for s in slots:
                        col = g * GROUP + s % GROUP
                        nc.gpsimd.indirect_dma_start(
                            out=ring[0:rows, s, :], out_offset=None, in_=D["uv"],
                            in_offset=bass.IndirectOffsetOnAxis(ap=index_now[0:rows, col // HALF, col % HALF:col % HALF + 1], axis=0)).then_inc(rows_in[p], 16)

            pool.wait_ge(index_ready, 1)
            nc.gpsimd.tensor_copy(index_now[:, 0, :], flat[:, 0, :]).then_inc(index_taken, 1)
            pool.wait_ge(index_taken, 1)
            with pool.Fori(0, MAIN_TILES) as k:
                tile(k, P, True)
            tile(MAIN_TILES, SAMPLE, False)

        @block.scalar
        def _(act):
            A = nc.scalar.activation

            def route(r, g):
                if g == SQUARES:
                    act.wait_ge(x_in, 16 * r + 16)
                    A(square[:], x[:], ACT.Square, accum_out=stat[:, 0:1]).then_inc(summed, 1)
                    act.wait_ge(summed, r + 1)
                    A(stat[:, 1:2], stat[:, 0:1], ACT.Sqrt, bias=eps[:], scale=1.0 / D_MODEL).then_inc(root, 1)
                if g == H_T:
                    act.wait_ge(h_turned, r + 1)
                    A(h_t[:], ps_t[:], ACT.Copy).then_inc(h_t_ready, 1)
                for n in range(UNITS):
                    if g == Q_COPY + UNIT * n:
                        act.wait_ge(q_made, UNITS * r + n + 1)
                        A(q_t[:, n % 2], ps_q[:, n % 2], ACT.Copy).then_inc(q_ready, 1)
                    if g == SCORE_COPY + UNIT * n:
                        act.wait_ge(s_made, UNITS * r + n + 1)
                        A(score[:, UNIT * n:UNIT * n + UNIT, :], ps_s[:, n % 2], ACT.Copy).then_inc(s_ready, 1)
                if g == EXP:
                    act.wait_ge(shifted, r + 1)
                    A(e[:], e[:], ACT.Exp).then_inc(e_ready, 1)

            def tile(k, rows, more):
                for g in range(GROUPS):
                    p, slots, use = place(g)
                    cols = slice(slots[0], slots[-1] + 1)
                    act.wait_ge(dots_ready, k * GROUPS + g + 1)
                    A(act_v[0:rows, cols], dot[0:rows, cols], ACT.Gelu_apprx_tanh).then_inc(act_ready, 1)
                    if more and g % EVERY == EVERY - 1:
                        route(k + 1, g // EVERY)
                act.wait_ge(tile_done, k + 1)
                A(square[:], acc[:].rearrange("p b c -> p (b c)"), ACT.Square, accum_out=end_stat[:, 0:1]).then_inc(end_summed, 1)
                act.wait_ge(end_summed, k + 1)
                A(end_stat[:, 1:2], end_stat[:, 0:1], ACT.Sqrt, bias=eps[:], scale=1.0 / D_MODEL).then_inc(end_root, 1)
                if more:
                    A(x_now[:], x[:], ACT.Copy).then_inc(x_now_ready, 1)

            act.wait_ge(eps_set, 1)
            for g in range(ROUTE_STEPS):
                route(0, g)
            A(x_now[:], x[:], ACT.Copy).then_inc(x_now_ready, 1)
            with act.Fori(0, MAIN_TILES) as k:
                tile(k, P, True)
            tile(MAIN_TILES, SAMPLE, False)

        @block.vector
        def _(dve):
            V = nc.vector
            chain = Chain(dve, route_step)
            end = Chain(dve, end_step)
            ROUTE_LINKS, END_LINKS = UNITS * 4 + 28, 2
            tt = lambda o, a, b, op: V.tensor_tensor(out=o, in0=a, in1=b, op=op)
            sums = cand.rearrange("p h a b -> p h (a b)")

            def route(r, g, more):
                if g == NORM:
                    dve.wait_ge(root, r + 1)
                    chain.link(V.reciprocal(stat[:, 2:3], stat[:, 1:2]))
                    V.scalar_tensor_tensor(out=h[:], in0=x[:], scalar=stat[:, 2:3], in1=ffn_w[:], op0=ALU.mult, op1=ALU.mult).then_inc(h_ready, 1)
                for n in range(UNITS):
                    pairs = [(j, j // 2, j % 2) for j in range(UNIT * n, UNIT * n + UNIT)]
                    if g == KEYS + UNIT * n:
                        dve.wait_ge(s_ready, UNITS * r + n + 1)
                        settle(dve, settled)
                        for j, a, b in pairs:
                            last = V.max(out=best[:, a, b, 0:8], in_=score[:, j, :])
                        chain.link(last)
                        settle(dve, settled)
                    if g == KEYS + UNIT * n + 1:
                        for j, a, b in pairs:
                            V.max_index(out=best_i[:, a, b, 0:8], in_max=best[:, a, b, 0:8], in_values=score[:, j, :])
                            last = V.match_replace(out=rest[:, j, :], in_to_replace=best[:, a, b, 0:8], in_values=score[:, j, :], imm_value=LEAST)
                        chain.link(last)
                        settle(dve, settled)
                    if g == KEYS + UNIT * n + 2:
                        for j, a, b in pairs:
                            last = V.max(out=best[:, a, b, 8:16], in_=rest[:, j, :])
                        chain.link(last)
                        settle(dve, settled)
                    if g == KEYS + UNIT * n + 3:
                        for j, a, b in pairs:
                            last = V.max_index(out=best_i[:, a, b, 8:16], in_max=best[:, a, b, 8:16], in_values=rest[:, j, :])
                        chain.link(last)
                if g == SUMS:
                    chain.link(V.tensor_copy(best_f[:], best_i[:]))
                    chain.link(tt(cand, best[:, :, 0, :].unsqueeze(3).to_broadcast([P, PH, TOPK, TOPK]),
                                  best[:, :, 1, :].unsqueeze(2).to_broadcast([P, PH, TOPK, TOPK]), ALU.add))
                    settle(dve, settled)
                for q in range(4):
                    heads = (2 * q, 2 * q + 1)
                    if g == SUMS + 1 + q:
                        for a in heads:
                            last = V.max(out=top[:, a, 0:8], in_=sums[:, a, :])
                        chain.link(last)
                        settle(dve, settled)
                    if g == SUMS + 5 + q:
                        for a in heads:
                            V.max_index(out=pos[:, a, 0:8], in_max=top[:, a, 0:8], in_values=sums[:, a, :])
                            last = V.match_replace(out=cand2[:, a, :], in_to_replace=top[:, a, 0:8], in_values=sums[:, a, :], imm_value=LEAST)
                        chain.link(last)
                        settle(dve, settled)
                for q in range(2):
                    heads = range(4 * q, 4 * q + 4)
                    if g == SUMS + 9 + q:
                        for a in heads:
                            last = V.max(out=top[:, a, 8:16], in_=cand2[:, a, :])
                        chain.link(last)
                        settle(dve, settled)
                    if g == SUMS + 11 + q:
                        for a in heads:
                            last = V.max_index(out=pos[:, a, 8:16], in_max=top[:, a, 8:16], in_values=cand2[:, a, :])
                        chain.link(last)
                if g == SUMS + 13:
                    tt(e[:], top[:], top[:, :, 0:1].to_broadcast([P, PH, TOPK]), ALU.subtract).then_inc(shifted, 1)
                    flat_pos = pos[:].rearrange("p h c -> p (h c)")
                    chain.link(V.tensor_scalar(pos_ab[:, 0, :], flat_pos, 4, None, ALU.logical_shift_right))
                    chain.link(V.tensor_scalar(pos_ab[:, 1, :], flat_pos, TOPK - 1, None, ALU.bitwise_and))
                    chain.link(V.tensor_copy(pos_f[:], pos_ab[:]))
                by_head = hit.rearrange("p (h c) j -> p h c j", h=PH)
                for b in range(2):
                    if g == SUMS + 14 + 3 * b:
                        chain.link(tt(hit, pos_f[:, b, :].unsqueeze(2).to_broadcast([P, SLOTS, TOPK]),
                                      count16[:].unsqueeze(1).to_broadcast([P, SLOTS, TOPK]), ALU.is_equal))
                    if g == SUMS + 15 + 3 * b:
                        chain.link(tt(by_head, by_head, best_f[:, :, b, :].unsqueeze(2).to_broadcast([P, PH, TOPK, TOPK]), ALU.mult))
                    if g == SUMS + 16 + 3 * b:
                        chain.link(V.tensor_reduce(out=picked[:, b, :], in_=hit, axis=AX.X, op=ALU.add))
                if g == SUMS + 20:
                    chain.link(V.scalar_tensor_tensor(out=pos_f[:, 0, :], in0=picked[:, 0, :], scalar=float(NK), in1=picked[:, 1, :],
                                                      op0=ALU.mult, op1=ALU.add))
                    if more:
                        dve.wait_ge(index_taken, 2 * r)
                    V.tensor_copy(index[:], pos_f[:, 0, :]).then_inc(index_ready, 1)
                if g == SUMS + 21:
                    dve.wait_ge(e_ready, r + 1)
                    chain.link(V.tensor_reduce(out=total[:, 0, :], in_=e[:], axis=AX.X, op=ALU.add))
                    chain.link(V.reciprocal(total[:, 1, :], total[:, 0, :]))
                    chain.link(tt(gate[:], e[:], total[:, 1, :].unsqueeze(2).to_broadcast([P, PH, TOPK]), ALU.mult))

            def tile(k, rows, more):
                end.start(END_LINKS * k)
                if more:
                    chain.start(ROUTE_LINKS * (k + 1))
                def weigh(g):
                    dve.wait_ge(act_ready, k * GROUPS + g + 1)
                    for s in place(g)[1]:
                        col = g * GROUP + s % GROUP
                        last = V.tensor_scalar(diag[0:rows, s, :], ident[0:rows, :], act_v[0:rows, s:s + 1],
                                               gate_now[0:rows, col:col + 1], ALU.mult, ALU.mult)
                    last.then_inc(diag_ready, 1)

                V.tensor_copy(gate_now[:], gate[:].rearrange("p h c -> p (h c)"))
                end.link(V.tensor_copy(h_now[:], h[:]))
                for g in range(GROUPS):
                    p, slots, use = place(g)
                    dve.wait_ge(rows_in[p], 16 * GROUP * (k * USES + use + 1))
                    for s in slots:
                        last = V.tensor_tensor_reduce(out=ring[0:rows, s, 0:D_MODEL], in0=ring[0:rows, s, 0:D_MODEL], in1=h_now[0:rows, :],
                                                      scale=1.0, scalar=0.0, op0=ALU.mult, op1=ALU.add, accum_out=dot[0:rows, s:s + 1])
                    last.then_inc(dots_ready, 1)
                    if more and g % EVERY == EVERY - 1:
                        route(k + 1, g // EVERY, True)
                    if g:
                        weigh(g - 1)
                weigh(GROUPS - 1)
                dve.wait_ge(end_root, k + 1)
                end.link(V.reciprocal(end_stat[:, 2:3], end_stat[:, 1:2]))
                dve.wait_ge(y_out, 16 * k + 16)
                V.scalar_tensor_tensor(out=out[:], in0=acc[:].rearrange("p b c -> p (b c)"), scalar=end_stat[:, 2:3], in1=final_w[:],
                                       op0=ALU.mult, op1=ALU.mult).then_inc(y_ready, 1)
                assert end.n == END_LINKS
                assert not more or chain.n == ROUTE_LINKS, chain.n

            V.memset(eps[:], EPS).then_inc(eps_set, 1)
            dve.sem_inc(y_out, 16)
            dve.sem_inc(y_ready, 1)
            dve.wait_ge(consts_in, 96)
            chain.start(0)
            for g in range(ROUTE_STEPS):
                route(0, g, False)
            with dve.Fori(0, MAIN_TILES) as k:
                tile(k, P, True)
            tile(MAIN_TILES, SAMPLE, False)

        @block.tensor
        def _(pe):
            T = nc.tensor

            def route(r, g):
                if g == TURN:
                    pe.wait_ge(h_ready, r + 1)
                    for c in range(KT):
                        last = T.transpose(ps_t[:, c, :], h[:, c * P:(c + 1) * P], ident[:])
                    last.then_inc(h_turned, 1)
                for j in range(PAIR):
                    n = j // UNIT
                    if g == QUERY + j:
                        if j == 0:
                            pe.wait_ge(h_t_ready, r + 1)
                        if n >= 2 and j % UNIT == 0:
                            pe.wait_ge(q_ready, UNITS * r + n - 1)
                        for c in range(KT):
                            last = T.matmul(ps_q[:, n % 2, j % UNIT, :], w_q[:, c, j * P:(j + 1) * P], h_t[:, c, :],
                                            start=c == 0, stop=c == KT - 1)
                        if j % UNIT == UNIT - 1:
                            last.then_inc(q_made, 1)
                for n in range(UNITS):
                    if g == SCORE + UNIT * n:
                        pe.wait_ge(q_ready, UNITS * r + n + 1)
                        if n >= 2:
                            pe.wait_ge(s_ready, UNITS * r + n - 1)
                        for j in range(UNIT):
                            last = T.matmul(ps_s[:, n % 2, j, :], q_t[:, n % 2, j, :], keys_t[:, UNIT * n + j, :], start=True, stop=True)
                        last.then_inc(s_made, 1)

            def add_x(half):
                for b in range(2):
                    last = T.matmul(acc[:, b, :], half_ident[:, half, :], x_now[:, b * 512:b * 512 + 512], start=half == 0, stop=half == 1)
                return last

            def tile(k, rows, more):
                pe.wait_ge(x_now_ready, k + 1)
                pe.wait_ge(y_ready, k + 1)
                add_x(0)
                for g in range(GROUPS):
                    p, slots, use = place(g)
                    pe.wait_ge(diag_ready, k * GROUPS + g + 1)
                    for s in slots:
                        for b in range(2):
                            last = T.matmul(acc[:, b, :], diag[0:rows, s, :], ring[0:rows, s, D_MODEL + b * 512:D_MODEL + b * 512 + 512],
                                            start=False, stop=False)
                    last.then_inc(group_done, 1)
                    if more and g % EVERY == EVERY - 1:
                        route(k + 1, g // EVERY)
                add_x(1).then_inc(tile_done, 1)

            pe.wait_ge(consts_in, 96)
            pe.wait_ge(w_q_in, 16)
            for g in range(ROUTE_STEPS):
                route(0, g)
            with pe.Fori(0, MAIN_TILES) as k:
                tile(k, P, True)
            tile(MAIN_TILES, SAMPLE, False)


def lay_out(x):
    r = lambda a: np.ascontiguousarray(a, np.float32)
    pairs = lambda a, *tail: a.reshape(PAIRS, 2, S5_STATE, *tail).transpose(1, 2, 0, *range(3, 3 + len(tail))).reshape(P, PAIRS, *tail)
    d = {}
    d["x_all"] = np.concatenate([x["x_prompt"][0], x["x_sample"].reshape(SAMPLE, D_MODEL), x["meta_tokens"],
                                 np.zeros((P - REST, D_MODEL), np.float32)])
    d["ident"] = np.eye(P, dtype=np.float32)
    d["half_ident"] = np.stack([np.diag(np.arange(P) < P // 2), np.diag(np.arange(P) >= P // 2)], 1)
    d["norm_mix_w"] = x["norm_mix_w"][0].reshape(KT, P).T
    w = x["w_in"][0]
    w = np.concatenate([w[:, :2 * D_MODEL], w[:, 2 * D_MODEL + XBC:], w[:, 2 * D_MODEL:2 * D_MODEL + XBC]], 1)
    d["w_in"] = w.reshape(KT, P, IN_PROJ).transpose(1, 0, 2)
    d["s5_par"] = np.stack([pairs(x["s5_lambda_re"][0]), pairs(x["s5_lambda_im"][0]),
                            pairs(np.repeat(x["s5_log_step"][0][:, None], S5_STATE, 1))], 1)
    d["s5_b"] = np.stack([pairs(x["s5_b_re"][0], S5_CH), pairs(x["s5_b_im"][0], S5_CH)], 1)
    d["s5_c"] = np.stack([pairs(x["s5_c_re"][0].transpose(0, 2, 1), S5_CH), pairs(x["s5_c_im"][0].transpose(0, 2, 1), S5_CH)], 1)
    d["s5_d"] = x["s5_d"][0].reshape(S5_GROUPS, S5_CH).T
    j = np.arange(P)
    seg = np.where(j < SAMPLE, j // STEPS, np.where(j < REST, SEQS, SEQS + 1 + j))
    same = seg[:, None] == seg[None, :]
    real = (j < REST)[:, None]
    d["after"], d["upto"], d["ones"] = j[:, None] > j[None, :], j[:, None] <= j[None, :], np.ones((P, P))
    d["after_seg"], d["upto_seg"] = d["after"] & same & real, d["upto"] & same & real
    d["in_seg"] = np.repeat((seg[:, None] == np.arange(SEQS + 1)[None, :])[:, :, None], P, 2)
    chan = lambda a: a.reshape(*a.shape[:-1], XB, P)
    d["conv_w"] = chan(x["m2_conv_w"][0]).transpose(2, 1, 0)
    d["conv_b"] = chan(x["m2_conv_b"][0]).T
    d["conv_past"] = chan(x["state_conv"][0]).transpose(3, 2, 0, 1)
    d["head_par"] = np.broadcast_to(np.stack([x["m2_dt_bias"][0], x["m2_a_log"][0], x["m2_d"][0]]), (P, 3, HEADS))
    d["ssm_h0"] = x["state_ssm"][0].transpose(3, 0, 1, 2)
    rows = lambda w: w.reshape(-1, P, w.shape[1]).transpose(1, 0, 2)
    d["w_glu"], d["w_out"], d["w_q"] = rows(x["s5_w_glu"][0]), rows(x["w_out"][0]), rows(x["peer_w_q"][0])
    d["mix_norm_w"] = np.concatenate([x["s5_norm_w"][0], x["m2_norm_w"][0]]).reshape(2 * KT, P).T
    d["keys_t"] = x["peer_sub_keys"][0].reshape(2 * PH, NK, P).transpose(2, 0, 1)
    d["norm_ffn_w"] = np.broadcast_to(x["norm_ffn_w"][0], (P, D_MODEL))
    d["final_norm_w"] = np.broadcast_to(x["final_norm_w"], (P, D_MODEL))
    d["count16"] = np.broadcast_to(np.arange(TOPK), (P, TOPK))
    d["uv"] = np.concatenate([x["peer_u"][0], x["peer_v"][0]], 1)
    h0 = np.stack([x["state_s5_re"][0], x["state_s5_im"][0]])
    d["s5_h0"] = h0.reshape(2, SEQS, PAIRS, 2, S5_STATE).transpose(3, 4, 2, 0, 1).reshape(P, PAIRS, 2, SEQS)
    return {k: r(v) for k, v in d.items()}


SCRATCH = {"u": (ROWS, D_MODEL), "z": (ROWS, D_MODEL), "dt": (ROWS, HEADS), "xbc": (P, XB, XCOLS), "y5": (ROWS, D_MODEL), "ym": (ROWS, D_MODEL),
           "x_mid": (ROWS, D_MODEL)}
OUTPUTS = {"y": (SEQ + SAMPLE, D_MODEL), "s5_end_sample": (P, PAIRS, 2, SEQS), "s5_end_prompt": (P, PAIRS, 2),
           "conv_end_sample": (P, XB, SEQS, TAPS - 1), "conv_end_prompt": (P, XB, TAPS - 1),
           "ssm_end_sample": (P, SEQS, HEADS, HD), "ssm_end_prompt": (P, HEADS, HD)}


def write_program(nc, D):
    project_tokens(nc, D)
    s5_scan(nc, D)
    mamba_scan(nc, D)
    mix_out(nc, D)
    route_and_experts(nc, D)


def kernel(**inputs):
    import concourse.bacc as bacc
    from concourse.bass_utils import run_bass_kernel_spmd

    x = {name: np.asarray(a) for name, a in inputs.items()}
    nc = bacc.Bacc("TRN2", target_bir_lowering=False, num_devices=1)
    arrays = lay_out(x)
    D = {name: nc.dram_tensor("in_" + name, a.shape, F32, kind="ExternalInput").ap() for name, a in arrays.items()}
    for name, shape in SCRATCH.items():
        D[name] = nc.dram_tensor("scratch_" + name, shape, I32 if name == "index" else F32).ap()
    for name, shape in OUTPUTS.items():
        D[name] = nc.dram_tensor("out_" + name, shape, F32, kind="ExternalOutput").ap()
    write_program(nc, D)
    got = run_bass_kernel_spmd(nc, [{"in_" + n: a for n, a in arrays.items()}], core_ids=[0]).results[0]
    out = {name: np.asarray(got["out_" + name]) for name in OUTPUTS}

    s5 = lambda a, part: a[:, :, part].reshape(2, S5_STATE, PAIRS, -1).transpose(3, 2, 0, 1).reshape(1, -1, S5_GROUPS, S5_STATE)
    ssm = lambda a: a.reshape(NS, -1, HEADS, HD).transpose(1, 2, 3, 0)[None]
    conv = lambda a: a.reshape(P, XB, -1, TAPS - 1).transpose(2, 3, 1, 0).reshape(1, -1, TAPS - 1, XBC)
    r = np.ascontiguousarray
    return (r(out["y"][:SEQ].reshape(1, SEQ, D_MODEL)), r(out["y"][SEQ:].reshape(SEQS, STEPS, D_MODEL)),
            r(s5(out["s5_end_prompt"], 0)), r(s5(out["s5_end_prompt"], 1)), r(ssm(out["ssm_end_prompt"])), r(conv(out["conv_end_prompt"])),
            r(s5(out["s5_end_sample"], 0)), r(s5(out["s5_end_sample"], 1)), r(ssm(out["ssm_end_sample"])), r(conv(out["conv_end_sample"])))
```

```python
import numpy as np
import concourse.bass as bass
from concourse import mybir
from contextlib import ExitStack, contextmanager

F32 = mybir.dt.float32
I32 = mybir.dt.int32
U32 = mybir.dt.uint32
ALU = mybir.AluOpType
ACT = mybir.ActivationFunctionType
AX = mybir.AxisListType

P = 128
D_MODEL = 1024
KT = D_MODEL // P
SEQ = 1024
N_META = 16
SEQS = 8
STEPS = 8
SAMPLE = SEQS * STEPS
MAIN_TILES = SEQ // P
TILES = MAIN_TILES + 1
ROWS = TILES * P
REST = SAMPLE + N_META
EPS = 1e-6

S5_CH = 16
S5_GROUPS = 64
S5_STATE = 64
PAIRS = S5_GROUPS // 2
Q = 8
CH_MAIN = SEQ // Q
CH_META = N_META // Q
CH_REST = SEQS + CH_META
CHUNKS = CH_REST + CH_MAIN
CH_PROMPT = CH_META + CH_MAIN
SCAN = 10
BLOCKS = CH_PROMPT // SCAN
assert BLOCKS * SCAN == CH_PROMPT

HEADS = 16
HPG = 8
HD = 64
NS = 128
XBC = 1536
XB = XBC // P
TAPS = 4
TOKW = 2 * D_MODEL + HEADS
IN_PROJ = TOKW + XBC
XCOLS = N_META + SEQ + SAMPLE

PH = 8
NK = 128
TOPK = 16
SLOTS = PH * TOPK

LAG = Q + 1
TWO_PI = 2.0 * np.pi
PI_HI = 6.28125
PI_LO = float(np.float32(TWO_PI - PI_HI))
ROUND = 1.5 * 2.0 ** 23
HALF_MAX = 1.5707963


class Chain:

    def __init__(self, eng, sem):
        self.eng, self.sem, self.base, self.n = eng, sem, 0, 0

    def link(self, ins):
        self.n += 1
        ins.then_inc(self.sem, 1)
        self.eng.wait_ge(self.sem, self.base + self.n)

    def start(self, base):
        self.base, self.n = base, 0


def settle(eng, sem):
    eng.sem_inc(sem, 1)


def s5_tables(nc, ctx):
    sb = lambda n, s: ctx.enter_context(nc.sbuf_tensor("s5_" + n, s, F32))
    return {"power": sb("power", [P, 2, PAIRS, LAG]),
            "down": sb("down", [P, 2, PAIRS, Q]),
            "b_bar": sb("b_bar", [P, PAIRS, 2, S5_CH]),
            "jump": sb("jump", [P, SCAN, 3, PAIRS])}


@contextmanager
def stage_semaphores(nc, prefix):
    held = []

    def new(name):
        held.append(nc.alloc_semaphore(prefix + name))
        return held[-1]

    yield new
    nc.clear_and_free_semaphores(held)
    nc.all_engine_barrier()


def project_tokens(nc, D, tables):
    with ExitStack() as ctx:
        sb = lambda n, s, d=F32: ctx.enter_context(nc.sbuf_tensor("pj_" + n, s, d))
        ident = sb("ident", [P, P])
        norm_w = sb("norm_w", [P, KT])
        w_in = sb("w_in", [P, KT, IN_PROJ])
        x = sb("x", [P, D_MODEL])
        square = sb("square", [P, D_MODEL])
        stat = sb("stat", [P, 4])
        normed = sb("normed", [P, D_MODEL])
        normed_t = sb("normed_t", [P, 2, KT, P])
        token_out = sb("token_out", [P, TOKW])
        chan_out = sb("chan_out", [P, XB, P])
        par = sb("par", [P, 3, PAIRS])
        b_in = sb("b_in", [P, 2, PAIRS, S5_CH])
        tmp = sb("tmp", [P, 16, PAIRS])
        b_tmp = sb("b_tmp", [P, 2, PAIRS, S5_CH])
        power, down, b_bar, jump = (tables[n] for n in ("power", "down", "b_bar", "jump"))
        t_psum = ctx.enter_context(nc.psum_tensor("pj_t_psum", [P, KT, P], F32))
        bank = ctx.enter_context(nc.psum_tensor("pj_bank", [P, 4, 512], F32))
        sem = ctx.enter_context(stage_semaphores(nc, "pj_"))
        consts_in, x_in, x_free = sem("consts_in"), sem("x_in"), sem("x_free")
        w_part_in = [sem(f"w_in{j}") for j in range(3)]
        root_ready, square_ready, normed_ready = sem("root_ready"), sem("square_ready"), sem("normed_ready")
        transposed, t_copied = sem("transposed"), sem("t_copied")
        even_done, odd_done = sem("even_done"), sem("odd_done")
        even_free, odd_free = sem("even_free"), sem("odd_free")
        stored, padded, dve_step = sem("stored"), sem("padded"), sem("dve_step")
        par_in, act_done, for_act, pool_step = sem("par_in"), sem("act_done"), sem("for_act"), sem("pool_step")
        lambda_inverted, pole_step = sem("lambda_inverted"), sem("pole_step")
        ITEMS = 8
        W_CUT = [0, 2 * 512, TOKW, IN_PROJ]
        block = ctx.enter_context(nc.Block())

        @block.sync
        def _(sp):
            sp.dma_start(ident[:], D["ident"]).then_inc(consts_in, 16)
            sp.dma_start(norm_w[:], D["norm_mix_w"]).then_inc(consts_in, 16)
            sp.dma_start(D["y5"][SEQ + REST:ROWS, :], D["x_all"][SEQ + REST:ROWS, :]).then_inc(padded, 16)
            sp.dma_start(x[:], D["x_all"][0:P, :]).then_inc(x_in, 16)
            sp.dma_start(par[:], D["s5_par"]).then_inc(par_in, 16)
            sp.dma_start(b_in[:], D["s5_b"]).then_inc(par_in, 16)
            for j in range(3):
                a, b = W_CUT[j], W_CUT[j + 1]
                sp.dma_start(w_in[:, :, a:b], D["w_in"][:, :, a:b]).then_inc(w_part_in[j], 16)

            def store(i, col, width, dst_cols):
                sp.wait_ge(even_free, i * 4 + 2 + 4)
                sp.wait_ge(odd_free, i * 4 + 2 + 4)
                rows = bass.ds(i * P, P)
                sp.dma_start(D["u"][rows, :], token_out[:, 0:D_MODEL]).then_inc(stored, 16)
                sp.dma_start(D["z"][rows, :], token_out[:, D_MODEL:2 * D_MODEL]).then_inc(stored, 16)
                sp.dma_start(D["dt"][rows, :], token_out[:, 2 * D_MODEL:TOKW]).then_inc(stored, 16)
                sp.dma_start(D["xbc"][:, :, dst_cols], chan_out[:, :, col:col + width]).then_inc(stored, 16)

            with sp.Fori(0, MAIN_TILES) as i:
                sp.wait_ge(x_free, i + 1)
                sp.dma_start(x[:], D["x_all"][bass.ds(i * P + P, P), :]).then_inc(x_in, 16)
                store(i, 0, P, bass.ds(i * P + N_META, P))
            store(MAIN_TILES, 0, SAMPLE, bass.ds(N_META + SEQ, SAMPLE))
            sp.dma_start(D["xbc"][:, :, 0:N_META], chan_out[:, :, SAMPLE:REST]).then_inc(stored, 16)
            sp.wait_ge(stored, 16 * (4 * TILES + 2))
            sp.wait_ge(padded, 16)

        @block.gpsimd
        def _(pool):
            chain = Chain(pool, pool_step)
            tt = lambda o, a, b, op: chain.link(nc.gpsimd.tensor_tensor(out=o, in0=a, in1=b, op=op))
            T = lambda j: tmp[:, j, :]
            pool.wait_ge(act_done, 1)
            tt(T(2), par[:, 1, :], T(0), ALU.mult)
            nc.gpsimd.tensor_tensor(out=T(1), in0=par[:, 0, :], in1=T(0), op=ALU.mult).then_inc(for_act, 1)
            chain.link(nc.gpsimd.tensor_scalar(T(8), T(2), 1.0 / TWO_PI, ROUND, ALU.mult, ALU.add))
            chain.link(nc.gpsimd.tensor_scalar(T(8), T(8), ROUND, None, ALU.subtract))
            chain.link(nc.gpsimd.tensor_scalar(T(9), T(8), -PI_HI, None, ALU.mult))
            tt(T(9), T(9), T(2), ALU.add)
            chain.link(nc.gpsimd.tensor_scalar(T(10), T(8), -PI_LO, None, ALU.mult))
            tt(T(9), T(9), T(10), ALU.add)
            chain.link(nc.gpsimd.tensor_scalar(T(9), T(9), 0.5, HALF_MAX, ALU.mult, ALU.min))
            nc.gpsimd.tensor_scalar(T(4), T(9), -HALF_MAX, None, ALU.max).then_inc(for_act, 1)
            pool.wait_ge(act_done, 3)
            nc.gpsimd.tensor_scalar(T(6), T(10), -1.0, float(np.pi / 2), ALU.mult, ALU.add).then_inc(for_act, 1)
            pool.wait_ge(act_done, 5)
            a_re, a_im = power[:, 0, :, 1], power[:, 1, :, 1]
            tt(T(8), T(5), T(5), ALU.mult)
            chain.link(nc.gpsimd.tensor_scalar(T(8), T(8), -2.0, 1.0, ALU.mult, ALU.add))
            tt(a_re, T(8), T(3), ALU.mult)
            tt(T(9), T(5), T(7), ALU.mult)
            chain.link(nc.gpsimd.tensor_scalar(T(9), T(9), 2.0, None, ALU.mult))
            tt(a_im, T(9), T(3), ALU.mult)
            chain.link(nc.gpsimd.memset(power[:, 0, :, 0], 1.0))
            chain.link(nc.gpsimd.memset(power[:, 1, :, 0], 0.0))

            def complex_mult(o_re, o_im, x_re, x_im, y_re, y_im, t0, t1):
                tt(t0, x_re, y_re, ALU.mult)
                tt(t1, x_im, y_im, ALU.mult)
                tt(o_re, t0, t1, ALU.subtract)
                tt(t0, x_re, y_im, ALU.mult)
                tt(t1, x_im, y_re, ALU.mult)
                tt(o_im, t0, t1, ALU.add)

            for n in range(2, LAG):
                complex_mult(power[:, 0, :, n], power[:, 1, :, n], power[:, 0, :, n - 1],
                             power[:, 1, :, n - 1], a_re, a_im, T(8), T(9))
            for s in range(Q):
                chain.link(nc.gpsimd.tensor_copy(down[:, :, :, s], power[:, :, :, Q - 1 - s]))
            for h in range(2):
                chain.link(nc.gpsimd.tensor_copy(jump[:, 0, 1 + h, :], power[:, h, :, Q]))
            for j in range(1, SCAN):
                complex_mult(jump[:, j, 1, :], jump[:, j, 2, :], jump[:, j - 1, 1, :], jump[:, j - 1, 2, :],
                             jump[:, 0, 1, :], jump[:, 0, 2, :], T(8), T(9))
            chain.link(nc.gpsimd.tensor_scalar(jump[:, :, 0, :], jump[:, :, 2, :], -1.0, None, ALU.mult))
            lre, lim = par[:, 0, :], par[:, 1, :]
            pool.wait_ge(lambda_inverted, 1)
            chain.link(nc.gpsimd.tensor_scalar(T(11), a_re, -1.0, None, ALU.add))
            tt(T(8), T(11), lre, ALU.mult)
            tt(T(9), a_im, lim, ALU.mult)
            tt(T(8), T(8), T(9), ALU.add)
            tt(T(12), T(8), T(15), ALU.mult)
            tt(T(8), a_im, lre, ALU.mult)
            tt(T(9), T(11), lim, ALU.mult)
            tt(T(8), T(8), T(9), ALU.subtract)
            tt(T(13), T(8), T(15), ALU.mult)
            f = lambda j: T(j).unsqueeze(2).to_broadcast([P, PAIRS, S5_CH])
            p0, p1 = b_tmp[:, 0], b_tmp[:, 1]
            complex_mult(b_bar[:, :, 0, :], b_bar[:, :, 1, :], f(12), f(13), b_in[:, 0], b_in[:, 1], p0, p1)

        @block.scalar
        def _(act):
            act.sem_inc(even_free, 2)
            act.wait_ge(square_ready, 1)

            def norm(i):
                act.wait_ge(x_in, 16 * (i + 1))
                act.wait_ge(normed_ready, i + 1)
                nc.scalar.activation(square[:], x[:], ACT.Square, accum_out=stat[:, 0:1]).then_inc(square_ready, 1)
                act.wait_ge(square_ready, i + 2)
                nc.scalar.activation(stat[:, 1:2], stat[:, 0:1], ACT.Sqrt, bias=stat[:, 3:4],
                                     scale=1.0 / D_MODEL).then_inc(root_ready, 1)

            def copy_out(i):
                for n, j in enumerate((0, 2, 4, 6)):
                    act.wait_ge(even_done, i * 4 + n + 1)
                    if j == 0:
                        act.wait_ge(stored, i * 64 + 16)
                    dst = (token_out[:, j * 512:(j + 1) * 512] if j < 4 else
                           token_out[:, 2048:TOKW] if j == 4 else chan_out[:, 4:8, :])
                    src = (bank[:, j % 4, :] if j < 4 else bank[:, 0, 0:HEADS] if j == 4 else
                           bank[:, 2, :].rearrange("p (b t) -> p b t", b=4))
                    nc.scalar.activation(dst, src, ACT.Copy).then_inc(even_free, 1)

            norm(0)
            act.wait_ge(par_in, 32)
            nc.scalar.activation(tmp[:, 0, :], par[:, 2, :], ACT.Exp).then_inc(act_done, 1)
            act.wait_ge(for_act, 1)
            nc.scalar.activation(tmp[:, 3, :], tmp[:, 1, :], ACT.Exp).then_inc(act_done, 1)
            act.wait_ge(for_act, 2)
            nc.scalar.activation(tmp[:, 10, :], tmp[:, 4, :], ACT.Abs).then_inc(act_done, 1)
            nc.scalar.activation(tmp[:, 5, :], tmp[:, 4, :], ACT.Sin).then_inc(act_done, 1)
            act.wait_ge(for_act, 3)
            nc.scalar.activation(tmp[:, 7, :], tmp[:, 6, :], ACT.Sin).then_inc(act_done, 1)
            with act.Fori(0, MAIN_TILES) as i:
                norm(i + 1)
                copy_out(i)
            copy_out(MAIN_TILES)

        @block.vector
        def _(dve):
            chain = Chain(dve, dve_step)
            dve.sem_inc(odd_free, 2)
            dve.sem_inc(t_copied, 1)
            dve.sem_inc(stored, 16)
            nc.vector.memset(stat[:, 3:4], EPS).then_inc(square_ready, 1)
            dve.sem_inc(normed_ready, 1)

            def norm(i):
                dve.wait_ge(root_ready, i + 1)
                chain.link(nc.vector.reciprocal(stat[:, 2:3], stat[:, 1:2]))
                dve.wait_ge(transposed, i + 1)
                nc.vector.tensor_scalar(normed[:], x[:], stat[:, 2:3], None, ALU.mult).then_inc(normed_ready, 1)
                dve.wait_ge(normed_ready, i + 2)
                dve.sem_inc(x_free, 1)

            def copy_out(i, items):
                for j in items:
                    dve.wait_ge(odd_done, i * 4 + j // 2 + 1)
                    if j == 1:
                        dve.wait_ge(stored, i * 64 + 16)
                    dst = (token_out[:, j * 512:(j + 1) * 512] if j < 4 else
                           chan_out[:, 0:4, :] if j == 5 else chan_out[:, 8:12, :])
                    src = bank[:, j % 4, :] if j < 4 else bank[:, j % 4, :].rearrange("p (b t) -> p b t", b=4)
                    nc.vector.tensor_copy(dst, src).then_inc(odd_free, 1)

            def copy_transposed(i, odd):
                dve.wait_ge(transposed, i + 2)
                nc.vector.tensor_tensor(out=normed_t[:, odd], in0=t_psum[:],
                                        in1=norm_w[:].unsqueeze(2).to_broadcast([P, KT, P]),
                                        op=ALU.mult).then_inc(t_copied, 1)

            dve.wait_ge(consts_in, 32)
            dve.sem_inc(transposed, 1)
            norm(0)
            dve.wait_ge(par_in, 32)
            poles = Chain(dve, pole_step)
            nc.vector.tensor_tensor(out=tmp[:, 13, :], in0=par[:, 0, :], in1=par[:, 0, :], op=ALU.mult)
            poles.link(nc.vector.tensor_tensor(out=tmp[:, 14, :], in0=par[:, 1, :], in1=par[:, 1, :], op=ALU.mult))
            poles.link(nc.vector.tensor_tensor(out=tmp[:, 14, :], in0=tmp[:, 13, :], in1=tmp[:, 14, :], op=ALU.add))
            nc.vector.reciprocal(tmp[:, 15, :], tmp[:, 14, :]).then_inc(lambda_inverted, 1)
            copy_transposed(0, 0)

            def tile(i, odd):
                chain.start(i + 1)
                norm(i + 1)
                copy_out(i, (1, 3))
                copy_transposed(i + 1, 1 - odd)
                copy_out(i, (5, 7))

            with dve.Fori(0, MAIN_TILES // 2) as i2:
                tile(2 * i2, 0)
                tile(2 * i2 + 1, 1)
            copy_out(MAIN_TILES, (1, 3, 5, 7))

        @block.tensor
        def _(pe):
            pe.wait_ge(consts_in, 32)

            def turn(i):
                pe.wait_ge(normed_ready, i + 2)
                pe.wait_ge(t_copied, i + 1)
                for k in range(KT):
                    last = nc.tensor.transpose(t_psum[:, k, :], normed[:, k * P:(k + 1) * P], ident[:])
                last.then_inc(transposed, 1)

            def tile(i, odd, first=False, more=True):
                pe.wait_ge(t_copied, i + 2)
                x_t = normed_t[:, odd]
                for j in range(ITEMS):
                    if j == ITEMS // 2 and more:
                        turn(i + 1)
                    even = j % 2 == 0
                    pe.wait_ge(even_free if even else odd_free, i * 4 + j // 2 + 1)
                    if first:
                        pe.wait_ge(w_part_in[0 if j < 2 else 1 if j < 5 else 2], 16)
                    b = bank[:, j % 4, :]
                    if j < 5:
                        a, w = j * 512, 512 if j < 4 else HEADS
                        for k in range(KT):
                            last = nc.tensor.matmul(b[:, 0:w], x_t[:, k, :], w_in[:, k, a:a + w],
                                                    start=k == 0, stop=k == KT - 1)
                    else:
                        for c in range(4):
                            a = TOKW + ((j - 5) * 4 + c) * P
                            for k in range(KT):
                                last = nc.tensor.matmul(b[:, c * P:(c + 1) * P], w_in[:, k, a:a + P],
                                                        x_t[:, k, :], start=k == 0, stop=k == KT - 1)
                    last.then_inc(even_done if even else odd_done, 1)

            turn(0)
            tile(0, 0, first=True)
            tile(1, 1)
            with pe.Fori(1, MAIN_TILES // 2) as i2:
                tile(2 * i2, 0)
                tile(2 * i2 + 1, 1)
            tile(MAIN_TILES, 0, more=False)


def s5_scan(nc, D, tables):
    G2 = 2 * S5_CH
    power, down, b_bar, jump = (tables[n] for n in ("power", "down", "b_bar", "jump"))
    with ExitStack() as ctx:
        cur = lambda c: (lambda n, s, d=F32: c.enter_context(nc.sbuf_tensor("s5s_" + n, s, d)))
        sb = cur(ctx)
        sem = ctx.enter_context(stage_semaphores(nc, "s5_"))
        ident = sb("ident", [P, P])
        out_w = sb("out_w", [P, PAIRS, 2, LAG * S5_CH])
        in_w = sb("in_w", [P, PAIRS, 2, Q * S5_CH])
        toep = sb("toep", [P, S5_GROUPS, Q * S5_CH])
        u = sb("u", [P, Q, D_MODEL])
        consts_in, u_in = sem("consts_in"), sem("u_in")

        with ExitStack() as c2:
            sb2 = cur(c2)
            c_in = sb2("c_in", [P, 2, PAIRS, S5_CH])
            skip = sb2("skip", [S5_CH, S5_GROUPS])
            prod = sb2("prod", [P, PAIRS // 2, LAG, S5_CH])
            prod2 = sb2("prod2", [P, PAIRS // 2, LAG, S5_CH])
            skip_eye = sb2("skip_eye", [S5_CH, S5_GROUPS, S5_CH])
            kernels = sb2("kernels", [S5_CH, S5_GROUPS, Q * S5_CH])
            b_apart = sb2("b_apart", [P, 2, 4, 2, 2, S5_CH])
            k_psum = c2.enter_context(nc.psum_tensor("s5_k_psum", [S5_CH, 2, 8, Q * S5_CH], F32))
            dve_step = sem("p_dve_step")
            toep_zero, b_ready, k_made, k_copied, k_ready, toep_in = (sem("toep_zero"), sem("b_ready"),
                sem("k_made"), sem("k_copied"), sem("k_ready"), sem("toep_in"))
            w_ready, apart_zero = sem("w_ready"), sem("apart_zero")
            block = c2.enter_context(nc.Block())

            @block.sync
            def _(sp):
                for t, n in ((c_in, "s5_c"), (skip, "s5_d"), (ident, "ident")):
                    sp.dma_start(t[:], D[n]).then_inc(consts_in, 16)
                sp.dma_start(u[:], D["u"][0:SEQ, :].rearrange("(k s) c -> k s c", s=Q)).then_inc(u_in, 16)
                sp.wait_ge(toep_zero, 1)
                for half in range(2):
                    sp.wait_ge(k_ready, half + 1)
                    part = slice(half * PAIRS, (half + 1) * PAIRS)
                    for s in range(Q):
                        sp.dma_start(toep[s * S5_CH:(s + 1) * S5_CH, part, s * S5_CH:],
                                     kernels[:, part, 0:(Q - s) * S5_CH]).then_inc(toep_in, 16)
                sp.wait_ge(toep_in, 2 * 16 * Q)

            @block.gpsimd
            def _(pool):
                nc.gpsimd.memset(b_apart[:], 0.0).then_inc(apart_zero, 1)
                nc.gpsimd.memset(toep[:], 0.0).then_inc(toep_zero, 1)
                pool.wait_ge(apart_zero, 1)
                pool.wait_ge(toep_zero, 1)
                with pool.Fori(0, PAIRS // 8) as r:
                    for j in range(2):
                        m = 2 * r + j
                        pool.wait_ge(k_made, m + 1)
                        for g in range(2):
                            rows = slice(g * 64, g * 64 + 64)
                            last = nc.gpsimd.tensor_copy(b_apart[rows, j, :, g, :, :], b_bar[rows, bass.ds(m * 4, 4), :, :])
                        last.then_inc(b_ready, 1)

            @block.scalar
            def _(act):
                act.sem_inc(k_copied, 2)
                with act.Fori(0, PAIRS // 8) as r:
                    for j in range(2):
                        m = 2 * r + j
                        act.wait_ge(k_made, m + 3)
                        nc.scalar.activation(kernels[:, bass.ds(m * 8, 8), :], k_psum[:, j], ACT.Copy).then_inc(k_copied, 1)

            @block.vector
            def _(dve):
                chain = Chain(dve, dve_step)
                V = nc.vector
                tt = lambda o, a, b, op: chain.link(V.tensor_tensor(out=o, in0=a, in1=b, op=op))

                def complex_mult(o_re, o_im, x_re, x_im, y_re, y_im, t0, t1):
                    tt(t0, x_re, y_re, ALU.mult)
                    tt(t1, x_im, y_im, ALU.mult)
                    tt(o_re, t0, t1, ALU.subtract)
                    tt(t0, x_re, y_im, ALU.mult)
                    tt(t1, x_im, y_re, ALU.mult)
                    tt(o_im, t0, t1, ALU.add)

                dve.wait_ge(consts_in, 48)
                skip_term = lambda part: kernels[:, part, 0:S5_CH]
                tt(skip_eye[:], skip[:].unsqueeze(2).to_broadcast([S5_CH, S5_GROUPS, S5_CH]),
                   ident[0:S5_CH, 0:S5_CH].unsqueeze(1).to_broadcast([S5_CH, S5_GROUPS, S5_CH]), ALU.mult)

                def output_weights(pairs):
                    shape = [P, PAIRS // 2, LAG, S5_CH]
                    lagged = lambda h: power[:, h, pairs].unsqueeze(3).to_broadcast(shape)
                    chans = lambda h: c_in[:, h, pairs].unsqueeze(2).to_broadcast(shape)
                    o = lambda h: out_w[:, pairs, h, :].rearrange("p g (l c) -> p g l c", c=S5_CH)
                    tt(prod[:], chans(0), lagged(0), ALU.mult)
                    tt(prod2[:], chans(1), lagged(1), ALU.mult)
                    tt(o(0), prod[:], prod2[:], ALU.subtract)
                    tt(prod[:], chans(0), lagged(1), ALU.mult)
                    tt(prod2[:], chans(1), lagged(0), ALU.mult)
                    V.scalar_tensor_tensor(
                        out=o(1).rearrange("p g l c -> p g (l c)"), in0=prod[:].rearrange("p g l c -> p g (l c)"),
                        scalar=-1.0, in1=prod2[:].rearrange("p g l c -> p g (l c)"), op0=ALU.mult, op1=ALU.subtract).then_inc(w_ready, 1)

                def input_weights(pairs):
                    shape = [P, PAIRS // 2, Q, S5_CH]
                    stepped = lambda h: down[:, h, pairs].unsqueeze(3).to_broadcast(shape)
                    chans = lambda h: b_bar[:, pairs, h, :].unsqueeze(2).to_broadcast(shape)
                    iw = lambda h: in_w[:, pairs, h, :].rearrange("p g (l c) -> p g l c", c=S5_CH)
                    complex_mult(iw(0), iw(1), stepped(0), stepped(1), chans(0), chans(1), prod[:, :, 0:Q, :], prod2[:, :, 0:Q, :])

                for half in range(2):
                    output_weights(slice(half * PAIRS // 2, (half + 1) * PAIRS // 2))
                    dve.wait_ge(w_ready, half + 1)
                for half in range(2):
                    dve.wait_ge(k_copied, (half + 1) * PAIRS // 8 + 2)
                    part = slice(half * PAIRS, (half + 1) * PAIRS)
                    V.tensor_tensor(out=skip_term(part), in0=skip_term(part), in1=skip_eye[:, part], op=ALU.add).then_inc(k_ready, 1)
                    input_weights(slice(half * PAIRS // 2, (half + 1) * PAIRS // 2))

            @block.tensor
            def _(pe):
                pe.sem_inc(k_made, 2)
                for half in range(2):
                    pe.wait_ge(w_ready, half + 1)
                    with pe.Fori(half * PAIRS // 16, (half + 1) * PAIRS // 16) as r:
                        for j in range(2):
                            m = 2 * r + j
                            pe.wait_ge(b_ready, m + 1)
                            pe.wait_ge(k_copied, m + 1)
                            for i in range(4):
                                for g in range(2):
                                    for h in range(2):
                                        last = nc.tensor.matmul(k_psum[:, j, 2 * i + g, :], b_apart[:, j, i, g, h, :],
                                                                out_w[:, bass.ds(m * 4 + i, 1), h, 0:Q * S5_CH],
                                                                start=h == 0, stop=h == 1)
                            last.then_inc(k_made, 1)

        state = sb("state", [P, PAIRS, 2, CHUNKS])

        with ExitStack() as c2:
            sb2 = cur(c2)
            u_pair = sb2("u_pair", [P, 2, 2, Q, S5_CH])
            u_rest = sb2("u_rest", [CH_REST, 2, 2, Q, S5_CH])
            in_pair = sb2("in_pair", [P, 2, 2, P])
            u_t = sb2("u_t", [P, 2, 2, CHUNKS])
            in_t = sb2("in_t", [P, 2, 2, P])
            ps = lambda n: c2.enter_context(nc.psum_tensor("s5p_" + n, [P, 2, 512], F32))
            u_psum, in_psum, v_psum, y_psum = ps("u_psum"), ps("in_psum"), ps("v_psum"), ps("y_psum")
            two = lambda t, n: t[:, 0:2 * n].rearrange("p (g n) -> p g n", g=2)
            u_picked, in_picked, rest_in = sem("u_picked"), sem("in_picked"), [sem("rest_in_even"), sem("rest_in_odd")]
            u_turned, in_turned, u_t_ready, in_t_ready = sem("u_turned"), sem("in_turned"), sem("u_t_ready"), sem("in_t_ready")
            v_made, v_kept, y_made, y_kept = sem("v_made"), sem("v_kept"), sem("y_made"), sem("y_kept")
            block = c2.enter_context(nc.Block())
            rest_rows = D["u"][SEQ:SEQ + REST, :].rearrange("(k s) c -> k s c", s=Q)

            @block.sync
            def _(sp):
                with sp.Fori(0, PAIRS // 2) as r2:
                    for j in range(2):
                        r = 2 * r2 + j
                        sp.wait_ge(u_turned, r + 1)
                        for g in range(2):
                            sp.dma_start(u_rest[:, j, g], rest_rows[:, :, bass.ds(r * G2 + g * S5_CH, S5_CH)]).then_inc(rest_in[j], 16)

            @block.gpsimd
            def _(pool):
                pool.wait_ge(u_in, 16)
                with pool.Fori(0, PAIRS // 2) as r2:
                    for j in range(2):
                        r = 2 * r2 + j
                        pool.wait_ge(u_turned, r + 1)
                        for g in range(2):
                            last = nc.gpsimd.tensor_copy(u_pair[:, j, g, :, :], u[:, :, bass.ds(r * G2 + g * S5_CH, S5_CH)])
                        last.then_inc(u_picked, 1)
                        pool.wait_ge(in_turned, r + 1)
                        nc.gpsimd.tensor_copy(in_pair[:, j].unsqueeze(1), in_w[:, bass.ds(r, 1), :, :]).then_inc(in_picked, 1)

            @block.tensor
            def _(pe):
                pe.sem_inc(u_turned, 2)
                pe.sem_inc(in_turned, 2)
                pe.sem_inc(y_made, 2)
                with pe.Fori(0, PAIRS // 2) as r2:
                    for j in range(2):
                        r = 2 * r2 + j
                        pe.wait_ge(u_picked, r + 1)
                        pe.wait_ge(rest_in[j], 32 * r2 + 32)
                        pe.wait_ge(u_t_ready, r + 1)
                        for g in range(2):
                            nc.tensor.transpose(u_psum[:, j, g * P:(g + 1) * P], u_pair[:, j, g].rearrange("p s c -> p (s c)"), ident[:])
                            last = nc.tensor.transpose(u_psum[:, j, 2 * P + g * CH_REST:2 * P + (g + 1) * CH_REST],
                                                       u_rest[:, j, g].rearrange("p s c -> p (s c)"), ident[0:CH_REST, 0:CH_REST])
                        last.then_inc(u_turned, 1)
                        pe.wait_ge(in_picked, r + 1)
                        pe.wait_ge(in_t_ready, r + 1)
                        for h in range(2):
                            last = nc.tensor.transpose(in_psum[:, j, h * P:(h + 1) * P], in_pair[:, j, h, :], ident[:])
                        last.then_inc(in_turned, 1)
                        pe.wait_ge(u_t_ready, r + 3)
                        pe.wait_ge(y_kept, r + 1)
                        for g in range(2):
                            last = nc.tensor.matmul(two(y_psum[:, j], P)[:, g, :], u_t[:, j, g, CH_REST:],
                                                    toep[:, bass.ds(r * 2 + g, 1), :], start=True, stop=True)
                        last.then_inc(y_made, 1)
                        pe.wait_ge(in_t_ready, r + 3)
                        pe.wait_ge(v_kept, r + 1)
                        for h in range(2):
                            for g in range(2):
                                last = nc.tensor.matmul(two(v_psum[g * 64:g * 64 + 64, j], CHUNKS)[:, h, :], in_t[:, j, h, g * 64:g * 64 + 64],
                                                        u_t[:, j, g, :], start=True, stop=True)
                        last.then_inc(v_made, 1)

            @block.scalar
            def _(act):
                act.sem_inc(u_t_ready, 2)
                act.sem_inc(y_kept, 2)
                with act.Fori(0, PAIRS // 2) as r2:
                    for j in range(2):
                        r = 2 * r2 + j
                        act.wait_ge(u_turned, r + 3)
                        act.wait_ge(v_made, r + 1)
                        nc.scalar.activation(u_t[:, j, :, CH_REST:], two(u_psum[:, j], P), ACT.Copy)
                        nc.scalar.activation(u_t[:, j, :, 0:CH_REST], two(u_psum[:, j, 2 * P:], CH_REST), ACT.Copy).then_inc(u_t_ready, 1)
                        act.wait_ge(y_made, r + 3)
                        for g in range(2):
                            last = nc.scalar.activation(u[:, :, bass.ds(r * G2 + g * S5_CH, S5_CH)],
                                                        two(y_psum[:, j], P)[:, g, :].rearrange("p (t c) -> p t c", c=S5_CH), ACT.Copy)
                        last.then_inc(y_kept, 1)

            @block.vector
            def _(dve):
                dve.sem_inc(in_t_ready, 2)
                dve.sem_inc(v_kept, 2)
                dve.sem_inc(v_made, 2)
                with dve.Fori(0, PAIRS // 2) as r2:
                    for j in range(2):
                        r = 2 * r2 + j
                        dve.wait_ge(in_turned, r + 3)
                        nc.vector.tensor_copy(in_t[:, j], two(in_psum[:, j], P)).then_inc(in_t_ready, 1)
                        dve.wait_ge(v_made, r + 3)
                        nc.vector.tensor_copy(state[:, bass.ds(r, 1), :, :], two(v_psum[:, j], CHUNKS).unsqueeze(1)).then_inc(v_kept, 1)

        rest_start = sb("rest_start", [P, PAIRS, 2, CH_REST])
        with ExitStack() as c2:
            sb2 = cur(c2)
            end = sb2("end", [P, PAIRS, 2, SEQS])
            last_prompt = sb2("last_prompt", [P, PAIRS, 2])
            t0 = sb2("t0", [P, PAIRS, 2, BLOCKS])
            t1 = sb2("t1", [P, PAIRS, 2, BLOCKS])
            h0_in, ends_ready, ends_out, sc_step = sem("h0_in"), sem("ends_ready"), sem("ends_out"), sem("sc_step")
            block = c2.enter_context(nc.Block())

            @block.sync
            def _(sp):
                sp.dma_start(rest_start[:, :, :, 0:SEQS], D["s5_h0"]).then_inc(h0_in, 16)
                sp.wait_ge(ends_ready, 1)
                sp.dma_start(D["s5_end_sample"], end[:]).then_inc(ends_out, 16)
                sp.dma_start(D["s5_end_prompt"], last_prompt[:]).then_inc(ends_out, 16)
                sp.wait_ge(ends_out, 32)

            @block.vector
            def _(dve):
                chain = Chain(dve, sc_step)
                V = nc.vector
                tt = lambda o, a, b, op: chain.link(V.tensor_tensor(out=o, in0=a, in1=b, op=op))

                def advance(dst, src, j, n, out=None):
                    a, b = t0[:, :, :, 0:n], t1[:, :, :, 0:n]
                    tab = lambda c: jump[:, j, c, :].unsqueeze(2).to_broadcast([P, PAIRS, n])
                    for h in range(2):
                        V.tensor_tensor(out=b[:, :, h], in0=src[:, :, 1 - h], in1=tab(2 * h), op=ALU.mult)
                        last = V.tensor_tensor(out=a[:, :, h], in0=src[:, :, h], in1=tab(1), op=ALU.mult)
                    chain.link(last)
                    tt(a, a, b, ALU.add)
                    tt(dst if out is None else out, dst, a, ALU.add)

                prompt = state[:, :, :, SEQS:].rearrange("p g h (b j) -> p g h b j", j=SCAN)
                for j in range(1, SCAN):
                    advance(prompt[:, :, :, :, j], prompt[:, :, :, :, j - 1], 0, BLOCKS)
                for b in range(1, BLOCKS):
                    advance(prompt[:, :, :, b:b + 1, SCAN - 1], prompt[:, :, :, b - 1:b, SCAN - 1], SCAN - 1, 1)
                for j in range(SCAN - 1):
                    advance(prompt[:, :, :, 1:, j], prompt[:, :, :, :BLOCKS - 1, SCAN - 1], j, BLOCKS - 1)
                dve.wait_ge(h0_in, 16)
                advance(state[:, :, :, 0:SEQS], rest_start[:, :, :, 0:SEQS], 0, SEQS, out=end[:])
                chain.link(V.tensor_copy(last_prompt[:], state[:, :, :, CHUNKS - 1]))
                chain.link(V.memset(rest_start[:, :, :, SEQS], 0.0))
                V.tensor_copy(rest_start[:, :, :, SEQS + 1], state[:, :, :, SEQS]).then_inc(ends_ready, 1)

        with ExitStack() as c2:
            sb2 = cur(c2)
            start = sb2("start", [P, 2, 2, 2, CHUNKS])
            u_rest = sb2("u_rest2", [P, 2, P])
            u_t = sb2("u_t2", [P, 2, P])
            rest = in_w[0:CH_REST].rearrange("k p g n -> k (p g) n")
            ps = lambda n, s: c2.enter_context(nc.psum_tensor("s5p_" + n, s, F32))
            u_psum = ps("u_psum2", [P, 2, P])
            y_psum, r_psum = ps("y_psum2", [P, 2, 512]), ps("r_psum", [P, 2, 512])
            pair_of = lambda t: t[:, 0:2 * P].rearrange("k (g n) -> k g n", g=2)
            rest_in, rest_picked, u_turned, u_t_ready = sem("rest_in2"), sem("rest_picked"), sem("u_turned2"), sem("u_t_ready2")
            zeroed, start_ready, y_made, y_kept, r_made, r_kept, r_out, y_out = (sem(n) for n in (
                "zeroed", "start_ready", "y_made2", "y_kept2", "r_made", "r_kept", "r_out", "y_out"))
            block = c2.enter_context(nc.Block())
            rest_u = D["u"][SEQ:SEQ + REST, :].rearrange("(k s) c -> k s c", s=Q)
            rest_y = D["y5"][SEQ:SEQ + REST, :].rearrange("(k s) c -> k s c", s=Q)

            @block.sync
            def _(sp):
                for s in range(Q):
                    sp.dma_start(rest[:, :, s * S5_CH:(s + 1) * S5_CH], rest_u[:, s, :].rearrange("k (g c) -> k g c", c=S5_CH)).then_inc(rest_in, 16)
                for n in range(4):
                    cols = slice(n * D_MODEL // 4, (n + 1) * D_MODEL // 4)
                    sp.wait_ge(y_kept, (n + 1) * PAIRS // 4 + 2)
                    sp.dma_start(D["y5"][0:SEQ, cols].rearrange("(k s) c -> k s c", s=Q), u[:, :, cols]).then_inc(y_out, 16)
                sp.wait_ge(r_kept, PAIRS + 2)
                for s in range(Q):
                    sp.dma_start(rest_y[:, s, :].rearrange("k (g c) -> k g c", c=S5_CH), rest[:, :, s * S5_CH:(s + 1) * S5_CH]).then_inc(r_out, 16)
                sp.wait_ge(r_out, 16 * Q)
                sp.wait_ge(y_out, 64)

            @block.gpsimd
            def _(pool):
                nc.gpsimd.memset(start[:], 0.0).then_inc(zeroed, 1)
                nc.gpsimd.memset(u_rest[:], 0.0).then_inc(zeroed, 1)
                pool.sem_inc(u_turned, 1)
                pool.wait_ge(rest_in, 16 * Q)
                pool.wait_ge(zeroed, 2)
                with pool.Fori(0, PAIRS // 2) as r2:
                    for j in range(2):
                        r = 2 * r2 + j
                        pool.wait_ge(u_turned, r + 1)
                        nc.gpsimd.tensor_copy(u_rest[0:CH_REST], rest[:, bass.ds(2 * r, 2), :]).then_inc(rest_picked, 1)
                        pool.wait_ge(r_made, r + 1)
                        for g in range(2):
                            rows = slice(g * 64, g * 64 + 64)
                            nc.gpsimd.tensor_copy(start[rows, j, g, :, 0:CH_REST].unsqueeze(1), rest_start[rows, bass.ds(r, 1), :, :])
                            last = nc.gpsimd.tensor_copy(start[rows, j, g, :, CH_REST:].unsqueeze(1),
                                                         state[rows, bass.ds(r, 1), :, CH_REST - 1:CHUNKS - 1])
                        last.then_inc(start_ready, 1)

            @block.scalar
            def _(act):
                act.sem_inc(u_t_ready, 1)
                act.sem_inc(r_kept, 2)
                with act.Fori(0, PAIRS // 2) as r2:
                    for j in range(2):
                        r = 2 * r2 + j
                        act.wait_ge(u_turned, r + 2)
                        nc.scalar.activation(u_t[:], u_psum[:], ACT.Copy).then_inc(u_t_ready, 1)
                        act.wait_ge(r_made, r + 3)
                        nc.scalar.activation(rest[:, bass.ds(2 * r, 2), :], pair_of(r_psum[0:CH_REST, j]), ACT.Copy).then_inc(r_kept, 1)

            @block.vector
            def _(dve):
                dve.sem_inc(y_kept, 2)
                with dve.Fori(0, PAIRS // 2) as r2:
                    for j in range(2):
                        r = 2 * r2 + j
                        dve.wait_ge(y_made, r + 1)
                        for g in range(2):
                            cols = u[:, :, bass.ds(r * G2 + g * S5_CH, S5_CH)]
                            more = pair_of(y_psum[:, j])[:, g, :].rearrange("p (t c) -> p t c", c=S5_CH)
                            last = nc.vector.tensor_tensor(out=cols, in0=cols, in1=more, op=ALU.add)
                        last.then_inc(y_kept, 1)

            @block.tensor
            def _(pe):
                pe.sem_inc(r_made, 2)
                with pe.Fori(0, PAIRS // 2) as r2:
                    for j in range(2):
                        r = 2 * r2 + j
                        pe.wait_ge(rest_picked, r + 1)
                        pe.wait_ge(u_t_ready, r + 1)
                        for g in range(2):
                            last = nc.tensor.transpose(u_psum[:, g, :], u_rest[:, g, :], ident[:])
                        last.then_inc(u_turned, 1)
                        pe.wait_ge(start_ready, r + 1)
                        pe.wait_ge(y_kept, r + 1)
                        for g in range(2):
                            for h in range(2):
                                last = nc.tensor.matmul(pair_of(y_psum[:, j])[:, g, :], start[:, j, g, h, CH_REST:],
                                                        out_w[:, bass.ds(r, 1), h, S5_CH:], start=h == 0, stop=h == 1)
                        last.then_inc(y_made, 1)
                        pe.wait_ge(r_kept, r + 1)
                        pe.wait_ge(u_t_ready, r + 2)
                        for g in range(2):
                            o = pair_of(r_psum[:, j])[:, g, :]
                            nc.tensor.matmul(o, u_t[:, g, :], toep[:, bass.ds(r * 2 + g, 1), :], start=True, stop=False)
                            for h in range(2):
                                last = nc.tensor.matmul(o, start[:, j, g, h, 0:P], out_w[:, bass.ds(r, 1), h, S5_CH:],
                                                        start=False, stop=h == 1)
                        last.then_inc(r_made, 1)


def mamba_scan(nc, D):
    SEGS = SEQS + 1
    with ExitStack() as ctx:
        sb = lambda n, s, d=F32: ctx.enter_context(nc.sbuf_tensor("m2s_" + n, s, d))
        sem = ctx.enter_context(stage_semaphores(nc, "m2_"))
        ident = sb("ident", [P, P])
        after = sb("after", [P, P])
        upto = sb("upto", [P, P])
        ones = sb("ones", [P, P])
        after_seg = sb("after_seg", [P, P])
        upto_seg = sb("upto_seg", [P, P])
        in_seg = sb("in_seg", [P, SEGS, P])
        conv_w = sb("conv_w", [P, XB, TAPS])
        conv_b = sb("conv_b", [P, XB])
        head_par = sb("head_par", [P, 3, HEADS])
        a_neg = sb("a_neg", [P, HEADS])
        window = sb("window", [P, XB, P + TAPS - 1])
        conv = sb("conv", [P, XB, P])
        tap = sb("tap", [P, XB, P])
        xbc = sb("xbc", [P, XB, P])
        dt_raw = sb("dt_raw", [P, HEADS])
        small = sb("small", [P, 6, HEADS])
        dt = sb("dt", [P, HEADS])
        da = sb("da", [P, HEADS])
        e_acs = sb("e_acs", [P, HEADS])
        e_rev = sb("e_rev", [P, HEADS])
        e_tot = sb("e_tot", [P, HEADS])
        x_tok = sb("x_tok", [P, HEADS, HD])
        b_tok = sb("b_tok", [P, 2, NS])
        x_dt = sb("x_dt", [P, HEADS, HD])
        x_w = sb("x_w", [P, HEADS, HD])
        x_skip = sb("x_skip", [P, HEADS, HD])
        da_upto = sb("da_upto", [P, HEADS, P])
        decay = sb("decay", [P, HEADS, P])
        cb_masked = sb("cb_masked", [P, 2, P])
        y = sb("y", [P, HEADS, HD])
        state = sb("state", [P, HEADS, HD])
        ps_a = ctx.enter_context(nc.psum_tensor("m2p_a", [P, 4, 512], F32))
        ps_b = ctx.enter_context(nc.psum_tensor("m2p_b", [P, 3, 512], F32))
        ps_c = ctx.enter_context(nc.psum_tensor("m2p_c", [P, 512], F32))
        CB = 256

        consts_in, tile_in, conv_done, xbc_ready = sem("consts_in"), sem("tile_in"), sem("conv_done"), sem("xbc_ready")
        turned, tok_ready, b_ready = sem("turned"), sem("tok_ready"), sem("b_ready")
        abs_ready, soft_ready, dt_ready, a_ready = sem("abs_ready"), sem("soft_ready"), sem("dt_ready"), sem("a_ready")
        upto_ready, sums_made, sums_ready = sem("upto_ready"), sem("sums_made"), sem("sums_ready")
        seg_made, decay_ready, w_ready = sem("seg_made"), sem("decay_ready"), sem("w_ready")
        xw_ready, skip_ready, y_made, y_ready, st_made = sem("xw_ready"), sem("skip_ready"), sem("y_made"), sem("y_ready"), sem("st_made")
        state_ready, y_out, dve_step, act_step = sem("state_ready"), sem("y_out"), sem("dve_step"), sem("act_step")
        heads = lambda t: t.unsqueeze(2).to_broadcast([P, HEADS, HD])
        tt = lambda e, o, a, b, op: e.tensor_tensor(out=o, in0=a, in1=b, op=op)

        def dve_conv(dve, chain, k, views, taps=range(TAPS)):
            V = nc.vector
            if taps[0] == 0:
                dve.wait_ge(tile_in, 32 * k + 32)
                dve.wait_ge(xbc_ready, k + 1)
            for w_in, o in views:
                dims = list(o(conv).shape)
                wt = lambda j: (conv_w[:, :, j].unsqueeze(2).to_broadcast(dims) if len(dims) == 3 else
                                conv_w[:, :, j].unsqueeze(2).unsqueeze(3).to_broadcast(dims))
                bias = (conv_b[:].unsqueeze(2).to_broadcast(dims) if len(dims) == 3 else
                        conv_b[:].unsqueeze(2).unsqueeze(3).to_broadcast(dims))
                for j in taps:
                    chain.link(tt(V, o(tap) if j else o(conv), w_in(j), wt(j), ALU.mult))
                    if j:
                        chain.link(tt(V, o(conv), o(conv), o(tap), ALU.add))
                if taps[-1] == TAPS - 1:
                    chain.link(tt(V, o(conv), o(conv), bias, ALU.add))
            if taps[-1] == TAPS - 1:
                dve.sem_inc(conv_done, 1)

        def dve_dt(dve, chain, k):
            V = nc.vector
            chain.link(tt(V, small[:, 0, :], dt_raw[:], head_par[:, 0, :], ALU.add))
            chain.link(V.tensor_scalar(small[:, 1, :], small[:, 0, :], -1.0, None, ALU.mult))
            tt(V, small[:, 1, :], small[:, 0, :], small[:, 1, :], ALU.max).then_inc(abs_ready, 1)

        def dve_da(dve, chain, k):
            V = nc.vector
            chain.link(V.tensor_scalar(small[:, 4, :], small[:, 0, :], 0.0, None, ALU.max))
            dve.wait_ge(soft_ready, k + 1)
            chain.link(tt(V, dt[:], small[:, 4, :], small[:, 3, :], ALU.add))
            tt(V, da[:], dt[:], a_neg[:], ALU.mult).then_inc(dt_ready, 1)

        def dve_tokens(dve, chain, k):
            V = nc.vector
            dve.wait_ge(turned, k + 1)
            chain.link(V.tensor_copy(x_tok[:], ps_b[:, 0:2, :].rearrange("p b (h d) -> p (b h) d", d=HD)))
            dve.sem_inc(tok_ready, 1)
            chain.link(tt(V, x_dt[:], x_tok[:], heads(dt[:]), ALU.mult))

        def dve_decays(dve, chain, k, cb_mask):
            V = nc.vector
            dve.wait_ge(sums_ready, k + 2)
            chain.link(tt(V, cb_masked[:], ps_c[:, CB:CB + 2 * P].rearrange("p (g l) -> p g l", g=2),
                          cb_mask.unsqueeze(1).to_broadcast([P, 2, P]), ALU.mult))
            dve.wait_ge(decay_ready, k + 1)
            for g in range(2):
                part = decay[:, g * HPG:(g + 1) * HPG, :]
                last = tt(V, part, part, cb_masked[:, g, :].unsqueeze(1).to_broadcast([P, HPG, P]), ALU.mult)
            last.then_inc(w_ready, 1)
            tt(V, x_w[:], x_dt[:], heads(e_rev[:]), ALU.mult).then_inc(xw_ready, 1)

        def dve_y(dve, chain, k):
            V = nc.vector
            dve.wait_ge(y_made, k + 1)
            dve.wait_ge(y_out, 16 * k + 16)
            chain.link(tt(V, y[:], ps_a[:, 2:4, :].rearrange("p b (h d) -> p (b h) d", d=HD), heads(e_acs[:]), ALU.mult))
            chain.link(tt(V, y[:], y[:], ps_a[:, 0:2, :].rearrange("p b (h d) -> p (b h) d", d=HD), ALU.add))
            dve.wait_ge(skip_ready, k + 1)
            tt(V, y[:], y[:], x_skip[:], ALU.add).then_inc(y_ready, 1)

        def pool_tile(pool, k, mask):
            G = nc.gpsimd
            pool.wait_ge(dt_ready, k + 1)
            pool.wait_ge(seg_made, k + 1)
            tt(G, da_upto[:], da[:].unsqueeze(2).to_broadcast([P, HEADS, P]),
               mask.unsqueeze(1).to_broadcast([P, HEADS, P]), ALU.mult).then_inc(upto_ready, 1)
            pool.wait_ge(tok_ready, k + 1)
            pool.wait_ge(y_ready, k + 1)
            tt(G, x_skip[:], x_tok[:], heads(head_par[:, 2, :]), ALU.mult).then_inc(skip_ready, 1)

        def pe_front(pe, k, m_after, m_upto):
            T = nc.tensor
            pe.wait_ge(xbc_ready, k + 2)
            pe.wait_ge(state_ready, k + 1)
            pe.wait_ge(b_ready, k + 1)
            for c in range(10):
                last = T.transpose(ps_b[:, c // 4, (c % 4) * P:(c % 4 + 1) * P], xbc[:, c, :], ident[:])
            last.then_inc(turned, 1)
            pe.wait_ge(dt_ready, k + 1)
            pe.wait_ge(sums_ready, k + 1)
            pe.wait_ge(w_ready, k + 1)
            for n, m in enumerate((m_upto, m_after, ones)):
                T.matmul(ps_c[:, n * HEADS:(n + 1) * HEADS], m[:], da[:], start=True, stop=True)
            for g in range(2):
                last = T.matmul(ps_c[:, CB + g * P:CB + (g + 1) * P], xbc[:, 8 + g, :], xbc[:, 10 + g, :], start=True, stop=True)
            last.then_inc(sums_made, 1)
            pe.wait_ge(upto_ready, k + 1)
            pe.wait_ge(y_ready, k + 1)
            for n in range(4):
                last = T.matmul(ps_a[:, n, :], m_after[:], da_upto[:, 4 * n:4 * n + 4, :].rearrange("p h l -> p (h l)"), start=True, stop=True)
            last.then_inc(seg_made, 1)

        def pe_inside(pe, k):
            pe.wait_ge(w_ready, k + 2)
            for h in range(HEADS):
                last = nc.tensor.matmul(ps_a[:, h // HPG, (h % HPG) * HD:(h % HPG + 1) * HD], decay[:, h, :], x_dt[:, h, :],
                                        start=True, stop=True)
            return last

        rest_steps = []

        with ExitStack() as c2:
            sb2 = lambda n, s, d=F32: c2.enter_context(nc.sbuf_tensor("m2r_" + n, s, d))
            sem2 = c2.enter_context(stage_semaphores(nc, "m2r_"))
            win_s = sb2("win_s", [P, XB, SEQS, STEPS + TAPS - 1])
            win_m = sb2("win_m", [P, XB, N_META + TAPS - 1])
            tail = sb2("tail", [P, XB, SEQS, TAPS - 1])
            start = sb2("start", [P, SEQS, HEADS, HD])
            c_apart = sb2("c_apart", [P, 2, SEQS, P])
            b_seg = sb2("b_seg", [P, 2, 2, NS])
            e_seg = sb2("e_seg", [P, SEGS, HEADS])
            xbc_raw_in, zeroed, c_ready, start_in, tail_ready, tail_out = (sem2(n) for n in (
                "xbc_raw_in", "zeroed", "c_ready", "start_in", "tail_ready", "tail_out"))
            seg_sum_made, seg_sum_ready, b_seg_ready, seg_state_made, seg_state_ready, ends_out = (sem2(n) for n in (
                "seg_sum_made", "seg_sum_ready", "b_seg_ready", "seg_state_made", "seg_state_ready", "ends_out"))
            block = c2.enter_context(nc.Block())

            @block.sync
            def _(sp):
                for t, n in ((ident, "ident"), (after, "after"), (upto, "upto"), (ones, "ones"), (after_seg, "after_seg"),
                             (upto_seg, "upto_seg"), (in_seg, "in_seg"), (conv_w, "conv_w"), (conv_b, "conv_b"), (head_par, "head_par")):
                    sp.dma_start(t[:], D[n]).then_inc(consts_in, 16)
                rest = SEQ + N_META
                sp.dma_start(tail[:], D["conv_past"]).then_inc(xbc_raw_in, 16)
                sp.dma_start(window[:, :, 0:SAMPLE], D["xbc"][:, :, rest:rest + SAMPLE]).then_inc(xbc_raw_in, 16)
                sp.wait_ge(zeroed, 1)
                sp.dma_start(win_m[:, :, TAPS - 1:], D["xbc"][:, :, 0:N_META]).then_inc(tile_in, 16)
                sp.dma_start(dt_raw[:], D["dt"][SEQ:ROWS, :]).then_inc(tile_in, 16)
                sp.dma_start(start[:], D["ssm_h0"]).then_inc(start_in, 16)
                sp.wait_ge(tail_ready, 1)
                sp.dma_start(D["conv_end_sample"], tail[:]).then_inc(tail_out, 16)
                sp.wait_ge(y_ready, 2)
                sp.dma_start(D["ym"][SEQ:ROWS, :], y[:].rearrange("p h d -> p (h d)")).then_inc(y_out, 16)
                sp.wait_ge(seg_state_ready, SEQS)
                sp.dma_start(D["ssm_end_sample"], start[:]).then_inc(ends_out, 16)
                sp.wait_ge(ends_out, 16)
                sp.wait_ge(tail_out, 16)
                sp.wait_ge(y_out, 32)

            @block.gpsimd
            def _(pool):
                G = nc.gpsimd
                G.memset(win_m[:, :, 0:TAPS - 1], 0.0).then_inc(zeroed, 1)
                G.memset(conv[:], 0.0).then_inc(zeroed, 1)
                G.memset(c_apart[:], 0.0).then_inc(zeroed, 1)
                pool.sem_inc(seg_made, 1)
                pool.sem_inc(y_ready, 1)
                pool_tile(pool, 0, upto_seg[:])

            @block.scalar
            def _(act):
                act.wait_ge(consts_in, 160)
                act.sem_inc(xbc_ready, 1)
                act.sem_inc(b_ready, 1)
                act.sem_inc(sums_ready, 1)
                nc.scalar.activation(small[:, 5, :], head_par[:, 1, :], ACT.Exp).then_inc(a_ready, 1)
                act.wait_ge(conv_done, 1)
                nc.scalar.activation(xbc[:], conv[:], ACT.Silu).then_inc(xbc_ready, 1)
                act.wait_ge(abs_ready, 1)
                nc.scalar.activation(small[:, 2, :], small[:, 1, :], ACT.Exp, scale=-1.0).then_inc(act_step, 1)
                act.wait_ge(act_step, 1)
                nc.scalar.activation(small[:, 3, :], small[:, 2, :], ACT.Ln, bias=ones[:, 0:1]).then_inc(soft_ready, 1)
                act.wait_ge(turned, 1)
                nc.scalar.activation(b_tok[:], ps_b[:, 2, 0:2 * NS].rearrange("p (g n) -> p g n", g=2), ACT.Copy).then_inc(b_ready, 1)
                act.wait_ge(sums_made, 1)
                nc.scalar.activation(e_acs[:], ps_c[:, 0:HEADS], ACT.Exp)
                nc.scalar.activation(e_rev[:], ps_c[:, HEADS:2 * HEADS], ACT.Exp).then_inc(sums_ready, 1)
                act.wait_ge(seg_made, 2)
                nc.scalar.activation(decay[:], ps_a[:].rearrange("p b (h l) -> p (b h) l", l=P), ACT.Exp).then_inc(decay_ready, 1)
                act.wait_ge(seg_sum_made, 1)
                nc.scalar.activation(e_seg[:], ps_c[:, 0:SEGS * HEADS].rearrange("p (b h) -> p b h", h=HEADS), ACT.Exp).then_inc(seg_sum_ready, 1)
                act.wait_ge(b_ready, 2)
                for b in range(SEGS):
                    if b >= 2:
                        act.wait_ge(seg_state_made, b - 1)
                    nc.scalar.activation(b_seg[:, b % 2], b_tok[:], ACT.Copy, scale=in_seg[:, b, 0:1]).then_inc(b_seg_ready, 1)

            @block.vector
            def _(dve):
                V = nc.vector
                chain = Chain(dve, dve_step)
                dve.sem_inc(y_out, 16)
                dve.sem_inc(w_ready, 1)
                dve.sem_inc(state_ready, 1)
                dve.wait_ge(a_ready, 1)
                chain.link(V.tensor_scalar(a_neg[:], small[:, 5, :], -1.0, None, ALU.mult))
                dve.wait_ge(xbc_raw_in, 32)
                chain.link(V.tensor_copy(win_s[:, :, :, 0:TAPS - 1], tail[:]))
                chain.link(V.tensor_copy(win_s[:, :, :, TAPS - 1:], window[:, :, 0:SAMPLE].rearrange("p x (b t) -> p x b t", b=SEQS)))
                V.tensor_copy(tail[:], win_s[:, :, :, STEPS:]).then_inc(tail_ready, 1)
                dve.wait_ge(zeroed, 3)
                dve_conv(dve, chain, 0, [
                    (lambda j: win_s[:, :, :, j:j + STEPS], lambda t: t[:, :, 0:SAMPLE].rearrange("p x (b t) -> p x b t", b=SEQS)),
                    (lambda j: win_m[:, :, j:j + N_META], lambda t: t[:, :, SAMPLE:REST])])
                dve_dt(dve, chain, 0)
                dve_da(dve, chain, 0)
                dve.wait_ge(xbc_ready, 2)
                for g in range(2):
                    c = c_apart[:, g]
                    diag = bass.AP(tensor=c.tensor, offset=c.offset, ap=[list(c.ap[0]), [P + STEPS, SEQS], [1, STEPS]])
                    last = V.tensor_copy(diag, xbc[:, 10 + g, 0:SAMPLE].rearrange("p (b t) -> p b t", b=SEQS))
                last.then_inc(c_ready, 1)
                dve_tokens(dve, chain, 0)
                dve_decays(dve, chain, 0, upto_seg[:])
                dve.wait_ge(xw_ready, 1)
                dve_y(dve, chain, 0)
                dve.wait_ge(seg_sum_ready, 1)
                dve.wait_ge(start_in, 16)
                for b in range(SEGS):
                    e = e_seg[:, b, :].unsqueeze(2).to_broadcast([P, HEADS, HD])
                    new = (ps_a if b % 2 else ps_b)[:, 0:2, :].rearrange("p b (h d) -> p (b h) d", d=HD)
                    if b < SEQS:
                        chain.link(tt(V, start[:, b], start[:, b], e, ALU.mult))
                        dve.wait_ge(seg_state_made, b + 1)
                        tt(V, start[:, b], start[:, b], new, ALU.add).then_inc(seg_state_ready, 1)
                    else:
                        dve.wait_ge(seg_state_made, b + 1)
                        V.tensor_copy(state[:], new).then_inc(state_ready, 1)
                rest_steps.append(chain.n)

            @block.tensor
            def _(pe):
                T = nc.tensor
                pe.wait_ge(consts_in, 160)
                pe_front(pe, 0, after_seg, upto_seg)
                last = pe_inside(pe, 0)
                pe.wait_ge(c_ready, 1)
                pe.wait_ge(start_in, 16)
                for g in range(2):
                    for b in range(SEQS):
                        last = T.matmul(ps_a[:, 2 + g, :], c_apart[:, g, b, :], start[:, b, g * HPG:(g + 1) * HPG, :].rearrange("p h d -> p (h d)"),
                                        start=b == 0, stop=b == SEQS - 1)
                last.then_inc(y_made, 1)
                pe.wait_ge(sums_ready, 2)
                pe.wait_ge(w_ready, 2)
                for b in range(SEGS):
                    last = T.matmul(ps_c[:, b * HEADS:(b + 1) * HEADS], in_seg[:, b, :], da[:], start=True, stop=True)
                last.then_inc(seg_sum_made, 1)
                pe.wait_ge(xw_ready, 1)
                pe.wait_ge(y_ready, 2)
                for b in range(SEGS):
                    pe.wait_ge(b_seg_ready, b + 1)
                    if b >= 2:
                        pe.wait_ge(seg_state_ready, b - 1)
                    for g in range(2):
                        last = T.matmul((ps_a if b % 2 else ps_b)[:, g, :], b_seg[:, b % 2, g, :],
                                        x_w[:, g * HPG:(g + 1) * HPG, :].rearrange("p h d -> p (h d)"), start=True, stop=True)
                    last.then_inc(seg_state_made, 1)

        with ExitStack() as c2:
            conv_tail = c2.enter_context(nc.sbuf_tensor("m2m_conv_tail", [P, XB, TAPS - 1], F32))
            prompt_out, tail_ready, window_free = sem("prompt_out"), sem("tail_ready"), sem("window_free")
            block = c2.enter_context(nc.Block())

            @block.sync
            def _(sp):
                def load(i):
                    sp.dma_start(window[:], D["xbc"][:, :, bass.ds(i * P + N_META - TAPS + 1, P + TAPS - 1)]).then_inc(tile_in, 16)
                    sp.dma_start(dt_raw[:], D["dt"][bass.ds(i * P, P), :]).then_inc(tile_in, 16)

                def store(i):
                    sp.wait_ge(y_ready, i + 3)
                    sp.dma_start(D["ym"][bass.ds(i * P, P), :], y[:].rearrange("p h d -> p (h d)")).then_inc(y_out, 16)

                load(0)
                with sp.Fori(0, MAIN_TILES - 1) as i:
                    sp.wait_ge(window_free, i + 1)
                    load(i + 1)
                    store(i)
                store(MAIN_TILES - 1)
                sp.wait_ge(state_ready, MAIN_TILES + 2)
                sp.dma_start(D["ssm_end_prompt"], state[:]).then_inc(prompt_out, 16)
                sp.wait_ge(tail_ready, 1)
                sp.dma_start(D["conv_end_prompt"], conv_tail[:]).then_inc(prompt_out, 16)
                sp.wait_ge(prompt_out, 32)
                sp.wait_ge(y_out, 16 * (MAIN_TILES + 2))

            @block.gpsimd
            def _(pool):
                with pool.Fori(1, TILES) as k:
                    pool_tile(pool, k, upto[:])

            @block.scalar
            def _(act):
                def soft(k):
                    act.wait_ge(abs_ready, k + 1)
                    nc.scalar.activation(small[:, 2, :], small[:, 1, :], ACT.Exp, scale=-1.0).then_inc(act_step, 1)
                    act.wait_ge(act_step, k + 1)
                    nc.scalar.activation(small[:, 3, :], small[:, 2, :], ACT.Ln, bias=ones[:, 0:1]).then_inc(soft_ready, 1)

                def silu(k):
                    act.wait_ge(conv_done, k + 1)
                    act.wait_ge(y_made, k)
                    nc.scalar.activation(xbc[:], conv[:], ACT.Silu).then_inc(xbc_ready, 1)

                def tile(k, more):
                    act.wait_ge(turned, k + 1)
                    nc.scalar.activation(b_tok[:], ps_b[:, 2, 0:2 * NS].rearrange("p (g n) -> p g n", g=2), ACT.Copy).then_inc(b_ready, 1)
                    act.wait_ge(sums_made, k + 1)
                    act.wait_ge(y_ready, k + 1)
                    nc.scalar.activation(e_acs[:], ps_c[:, 0:HEADS], ACT.Exp)
                    nc.scalar.activation(e_rev[:], ps_c[:, HEADS:2 * HEADS], ACT.Exp)
                    nc.scalar.activation(e_tot[:], ps_c[:, 2 * HEADS:3 * HEADS], ACT.Exp).then_inc(sums_ready, 1)
                    act.wait_ge(seg_made, k + 2)
                    nc.scalar.activation(decay[:], ps_a[:].rearrange("p b (h l) -> p (b h) l", l=P), ACT.Exp).then_inc(decay_ready, 1)
                    if more:
                        soft(k + 1)
                        silu(k + 1)

                soft(1)
                silu(1)
                with act.Fori(1, MAIN_TILES) as k:
                    tile(k, True)
                tile(MAIN_TILES, False)

            @block.vector
            def _(dve):
                V = nc.vector
                chain = Chain(dve, dve_step)
                STEPS_PER = 19
                begin = rest_steps[0]
                tail_cols = slice(P, P + TAPS - 1)

                views = [(lambda j: window[:, :, j:j + P], lambda t: t[:])]

                def first_taps(k):
                    dve_conv(dve, chain, k, views, range(TAPS - 1))
                    dve_dt(dve, chain, k)

                def last_tap(k):
                    dve_conv(dve, chain, k, views, range(TAPS - 1, TAPS))
                    chain.link(V.tensor_copy(conv_tail[:], window[:, :, tail_cols]))
                    dve.sem_inc(window_free, 1)

                def tile(k, more):
                    chain.start(front + (k - 1) * STEPS_PER)
                    dve_tokens(dve, chain, k)
                    if more:
                        first_taps(k + 1)
                    dve_decays(dve, chain, k, upto[:])
                    if more:
                        last_tap(k + 1)
                        dve_da(dve, chain, k + 1)
                    dve.wait_ge(y_made, k + 1)
                    chain.link(tt(V, state[:], state[:], heads(e_tot[:]), ALU.mult))
                    dve.wait_ge(st_made, k)
                    tt(V, state[:], state[:], ps_b[:, 0:2, :].rearrange("p b (h d) -> p (b h) d", d=HD), ALU.add).then_inc(state_ready, 1)
                    dve_y(dve, chain, k)
                    assert chain.n == STEPS_PER or not more, chain.n

                chain.start(begin)
                first_taps(1)
                last_tap(1)
                dve_da(dve, chain, 1)
                front = begin + chain.n
                with dve.Fori(1, MAIN_TILES) as k:
                    tile(k, True)
                tile(MAIN_TILES, False)
                dve.wait_ge(state_ready, TILES + 1)
                dve.sem_inc(tail_ready, 1)

            @block.tensor
            def _(pe):
                T = nc.tensor
                with pe.Fori(1, TILES) as k:
                    pe_front(pe, k, after, upto)
                    last = pe_inside(pe, k)
                    for g in range(2):
                        last = T.matmul(ps_a[:, 2 + g, :], xbc[:, 10 + g, :], state[:, g * HPG:(g + 1) * HPG, :].rearrange("p h d -> p (h d)"),
                                        start=True, stop=True)
                    last.then_inc(y_made, 1)
                    pe.wait_ge(xw_ready, k + 1)
                    pe.wait_ge(b_ready, k + 2)
                    for g in range(2):
                        last = T.matmul(ps_b[:, g, :], b_tok[:, g, :], x_w[:, g * HPG:(g + 1) * HPG, :].rearrange("p h d -> p (h d)"),
                                        start=True, stop=True)
                    last.then_inc(st_made, 1)


def mix_out(nc, D):
    with ExitStack() as ctx:
        sb = lambda n, s, d=F32: ctx.enter_context(nc.sbuf_tensor("mo_" + n, s, d))
        sem = ctx.enter_context(stage_semaphores(nc, "mo_"))
        ident = sb("ident", [P, P])
        w_glu = sb("w_glu", [P, KT, D_MODEL])
        w_out = sb("w_out", [P, 2 * KT, D_MODEL])
        norm_w = sb("norm_w", [P, 2 * KT])
        eps = sb("eps", [P, 1])
        y5 = sb("y5", [P, D_MODEL])
        z = sb("z", [P, D_MODEL])
        ym = sb("ym", [P, D_MODEL])
        x = sb("x", [P, D_MODEL])
        g = sb("g", [P, D_MODEL])
        g_t = sb("g_t", [P, KT, P])
        sig = sb("sig", [P, D_MODEL])
        z_silu = sb("z_silu", [P, D_MODEL])
        square = sb("square", [P, D_MODEL])
        s5_n = sb("s5_n", [P, D_MODEL])
        m2_n = sb("m2_n", [P, D_MODEL])
        both_t = sb("both_t", [P, 2 * KT, P])
        x_mid = sb("x_mid", [P, D_MODEL])
        stat = sb("stat", [P, 3, 3])
        ps = lambda n: ctx.enter_context(nc.psum_tensor("mo_" + n, [P, KT, P], F32))
        ps_s5, ps_m2, ps_glu, ps_out = ps("ps_s5"), ps("ps_m2"), ps("ps_glu"), ps("ps_out")
        glu_in, out_in, consts_in, y_in, x_in, eps_set = (sem(n) for n in ("glu_in", "out_in", "consts_in", "y_in", "x_in", "eps_set"))
        g_ready, z_ready, m2_gated, m2_summed, m2_root = (sem(n) for n in ("g_ready", "z_ready", "m2_gated", "m2_summed", "m2_root"))
        sig_ready, s5_gated, s5_summed, s5_root = (sem(n) for n in ("sig_ready", "s5_gated", "s5_summed", "s5_root"))
        g_turned, g_t_ready, m2_n_ready, m2_turned, m2_t_ready = (sem(n) for n in ("g_turned", "g_t_ready", "m2_n_ready", "m2_turned", "m2_t_ready"))
        glu_made, s5_n_ready, s5_turned, s5_t_ready = (sem(n) for n in ("glu_made", "s5_n_ready", "s5_turned", "s5_t_ready"))
        out_made, x_mid_ready, x_mid_out, dve_step = (sem(n) for n in ("out_made", "x_mid_ready", "x_mid_out", "dve_step"))
        flat = lambda t: t[:].rearrange("p b c -> p (b c)")
        block = ctx.enter_context(nc.Block())

        @block.sync
        def _(sp):
            def load_y(k):
                for t, n in ((y5, "y5"), (z, "z"), (ym, "ym")):
                    sp.dma_start(t[:], D[n][bass.ds(k * P, P), :]).then_inc(y_in, 16)

            def store(k):
                sp.wait_ge(x_mid_ready, k + 2)
                sp.dma_start(D["x_mid"][bass.ds(k * P, P), :], x_mid[:]).then_inc(x_mid_out, 16)

            load_y(0)
            sp.dma_start(x[:], D["x_all"][0:P, :]).then_inc(x_in, 16)
            sp.dma_start(ident[:], D["ident"]).then_inc(consts_in, 16)
            sp.dma_start(norm_w[:], D["mix_norm_w"]).then_inc(consts_in, 16)
            sp.dma_start(w_glu[:], D["w_glu"]).then_inc(glu_in, 16)
            sp.dma_start(w_out[:], D["w_out"]).then_inc(out_in, 16)
            with sp.Fori(0, MAIN_TILES) as k:
                sp.wait_ge(m2_gated, k + 1)
                sp.wait_ge(g_ready, k + 1)
                load_y(k + 1)
                store(k)
                sp.dma_start(x[:], D["x_all"][bass.ds(k * P + P, P), :]).then_inc(x_in, 16)
            store(MAIN_TILES)
            sp.wait_ge(x_mid_out, 16 * (TILES + 1))

        @block.scalar
        def _(act):
            A = nc.scalar.activation
            act.sem_inc(sig_ready, 1)
            act.wait_ge(eps_set, 1)
            with act.Fori(0, TILES) as k:
                act.wait_ge(y_in, 48 * k + 48)
                act.wait_ge(s5_gated, k + 1)
                A(g[:], y5[:], ACT.Gelu_apprx_tanh).then_inc(g_ready, 1)
                A(z_silu[:], z[:], ACT.Silu).then_inc(z_ready, 1)
                act.wait_ge(m2_gated, k + 1)
                for h in range(2):
                    half = slice(h * 512, h * 512 + 512)
                    last = A(square[:, half], m2_n[:, half], ACT.Square, accum_out=stat[:, 0, 1 + h:2 + h])
                last.then_inc(m2_summed, 1)
                act.wait_ge(m2_summed, k + 1)
                A(stat[:, 1, 1:3], stat[:, 0, 1:3], ACT.Sqrt, bias=eps[:], scale=2.0 / D_MODEL).then_inc(m2_root, 1)
                act.wait_ge(g_turned, k + 1)
                A(g_t[:], ps_s5[:], ACT.Copy).then_inc(g_t_ready, 1)
                act.wait_ge(glu_made, k + 1)
                A(sig[:], flat(ps_glu), ACT.Sigmoid).then_inc(sig_ready, 1)
                act.wait_ge(s5_gated, k + 2)
                A(square[:], s5_n[:], ACT.Square, accum_out=stat[:, 0, 0:1]).then_inc(s5_summed, 1)
                act.wait_ge(s5_summed, k + 1)
                A(stat[:, 1, 0:1], stat[:, 0, 0:1], ACT.Sqrt, bias=eps[:], scale=1.0 / D_MODEL).then_inc(s5_root, 1)

        @block.vector
        def _(dve):
            V = nc.vector
            chain = Chain(dve, dve_step)
            STEPS_PER = 2
            dve.sem_inc(s5_gated, 1)
            dve.sem_inc(x_mid_out, 16)
            dve.sem_inc(x_mid_ready, 1)
            dve.sem_inc(s5_t_ready, 1)
            V.memset(eps[:], EPS).then_inc(eps_set, 1)
            dve.wait_ge(consts_in, 32)
            weigh = lambda o, src, w: V.tensor_tensor(out=o, in0=src[:], in1=w.unsqueeze(2).to_broadcast([P, KT, P]), op=ALU.mult)

            def norm_m2(k):
                dve.wait_ge(z_ready, k + 1)
                V.tensor_tensor(out=m2_n[:], in0=ym[:], in1=z_silu[:], op=ALU.mult).then_inc(m2_gated, 1)
                dve.wait_ge(m2_root, k + 1)
                chain.link(V.reciprocal(stat[:, 2, 1:3], stat[:, 1, 1:3]))
                for h in range(2):
                    half = slice(h * 512, h * 512 + 512)
                    last = V.tensor_scalar(m2_n[:, half], m2_n[:, half], stat[:, 2, 1 + h:2 + h], None, ALU.mult)
                last.then_inc(m2_n_ready, 1)

            def tile(k, more):
                chain.start(1 + STEPS_PER * k)
                dve.wait_ge(m2_turned, k + 1)
                weigh(both_t[:, KT:, :], ps_m2, norm_w[:, KT:]).then_inc(m2_t_ready, 1)
                dve.wait_ge(sig_ready, k + 2)
                V.tensor_tensor(out=s5_n[:], in0=g[:], in1=sig[:], op=ALU.mult).then_inc(s5_gated, 1)
                dve.wait_ge(s5_root, k + 1)
                chain.link(V.reciprocal(stat[:, 2, 0:1], stat[:, 1, 0:1]))
                V.tensor_scalar(s5_n[:], s5_n[:], stat[:, 2, 0:1], None, ALU.mult).then_inc(s5_n_ready, 1)
                dve.wait_ge(s5_turned, k + 1)
                weigh(both_t[:, 0:KT, :], ps_s5, norm_w[:, 0:KT]).then_inc(s5_t_ready, 1)
                if more:
                    norm_m2(k + 1)
                dve.wait_ge(out_made, k + 1)
                dve.wait_ge(x_in, 16 * k + 16)
                dve.wait_ge(x_mid_out, 16 * k + 16)
                V.tensor_tensor(out=x_mid[:], in0=x[:], in1=flat(ps_out), op=ALU.add).then_inc(x_mid_ready, 1)
                assert chain.n == STEPS_PER or not more

            chain.start(0)
            norm_m2(0)
            with dve.Fori(0, MAIN_TILES) as k:
                tile(k, True)
            tile(MAIN_TILES, False)

        @block.tensor
        def _(pe):
            T = nc.tensor

            def turn(dst, src):
                for c in range(KT):
                    last = T.transpose(dst[:, c, :], src[:, c * P:(c + 1) * P], ident[:])
                return last

            def project(dst, src_t, w, c0, n, first, final):
                for half in range(2):
                    for c in range(c0, c0 + n):
                        last = T.matmul(flat(dst)[:, half * 512:half * 512 + 512], src_t[:, c, :], w[:, c, half * 512:half * 512 + 512],
                                        start=first and c == c0, stop=final and c == c0 + n - 1)
                return last

            pe.wait_ge(consts_in, 32)
            with pe.Fori(0, TILES) as k:
                pe.wait_ge(g_ready, k + 1)
                pe.wait_ge(s5_t_ready, k + 1)
                turn(ps_s5, g).then_inc(g_turned, 1)
                pe.wait_ge(m2_n_ready, k + 1)
                turn(ps_m2, m2_n).then_inc(m2_turned, 1)
                pe.wait_ge(g_t_ready, k + 1)
                pe.wait_ge(sig_ready, k + 1)
                pe.wait_ge(glu_in, 16)
                project(ps_glu, g_t, w_glu, 0, KT, True, True).then_inc(glu_made, 1)
                pe.wait_ge(m2_t_ready, k + 1)
                pe.wait_ge(x_mid_ready, k + 1)
                pe.wait_ge(out_in, 16)
                project(ps_out, both_t, w_out, KT, KT, True, False)
                pe.wait_ge(s5_n_ready, k + 1)
                turn(ps_s5, s5_n).then_inc(s5_turned, 1)
                pe.wait_ge(s5_t_ready, k + 2)
                project(ps_out, both_t, w_out, 0, KT, False, True).then_inc(out_made, 1)


def route_and_experts(nc, D):
    PAIR = 2 * PH
    LEAST = -3.0e38
    RING, GROUP = 8, 1
    RING_GROUPS = RING // GROUP
    GROUPS = SLOTS // GROUP
    USES = GROUPS // RING_GROUPS
    HALF = SLOTS // 2
    assert 2 * SAMPLE == P
    UNITS, UNIT = PAIR // 4, 4
    ROUTE_STEPS = 64
    ROUTE_LINKS, END_LINKS = UNITS * 4 + 28, 2
    EVERY = GROUPS // ROUTE_STEPS
    SQUARES, NORM, TURN, H_T, QUERY = 3, 5, 6, 7, 8
    Q_COPY, SCORE, SCORE_COPY, KEYS = QUERY + UNIT + 1, QUERY + UNIT + 2, QUERY + UNIT + 4, QUERY + UNIT + 5
    SUMS = KEYS + UNIT * UNITS
    EXP = SUMS + 16
    assert SUMS + 22 < ROUTE_STEPS - 8
    with ExitStack() as ctx:
        sb = lambda n, s, d=F32: ctx.enter_context(nc.sbuf_tensor("pe_" + n, s, d))
        sem = ctx.enter_context(stage_semaphores(nc, "pe_"))
        ident = sb("ident", [P, P])
        half_ident = sb("half_ident", [P, 2, P])
        fold_ident = sb("fold_ident", [P, SAMPLE])
        ffn_w = sb("ffn_w", [P, D_MODEL])
        final_w = sb("final_w", [P, D_MODEL])
        count16 = sb("count16", [P, TOPK])
        eps = sb("eps", [P, 1])
        square = sb("square", [P, D_MODEL])
        w_q = sb("w_q", [P, KT, PAIR * P])
        keys_t = sb("keys_t", [P, PAIR, NK])
        x = sb("x", [P, D_MODEL])
        stat = sb("stat", [P, 3])
        h = sb("h", [P, D_MODEL])
        h_t = sb("h_t", [P, KT, P])
        q_t = sb("q_t", [P, 2, UNIT, P])
        work_a = sb("work_a", [P, PH * TOPK * TOPK])
        work_b = sb("work_b", [P, PH * TOPK * TOPK])
        rest = work_a[:].rearrange("p (j n) -> p j n", j=PAIR)
        cand = work_a[:].rearrange("p (h a b) -> p h a b", h=PH, a=TOPK)
        hit = work_a[:].rearrange("p (s j) -> p s j", s=SLOTS)
        score = work_b[:].rearrange("p (j n) -> p j n", j=PAIR)
        cand2 = work_b[:].rearrange("p (h c) -> p h c", h=PH)
        best = sb("best", [P, PH, 2, TOPK])
        best_i = sb("best_i", [P, PH, 2, TOPK], U32)
        best_f = sb("best_f", [P, PH, 2, TOPK])
        top = sb("top", [P, PH, TOPK])
        pos = sb("pos", [P, PH, TOPK], U32)
        pos_ab = sb("pos_ab", [P, 2, SLOTS], U32)
        pos_f = sb("pos_f", [P, 2, SLOTS])
        picked = sb("picked", [P, 2, SLOTS])
        index = sb("index", [P, SLOTS], I32)
        e = sb("e", [P, PH, TOPK])
        total = sb("total", [P, 2, PH])
        gate = sb("gate", [P, PH, TOPK])
        ring = sb("ring", [P, RING, 2 * D_MODEL])
        diag = sb("diag", [P, RING, P])
        x_now = sb("x_now", [P, D_MODEL])
        h_now = sb("h_now", [P, D_MODEL])
        gate_now = sb("gate_now", [P, SLOTS])
        index_now = sb("index_now", [P, 2, HALF], I32)
        dot = sb("dot", [P, RING])
        act_v = sb("act_v", [P, RING])
        out = sb("out", [P, D_MODEL])
        end_stat = sb("end_stat", [P, 3])
        acc = ctx.enter_context(nc.psum_tensor("pe_acc", [P, 2, 512], F32))
        ps_t = ctx.enter_context(nc.psum_tensor("pe_ps_t", [P, KT, P], F32))
        ps_q = ctx.enter_context(nc.psum_tensor("pe_ps_q", [P, 2, UNIT, P], F32))
        ps_s = ctx.enter_context(nc.psum_tensor("pe_ps_s", [P, 2, UNIT, P], F32))
        consts_in, x_in, eps_set, summed, root, h_ready = (sem(n) for n in (
            "consts_in", "x_in", "eps_set", "summed", "root", "h_ready"))
        folded = sem("folded")
        w_q_in = [sem(f"w_q_in{n}") for n in range(UNITS)]
        h_turned, h_t_ready, q_made, q_ready, s_made, s_ready = (sem(n) for n in (
            "h_turned", "h_t_ready", "q_made", "q_ready", "s_made", "s_ready"))
        shifted, e_ready, index_ready, index_taken, route_step, settled = (sem(n) for n in (
            "shifted", "e_ready", "index_ready", "index_taken", "route_step", "settled"))
        dots_ready, act_ready, diag_ready, group_done = sem("dots_ready"), sem("act_ready"), sem("diag_ready"), sem("group_done")
        rows_in = [sem(f"rows_in{g}") for g in range(RING_GROUPS)]
        x_now_ready, tile_done, end_summed, end_root, end_step, y_ready, y_out = (sem(n) for n in (
            "x_now_ready", "tile_done", "end_summed", "end_root", "end_step", "y_ready", "y_out"))
        block = ctx.enter_context(nc.Block())

        def place(g):
            p = g % RING_GROUPS
            return p, range(p * GROUP, (p + 1) * GROUP), g // RING_GROUPS

        @block.sync
        def _(sp):
            sp.dma_start(x[:], D["x_mid"][0:P, :]).then_inc(x_in, 16)
            for t, n in ((ident, "ident"), (ffn_w, "norm_ffn_w"), (count16, "count16"), (keys_t, "keys_t"),
                         (half_ident, "half_ident"), (fold_ident, "fold_ident"), (final_w, "final_norm_w")):
                sp.dma_start(t[:], D[n]).then_inc(consts_in, 16)
            for n in range(UNITS):
                cols = slice(n * UNIT * P, (n + 1) * UNIT * P)
                sp.dma_start(w_q[:, :, cols], D["w_q"][:, :, cols]).then_inc(w_q_in[n], 16)

            def load(k):
                sp.wait_ge(x_now_ready, k + 1)
                sp.dma_start(x[:], D["x_mid"][bass.ds(k * P + P, P), :]).then_inc(x_in, 16)

            def store(k):
                sp.wait_ge(y_ready, k + 2)
                sp.dma_start(D["y"][bass.ds(k * P, P), :], out[:]).then_inc(y_out, 16)

            with sp.Fori(0, MAIN_TILES - 1) as k:
                load(k)
                store(k)
            load(MAIN_TILES - 1)
            sp.wait_ge(route_step, ROUTE_LINKS * TILES)
            sp.wait_ge(index_taken, 2 * MAIN_TILES + 1)
            for t in (index[:], gate[:].rearrange("p h c -> p (h c)")):
                sp.dma_start(t[SAMPLE:P, 0:HALF], t[0:SAMPLE, HALF:SLOTS]).then_inc(folded, 16)
            sp.dma_start(h[SAMPLE:P, :], h[0:SAMPLE, :]).then_inc(folded, 16)
            store(MAIN_TILES - 1)
            sp.wait_ge(y_ready, TILES + 1)
            sp.dma_start(D["y"][SEQ:SEQ + SAMPLE, :], out[0:SAMPLE, :]).then_inc(y_out, 16)
            sp.wait_ge(y_out, 16 * (TILES + 1))

        @block.gpsimd
        def _(pool):
            flat = index[:].rearrange("p (b s) -> p b s", b=2)
            pool.sem_inc(group_done, RING_GROUPS)

            def tile(k, groups, route):
                for g in range(groups):
                    p, slots, use = place(g)
                    pool.wait_ge(group_done, k * GROUPS + g + 1)
                    if g == RING_GROUPS and route:
                        settle(pool, settled)
                        nc.gpsimd.tensor_copy(index_now[:, 1, :], flat[:, 1, :]).then_inc(index_taken, 1)
                        pool.wait_ge(index_taken, 2 * k + 2)
                    if g == GROUPS - RING_GROUPS and route:
                        pool.wait_ge(index_ready, k + 2)
                        settle(pool, settled)
                        nc.gpsimd.tensor_copy(index_now[:, 0, :], flat[:, 0, :]).then_inc(index_taken, 1)
                        pool.wait_ge(index_taken, 2 * k + 3)
                    settle(pool, settled)
                    for s in slots:
                        col = g * GROUP + s % GROUP
                        row = index_now[:, col // HALF, col % HALF:col % HALF + 1] if route else index[:, col:col + 1]
                        nc.gpsimd.indirect_dma_start(out=ring[:, s, :], out_offset=None, in_=D["uv"],
                                                     in_offset=bass.IndirectOffsetOnAxis(ap=row, axis=0)).then_inc(rows_in[p], 16)

            pool.wait_ge(index_ready, 1)
            nc.gpsimd.tensor_copy(index_now[:, 0, :], flat[:, 0, :]).then_inc(index_taken, 1)
            pool.wait_ge(index_taken, 1)
            with pool.Fori(0, MAIN_TILES) as k:
                tile(k, GROUPS, True)
            pool.wait_ge(folded, 48)
            tile(MAIN_TILES, GROUPS // 2, False)

        @block.scalar
        def _(act):
            A = nc.scalar.activation

            def route(r, g):
                if g == SQUARES:
                    act.wait_ge(x_in, 16 * r + 16)
                    A(square[:], x[:], ACT.Square, accum_out=stat[:, 0:1]).then_inc(summed, 1)
                    act.wait_ge(summed, r + 1)
                    A(stat[:, 1:2], stat[:, 0:1], ACT.Sqrt, bias=eps[:], scale=1.0 / D_MODEL).then_inc(root, 1)
                if g == H_T:
                    act.wait_ge(h_turned, r + 1)
                    A(h_t[:], ps_t[:], ACT.Copy).then_inc(h_t_ready, 1)
                for n in range(UNITS):
                    if g == Q_COPY + UNIT * n:
                        act.wait_ge(q_made, UNITS * r + n + 1)
                        A(q_t[:, n % 2], ps_q[:, n % 2], ACT.Copy).then_inc(q_ready, 1)
                    if g == SCORE_COPY + UNIT * n:
                        act.wait_ge(s_made, UNITS * r + n + 1)
                        A(score[:, UNIT * n:UNIT * n + UNIT, :], ps_s[:, n % 2], ACT.Copy).then_inc(s_ready, 1)
                if g == EXP:
                    act.wait_ge(shifted, r + 1)
                    A(e[:], e[:], ACT.Exp).then_inc(e_ready, 1)

            def tile(k, groups, more):
                for g in range(groups):
                    p, slots, use = place(g)
                    cols = slice(slots[0], slots[-1] + 1)
                    act.wait_ge(dots_ready, k * GROUPS + g + 1)
                    A(act_v[:, cols], dot[:, cols], ACT.Gelu_apprx_tanh).then_inc(act_ready, 1)
                    if more and g % EVERY == EVERY - 1:
                        route(k + 1, g // EVERY)
                act.wait_ge(tile_done, k + 1)
                A(square[:], acc[:].rearrange("p b c -> p (b c)"), ACT.Square, accum_out=end_stat[:, 0:1]).then_inc(end_summed, 1)
                act.wait_ge(end_summed, k + 1)
                A(end_stat[:, 1:2], end_stat[:, 0:1], ACT.Sqrt, bias=eps[:], scale=1.0 / D_MODEL).then_inc(end_root, 1)
                if more:
                    A(x_now[:], x[:], ACT.Copy).then_inc(x_now_ready, 1)

            act.wait_ge(eps_set, 1)
            for g in range(ROUTE_STEPS):
                route(0, g)
            A(x_now[:], x[:], ACT.Copy).then_inc(x_now_ready, 1)
            with act.Fori(0, MAIN_TILES) as k:
                tile(k, GROUPS, True)
            tile(MAIN_TILES, GROUPS // 2, False)

        @block.vector
        def _(dve):
            V = nc.vector
            chain = Chain(dve, route_step)
            end = Chain(dve, end_step)
            tt = lambda o, a, b, op: V.tensor_tensor(out=o, in0=a, in1=b, op=op)
            sums = cand.rearrange("p h a b -> p h (a b)")
            flat_gate = gate[:].rearrange("p h c -> p (h c)")

            def route(r, g, more):
                if g == NORM:
                    dve.wait_ge(root, r + 1)
                    chain.link(V.reciprocal(stat[:, 2:3], stat[:, 1:2]))
                    V.scalar_tensor_tensor(out=h[:], in0=x[:], scalar=stat[:, 2:3], in1=ffn_w[:], op0=ALU.mult, op1=ALU.mult).then_inc(h_ready, 1)
                for n in range(UNITS):
                    pairs = [(j, j // 2, j % 2) for j in range(UNIT * n, UNIT * n + UNIT)]
                    if g == KEYS + UNIT * n:
                        dve.wait_ge(s_ready, UNITS * r + n + 1)
                        settle(dve, settled)
                        for j, a, b in pairs:
                            last = V.max(out=best[:, a, b, 0:8], in_=score[:, j, :])
                        chain.link(last)
                        settle(dve, settled)
                    if g == KEYS + UNIT * n + 1:
                        for j, a, b in pairs:
                            V.max_index(out=best_i[:, a, b, 0:8], in_max=best[:, a, b, 0:8], in_values=score[:, j, :])
                            last = V.match_replace(out=rest[:, j, :], in_to_replace=best[:, a, b, 0:8], in_values=score[:, j, :], imm_value=LEAST)
                        chain.link(last)
                        settle(dve, settled)
                    if g == KEYS + UNIT * n + 2:
                        for j, a, b in pairs:
                            last = V.max(out=best[:, a, b, 8:16], in_=rest[:, j, :])
                        chain.link(last)
                        settle(dve, settled)
                    if g == KEYS + UNIT * n + 3:
                        for j, a, b in pairs:
                            last = V.max_index(out=best_i[:, a, b, 8:16], in_max=best[:, a, b, 8:16], in_values=rest[:, j, :])
                        chain.link(last)
                if g == SUMS:
                    chain.link(V.tensor_copy(best_f[:], best_i[:]))
                    chain.link(tt(cand, best[:, :, 0, :].unsqueeze(3).to_broadcast([P, PH, TOPK, TOPK]),
                                  best[:, :, 1, :].unsqueeze(2).to_broadcast([P, PH, TOPK, TOPK]), ALU.add))
                    settle(dve, settled)
                for q in range(4):
                    heads = (2 * q, 2 * q + 1)
                    if g == SUMS + 1 + q:
                        for a in heads:
                            last = V.max(out=top[:, a, 0:8], in_=sums[:, a, :])
                        chain.link(last)
                        settle(dve, settled)
                    if g == SUMS + 5 + q:
                        for a in heads:
                            V.max_index(out=pos[:, a, 0:8], in_max=top[:, a, 0:8], in_values=sums[:, a, :])
                            last = V.match_replace(out=cand2[:, a, :], in_to_replace=top[:, a, 0:8], in_values=sums[:, a, :], imm_value=LEAST)
                        chain.link(last)
                        settle(dve, settled)
                for q in range(2):
                    heads = range(4 * q, 4 * q + 4)
                    if g == SUMS + 9 + q:
                        for a in heads:
                            last = V.max(out=top[:, a, 8:16], in_=cand2[:, a, :])
                        chain.link(last)
                        settle(dve, settled)
                    if g == SUMS + 11 + q:
                        for a in heads:
                            last = V.max_index(out=pos[:, a, 8:16], in_max=top[:, a, 8:16], in_values=cand2[:, a, :])
                        chain.link(last)
                if g == SUMS + 13:
                    tt(e[:], top[:], top[:, :, 0:1].to_broadcast([P, PH, TOPK]), ALU.subtract).then_inc(shifted, 1)
                    flat_pos = pos[:].rearrange("p h c -> p (h c)")
                    chain.link(V.tensor_scalar(pos_ab[:, 0, :], flat_pos, 4, None, ALU.logical_shift_right))
                    chain.link(V.tensor_scalar(pos_ab[:, 1, :], flat_pos, TOPK - 1, None, ALU.bitwise_and))
                    chain.link(V.tensor_copy(pos_f[:], pos_ab[:]))
                by_head = hit.rearrange("p (h c) j -> p h c j", h=PH)
                for b in range(2):
                    if g == SUMS + 14 + 3 * b:
                        chain.link(tt(hit, pos_f[:, b, :].unsqueeze(2).to_broadcast([P, SLOTS, TOPK]),
                                      count16[:].unsqueeze(1).to_broadcast([P, SLOTS, TOPK]), ALU.is_equal))
                    if g == SUMS + 15 + 3 * b:
                        chain.link(tt(by_head, by_head, best_f[:, :, b, :].unsqueeze(2).to_broadcast([P, PH, TOPK, TOPK]), ALU.mult))
                    if g == SUMS + 16 + 3 * b:
                        chain.link(V.tensor_reduce(out=picked[:, b, :], in_=hit, axis=AX.X, op=ALU.add))
                if g == SUMS + 20:
                    chain.link(V.scalar_tensor_tensor(out=pos_f[:, 0, :], in0=picked[:, 0, :], scalar=float(NK), in1=picked[:, 1, :],
                                                      op0=ALU.mult, op1=ALU.add))
                    if more:
                        dve.wait_ge(index_taken, 2 * r)
                    V.tensor_copy(index[:], pos_f[:, 0, :]).then_inc(index_ready, 1)
                if g == SUMS + 21:
                    dve.wait_ge(e_ready, r + 1)
                    chain.link(V.tensor_reduce(out=total[:, 0, :], in_=e[:], axis=AX.X, op=ALU.add))
                    chain.link(V.reciprocal(total[:, 1, :], total[:, 0, :]))
                    chain.link(tt(gate[:], e[:], total[:, 1, :].unsqueeze(2).to_broadcast([P, PH, TOPK]), ALU.mult))

            def tile(k, groups, more):
                end.start(END_LINKS * k)
                if more:
                    chain.start(ROUTE_LINKS * (k + 1))
                tokens, gates, eye, width = (h_now, gate_now, ident, P) if more else (h, flat_gate, fold_ident, SAMPLE)

                def weigh(g):
                    dve.wait_ge(act_ready, k * GROUPS + g + 1)
                    for s in place(g)[1]:
                        col = g * GROUP + s % GROUP
                        last = V.tensor_scalar(diag[:, s, 0:width], eye[:], act_v[:, s:s + 1], gates[:, col:col + 1], ALU.mult, ALU.mult)
                    last.then_inc(diag_ready, 1)

                if more:
                    V.tensor_copy(gate_now[:], flat_gate)
                    end.link(V.tensor_copy(h_now[:], h[:]))
                else:
                    dve.wait_ge(folded, 48)
                for g in range(groups):
                    p, slots, use = place(g)
                    dve.wait_ge(rows_in[p], 16 * GROUP * (k * USES + use + 1))
                    for s in slots:
                        last = V.tensor_tensor_reduce(out=ring[:, s, 0:D_MODEL], in0=ring[:, s, 0:D_MODEL], in1=tokens[:],
                                                      scale=1.0, scalar=0.0, op0=ALU.mult, op1=ALU.add, accum_out=dot[:, s:s + 1])
                    last.then_inc(dots_ready, 1)
                    if more and g % EVERY == EVERY - 1:
                        route(k + 1, g // EVERY, True)
                    if g:
                        weigh(g - 1)
                weigh(groups - 1)
                dve.wait_ge(end_root, k + 1)
                end.link(V.reciprocal(end_stat[:, 2:3], end_stat[:, 1:2]))
                dve.wait_ge(y_out, 16 * k + 16)
                V.scalar_tensor_tensor(out=out[:], in0=acc[:].rearrange("p b c -> p (b c)"), scalar=end_stat[:, 2:3], in1=final_w[:],
                                       op0=ALU.mult, op1=ALU.mult).then_inc(y_ready, 1)
                assert end.n == END_LINKS or not more
                assert not more or chain.n == ROUTE_LINKS, chain.n

            V.memset(eps[:], EPS).then_inc(eps_set, 1)
            dve.sem_inc(y_out, 16)
            dve.sem_inc(y_ready, 1)
            dve.wait_ge(consts_in, 112)
            chain.start(0)
            for g in range(ROUTE_STEPS):
                route(0, g, False)
            with dve.Fori(0, MAIN_TILES) as k:
                tile(k, GROUPS, True)
            tile(MAIN_TILES, GROUPS // 2, False)

        @block.tensor
        def _(pe):
            T = nc.tensor

            def route(r, g):
                if g == TURN:
                    pe.wait_ge(h_ready, r + 1)
                    for c in range(KT):
                        last = T.transpose(ps_t[:, c, :], h[:, c * P:(c + 1) * P], ident[:])
                    last.then_inc(h_turned, 1)
                for j in range(PAIR):
                    n = j // UNIT
                    if g == QUERY + j:
                        if j == 0:
                            pe.wait_ge(h_t_ready, r + 1)
                        if n >= 2 and j % UNIT == 0:
                            pe.wait_ge(q_ready, UNITS * r + n - 1)
                        for c in range(KT):
                            last = T.matmul(ps_q[:, n % 2, j % UNIT, :], w_q[:, c, j * P:(j + 1) * P], h_t[:, c, :],
                                            start=c == 0, stop=c == KT - 1)
                        if j % UNIT == UNIT - 1:
                            last.then_inc(q_made, 1)
                for n in range(UNITS):
                    if g == SCORE + UNIT * n:
                        pe.wait_ge(q_ready, UNITS * r + n + 1)
                        if n >= 2:
                            pe.wait_ge(s_ready, UNITS * r + n - 1)
                        for j in range(UNIT):
                            last = T.matmul(ps_s[:, n % 2, j, :], q_t[:, n % 2, j, :], keys_t[:, UNIT * n + j, :], start=True, stop=True)
                        last.then_inc(s_made, 1)

            def add_x(half):
                for b in range(2):
                    last = T.matmul(acc[:, b, :], half_ident[:, half, :], x_now[:, b * 512:b * 512 + 512], start=half == 0, stop=half == 1)
                return last

            def tile(k, groups, more):
                width = P if more else SAMPLE
                pe.wait_ge(x_now_ready, k + 1)
                pe.wait_ge(y_ready, k + 1)
                add_x(0)
                for g in range(groups):
                    p, slots, use = place(g)
                    pe.wait_ge(diag_ready, k * GROUPS + g + 1)
                    for s in slots:
                        for b in range(2):
                            last = T.matmul(acc[0:width, b, :], diag[:, s, 0:width], ring[:, s, D_MODEL + b * 512:D_MODEL + b * 512 + 512],
                                            start=False, stop=False)
                    last.then_inc(group_done, 1)
                    if more and g % EVERY == EVERY - 1:
                        route(k + 1, g // EVERY)
                add_x(1).then_inc(tile_done, 1)

            pe.wait_ge(consts_in, 112)
            for g in range(ROUTE_STEPS):
                if g >= QUERY and (g - QUERY) % UNIT == 0 and g < QUERY + PAIR:
                    pe.wait_ge(w_q_in[(g - QUERY) // UNIT], 16)
                route(0, g)
            with pe.Fori(0, MAIN_TILES) as k:
                tile(k, GROUPS, True)
            tile(MAIN_TILES, GROUPS // 2, False)


def lay_out(x):
    r = lambda a: np.ascontiguousarray(a, np.float32)
    pairs = lambda a, *tail: a.reshape(PAIRS, 2, S5_STATE, *tail).transpose(1, 2, 0, *range(3, 3 + len(tail))).reshape(P, PAIRS, *tail)
    d = {}
    d["x_all"] = np.concatenate([x["x_prompt"][0], x["x_sample"].reshape(SAMPLE, D_MODEL), x["meta_tokens"],
                                 np.zeros((P - REST, D_MODEL), np.float32)])
    d["ident"] = np.eye(P, dtype=np.float32)
    d["fold_ident"] = np.tile(np.eye(SAMPLE), (P // SAMPLE, 1))
    d["half_ident"] = np.stack([np.diag(np.arange(P) < P // 2), np.diag(np.arange(P) >= P // 2)], 1)
    d["norm_mix_w"] = x["norm_mix_w"][0].reshape(KT, P).T
    w = x["w_in"][0]
    w = np.concatenate([w[:, :2 * D_MODEL], w[:, 2 * D_MODEL + XBC:], w[:, 2 * D_MODEL:2 * D_MODEL + XBC]], 1)
    d["w_in"] = w.reshape(KT, P, IN_PROJ).transpose(1, 0, 2)
    d["s5_par"] = np.stack([pairs(x["s5_lambda_re"][0]), pairs(x["s5_lambda_im"][0]),
                            pairs(np.repeat(x["s5_log_step"][0][:, None], S5_STATE, 1))], 1)
    d["s5_b"] = np.stack([pairs(x["s5_b_re"][0], S5_CH), pairs(x["s5_b_im"][0], S5_CH)], 1)
    d["s5_c"] = np.stack([pairs(x["s5_c_re"][0].transpose(0, 2, 1), S5_CH), pairs(x["s5_c_im"][0].transpose(0, 2, 1), S5_CH)], 1)
    d["s5_d"] = x["s5_d"][0].reshape(S5_GROUPS, S5_CH).T
    j = np.arange(P)
    seg = np.where(j < SAMPLE, j // STEPS, np.where(j < REST, SEQS, SEQS + 1 + j))
    same = seg[:, None] == seg[None, :]
    real = (j < REST)[:, None]
    d["after"], d["upto"], d["ones"] = j[:, None] > j[None, :], j[:, None] <= j[None, :], np.ones((P, P))
    d["after_seg"], d["upto_seg"] = d["after"] & same & real, d["upto"] & same & real
    d["in_seg"] = np.repeat((seg[:, None] == np.arange(SEQS + 1)[None, :])[:, :, None], P, 2)
    chan = lambda a: a.reshape(*a.shape[:-1], XB, P)
    d["conv_w"] = chan(x["m2_conv_w"][0]).transpose(2, 1, 0)
    d["conv_b"] = chan(x["m2_conv_b"][0]).T
    d["conv_past"] = chan(x["state_conv"][0]).transpose(3, 2, 0, 1)
    d["head_par"] = np.broadcast_to(np.stack([x["m2_dt_bias"][0], x["m2_a_log"][0], x["m2_d"][0]]), (P, 3, HEADS))
    d["ssm_h0"] = x["state_ssm"][0].transpose(3, 0, 1, 2)
    rows = lambda w: w.reshape(-1, P, w.shape[1]).transpose(1, 0, 2)
    d["w_glu"], d["w_out"], d["w_q"] = rows(x["s5_w_glu"][0]), rows(x["w_out"][0]), rows(x["peer_w_q"][0])
    d["mix_norm_w"] = np.concatenate([x["s5_norm_w"][0], x["m2_norm_w"][0]]).reshape(2 * KT, P).T
    d["keys_t"] = x["peer_sub_keys"][0].reshape(2 * PH, NK, P).transpose(2, 0, 1)
    d["norm_ffn_w"] = np.broadcast_to(x["norm_ffn_w"][0], (P, D_MODEL))
    d["final_norm_w"] = np.broadcast_to(x["final_norm_w"], (P, D_MODEL))
    d["count16"] = np.broadcast_to(np.arange(TOPK), (P, TOPK))
    d["uv"] = np.concatenate([x["peer_u"][0], x["peer_v"][0]], 1)
    h0 = np.stack([x["state_s5_re"][0], x["state_s5_im"][0]])
    d["s5_h0"] = h0.reshape(2, SEQS, PAIRS, 2, S5_STATE).transpose(3, 4, 2, 0, 1).reshape(P, PAIRS, 2, SEQS)
    return {k: r(v) for k, v in d.items()}


SCRATCH = {"u": (ROWS, D_MODEL), "z": (ROWS, D_MODEL), "dt": (ROWS, HEADS), "xbc": (P, XB, XCOLS), "y5": (ROWS, D_MODEL), "ym": (ROWS, D_MODEL),
           "x_mid": (ROWS, D_MODEL)}
OUTPUTS = {"y": (SEQ + SAMPLE, D_MODEL), "s5_end_sample": (P, PAIRS, 2, SEQS), "s5_end_prompt": (P, PAIRS, 2),
           "conv_end_sample": (P, XB, SEQS, TAPS - 1), "conv_end_prompt": (P, XB, TAPS - 1),
           "ssm_end_sample": (P, SEQS, HEADS, HD), "ssm_end_prompt": (P, HEADS, HD)}


def write_program(nc, D):
    with ExitStack() as ctx:
        tables = s5_tables(nc, ctx)
        project_tokens(nc, D, tables)
        s5_scan(nc, D, tables)
    mamba_scan(nc, D)
    mix_out(nc, D)
    route_and_experts(nc, D)


def kernel(**inputs):
    import concourse.bacc as bacc
    from concourse.bass_utils import run_bass_kernel_spmd

    x = {name: np.asarray(a) for name, a in inputs.items()}
    nc = bacc.Bacc("TRN2", target_bir_lowering=False, num_devices=1)
    arrays = lay_out(x)
    D = {name: nc.dram_tensor("in_" + name, a.shape, F32, kind="ExternalInput").ap() for name, a in arrays.items()}
    for name, shape in SCRATCH.items():
        D[name] = nc.dram_tensor("scratch_" + name, shape, I32 if name == "index" else F32).ap()
    for name, shape in OUTPUTS.items():
        D[name] = nc.dram_tensor("out_" + name, shape, F32, kind="ExternalOutput").ap()
    write_program(nc, D)
    got = run_bass_kernel_spmd(nc, [{"in_" + n: a for n, a in arrays.items()}], core_ids=[0]).results[0]
    out = {name: np.asarray(got["out_" + name]) for name in OUTPUTS}

    s5 = lambda a, part: a[:, :, part].reshape(2, S5_STATE, PAIRS, -1).transpose(3, 2, 0, 1).reshape(1, -1, S5_GROUPS, S5_STATE)
    ssm = lambda a: a.reshape(NS, -1, HEADS, HD).transpose(1, 2, 3, 0)[None]
    conv = lambda a: a.reshape(P, XB, -1, TAPS - 1).transpose(2, 3, 1, 0).reshape(1, -1, TAPS - 1, XBC)
    r = np.ascontiguousarray
    return (r(out["y"][:SEQ].reshape(1, SEQ, D_MODEL)), r(out["y"][SEQ:].reshape(SEQS, STEPS, D_MODEL)),
            r(s5(out["s5_end_prompt"], 0)), r(s5(out["s5_end_prompt"], 1)), r(ssm(out["ssm_end_prompt"])), r(conv(out["conv_end_prompt"])),
            r(s5(out["s5_end_sample"], 0)), r(s5(out["s5_end_sample"], 1)), r(ssm(out["ssm_end_sample"])), r(conv(out["conv_end_sample"])))
```
